# Optimizing a Trainium2 kernel written in Bass

```python
import jax, jax.numpy as jnp
from jax import lax
import numpy as np

D_MODEL = 1024
BATCH = 1
SEQ = 512
DEPTH = 1
DEC_BATCH = 1
DEC_SEQ = 1024
PAST_LEN = 128

GRID_W = 64
N_Q_HEADS = 8
N_KV_HEADS = 2
GQA_GROUP = N_Q_HEADS // N_KV_HEADS
HEAD_DIM = 64
ATTN_WIDTH = N_Q_HEADS * HEAD_DIM
KV_WIDTH = N_KV_HEADS * HEAD_DIM
ROPE_THETA = 10000.0
Q_BLOCK = 128
M_HEADS = 4
M_HEAD_DIM = 128
M_WIDTH = M_HEADS * M_HEAD_DIM
M_CHUNK = 64
N_GATE_PRE = 4 * M_HEADS
D_FF = 2816
CONV_W = 3
EPS = 1e-6
IN_SIZES = (ATTN_WIDTH, KV_WIDTH, KV_WIDTH,
            M_WIDTH, M_WIDTH, M_WIDTH, M_WIDTH,
            N_GATE_PRE,
            D_MODEL, D_MODEL)
D_IN = ATTN_WIDTH + 2 * KV_WIDTH + 4 * M_WIDTH + N_GATE_PRE + 2 * D_MODEL

kernel_name = "hybrid_axial_gqa_mlstm_convffn_encoder"

def rmsnorm(x, g):
    xf = x.astype(jnp.float32)
    y = xf * lax.rsqrt(jnp.mean(xf * xf, axis=-1, keepdims=True) + EPS) * g.astype(jnp.float32)
    return y.astype(x.dtype)

def axial_angles(S):
    rows = S // GRID_W
    r = jnp.repeat(jnp.arange(rows, dtype=jnp.float32), GRID_W)
    c = jnp.tile(jnp.arange(GRID_W, dtype=jnp.float32), rows)
    n_pairs_axis = HEAD_DIM // 4
    freq = ROPE_THETA ** (-jnp.arange(n_pairs_axis, dtype=jnp.float32) / n_pairs_axis)
    ang = jnp.concatenate([r[:, None] * freq, c[:, None] * freq], axis=-1)
    return jnp.cos(ang), jnp.sin(ang)

def apply_rope(x, cos, sin):
    B, S, H, dh = x.shape
    xf = x.astype(jnp.float32).reshape(B, S, H, dh // 2, 2)
    x0, x1 = xf[..., 0], xf[..., 1]
    c, s = cos[None, :, None, :], sin[None, :, None, :]
    out = jnp.stack([x0 * c - x1 * s, x0 * s + x1 * c], axis=-1)
    return out.reshape(B, S, H, dh).astype(x.dtype)

def axial_gqa(q, k, v, q_norm, k_norm):
    B, S, _ = q.shape
    q = rmsnorm(q.reshape(B, S, N_Q_HEADS, HEAD_DIM), q_norm)
    k = rmsnorm(k.reshape(B, S, N_KV_HEADS, HEAD_DIM), k_norm)
    v = v.reshape(B, S, N_KV_HEADS, HEAD_DIM)
    cos, sin = axial_angles(S)
    q = apply_rope(q, cos, sin)
    k = apply_rope(k, cos, sin)
    q = q.reshape(B, S, N_KV_HEADS, GQA_GROUP, HEAD_DIM).transpose(0, 2, 3, 1, 4) * (HEAD_DIM ** -0.5)
    k = k.transpose(0, 2, 1, 3)
    v = v.transpose(0, 2, 1, 3)
    nb = S // Q_BLOCK
    qb = q.reshape(B, N_KV_HEADS, GQA_GROUP, nb, Q_BLOCK, HEAD_DIM).transpose(3, 0, 1, 2, 4, 5)

    def block(qblk):
        s = jnp.einsum('bkgqd,bksd->bkgqs', qblk, k).astype(jnp.float32)
        p = jax.nn.softmax(s, axis=-1).astype(v.dtype)
        return jnp.einsum('bkgqs,bksd->bkgqd', p, v)

    o = lax.map(block, qb)
    return o.transpose(1, 0, 4, 2, 3, 5).reshape(B, S, ATTN_WIDTH)

def mlstm_scan(q, k, v, li, lf):
    B, H, S, dk = q.shape
    dv = v.shape[-1]
    L = M_CHUNK
    N = S // L

    def chunks(a):
        return jnp.moveaxis(a.reshape((B, H, N, L) + a.shape[3:]), 2, 0)

    tri = jnp.tril(jnp.ones((L, L), dtype=bool))

    def step(carry, inp):
        C, n, m = carry
        qc, kc, vc, ic, fc = inp
        b = jnp.cumsum(fc, axis=-1)
        Dm = jnp.where(tri, b[..., :, None] - b[..., None, :] + ic[..., None, :], -jnp.inf)
        inter = b + m[..., None]
        mt = jnp.maximum(jnp.max(Dm, axis=-1), inter)
        W = jnp.exp(Dm - mt[..., None]) * jnp.einsum('bhtd,bhsd->bhts', qc, kc)
        dec = jnp.exp(inter - mt)
        num = jnp.einsum('bhts,bhse->bhte', W, vc) + dec[..., None] * jnp.einsum('bhtd,bhde->bhte', qc, C)
        den = jnp.sum(W, axis=-1) + dec * jnp.einsum('bhtd,bhd->bht', qc, n)
        h = num / jnp.maximum(jnp.abs(den), jnp.exp(-mt))[..., None]
        bL = b[..., -1]
        ws = bL[..., None] - b + ic
        m_new = jnp.maximum(bL + m, jnp.max(ws, axis=-1))
        a = jnp.exp(bL + m - m_new)
        w = jnp.exp(ws - m_new[..., None])
        C = a[..., None, None] * C + jnp.einsum('bhs,bhsd,bhse->bhde', w, kc, vc)
        n = a[..., None] * n + jnp.einsum('bhs,bhsd->bhd', w, kc)
        return (C, n, m_new), h

    init = (jnp.zeros((B, H, dk, dv), jnp.float32), jnp.zeros((B, H, dk), jnp.float32),
            jnp.zeros((B, H), jnp.float32))
    _, hs = lax.scan(step, init, (chunks(q), chunks(k), chunks(v), chunks(li), chunks(lf)))
    return jnp.moveaxis(hs, 0, 2).reshape(B, H, S, dv)

def bidir_mlstm(q, k, v, o, gate_pre, b_if, mlstm_norm):
    B, S, _ = q.shape

    def heads(a):
        return a.astype(jnp.float32).reshape(B, S, M_HEADS, M_HEAD_DIM).transpose(0, 2, 1, 3)

    qh, kh, vh = heads(q), heads(k) * (M_HEAD_DIM ** -0.5), heads(v)
    g = (gate_pre.astype(jnp.float32) + b_if.astype(jnp.float32)).reshape(B, S, 4, M_HEADS)
    g = g.transpose(2, 0, 3, 1)
    i_f, lf_f = g[0], jax.nn.log_sigmoid(g[1])
    i_b, lf_b = g[2], jax.nn.log_sigmoid(g[3])
    h_f = mlstm_scan(qh, kh, vh, i_f, lf_f)
    flip = lambda a: jnp.flip(a, axis=2)
    h_b = flip(mlstm_scan(flip(qh), flip(kh), flip(vh), flip(i_b), flip(lf_b)))
    h = (h_f + h_b).transpose(0, 2, 1, 3)
    h = rmsnorm(h, mlstm_norm.reshape(M_HEADS, M_HEAD_DIM)).reshape(B, S, M_WIDTH)
    return (h * jax.nn.sigmoid(o.astype(jnp.float32))).astype(q.dtype)

def dwconv_centred(g, w, b):
    S = g.shape[1]
    gp = jnp.pad(g, ((0, 0), (CONV_W // 2, CONV_W // 2), (0, 0)))
    out = gp[:, 0:S] * w[0]
    for j in range(1, CONV_W):
        out = out + gp[:, j:j + S] * w[j]
    return out + b

def block_layer(x, norm_mix_pre, w_in, b_if, q_norm, k_norm, mlstm_norm, w_attn_o, w_mlstm_o,
                w_out, norm_mix_post, norm_ffn_pre, w_up, conv_w, conv_b, w_down, norm_ffn_post):
    h = rmsnorm(x, norm_mix_pre)
    z = h @ w_in
    idx = [int(i) for i in np.cumsum(IN_SIZES)[:-1]]
    aq, ak, av, mq, mk, mv, mo, gate_pre, ga, gm = jnp.split(z, idx, axis=-1)
    a_out = axial_gqa(aq, ak, av, q_norm, k_norm) @ w_attn_o
    m_out = bidir_mlstm(mq, mk, mv, mo, gate_pre, b_if, mlstm_norm) @ w_mlstm_o
    merged = jax.nn.sigmoid(ga) * a_out + jax.nn.sigmoid(gm) * m_out
    x = x + rmsnorm(merged @ w_out, norm_mix_post)
    h = rmsnorm(x, norm_ffn_pre)
    u = h @ w_up
    gate, val = u[..., :D_FF], u[..., D_FF:]
    gate = dwconv_centred(gate, conv_w, conv_b)
    y = (jax.nn.gelu(gate, approximate=True) * val) @ w_down
    return x + rmsnorm(y, norm_ffn_post)

def setup_inputs(seed: int = 0) -> dict:
    key = jax.random.key(seed)
    ks = jax.random.split(key, 24)
    f32 = jnp.float32

    def w(k, shape, fan_in):
        return jax.random.normal(k, shape, f32) * (fan_in ** -0.5)

    def gain(k, shape):
        return 1.0 + 0.05 * jax.random.normal(k, shape, f32)

    kb = jax.random.split(ks[17], 4)
    fbias = jnp.linspace(3.0, 6.0, M_HEADS, dtype=f32)
    b_if = jnp.concatenate([
        0.1 * jax.random.normal(kb[0], (M_HEADS,), f32),
        fbias + 0.1 * jax.random.normal(kb[1], (M_HEADS,), f32),
        0.1 * jax.random.normal(kb[2], (M_HEADS,), f32),
        fbias + 0.1 * jax.random.normal(kb[3], (M_HEADS,), f32)])
    b_if = jnp.tile(b_if[None], (DEPTH, 1))
    return {
        "x_prompt": jax.random.normal(ks[0], (BATCH, SEQ, D_MODEL), f32),
        "x_sample": jax.random.normal(ks[1], (DEC_BATCH, DEC_SEQ, D_MODEL), f32),
        "norm_mix_pre": gain(ks[2], (DEPTH, D_MODEL)),
        "w_in": w(ks[3], (DEPTH, D_MODEL, D_IN), D_MODEL),
        "b_if": b_if,
        "q_norm": gain(ks[4], (DEPTH, HEAD_DIM)),
        "k_norm": gain(ks[5], (DEPTH, HEAD_DIM)),
        "mlstm_norm": gain(ks[6], (DEPTH, M_WIDTH)),
        "w_attn_o": w(ks[7], (DEPTH, ATTN_WIDTH, D_MODEL), ATTN_WIDTH),
        "w_mlstm_o": w(ks[8], (DEPTH, M_WIDTH, D_MODEL), M_WIDTH),
        "w_out": w(ks[9], (DEPTH, D_MODEL, D_MODEL), D_MODEL),
        "norm_mix_post": gain(ks[10], (DEPTH, D_MODEL)),
        "norm_ffn_pre": gain(ks[11], (DEPTH, D_MODEL)),
        "w_up": w(ks[12], (DEPTH, D_MODEL, 2 * D_FF), D_MODEL),
        "conv_w": w(ks[13], (DEPTH, CONV_W, D_FF), CONV_W),
        "conv_b": 0.01 * jax.random.normal(ks[14], (DEPTH, D_FF), f32),
        "w_down": w(ks[15], (DEPTH, D_FF, D_MODEL), D_FF),
        "norm_ffn_post": gain(ks[16], (DEPTH, D_MODEL)),
    }

def reference(x_prompt, x_sample, norm_mix_pre, w_in, b_if, q_norm, k_norm, mlstm_norm,
              w_attn_o, w_mlstm_o, w_out, norm_mix_post, norm_ffn_pre, w_up, conv_w, conv_b,
              w_down, norm_ffn_post):
    def trunk(x):
        for l in range(DEPTH):
            x = block_layer(x, norm_mix_pre[l], w_in[l], b_if[l], q_norm[l], k_norm[l],
                            mlstm_norm[l], w_attn_o[l], w_mlstm_o[l], w_out[l], norm_mix_post[l],
                            norm_ffn_pre[l], w_up[l], conv_w[l], conv_b[l], w_down[l],
                            norm_ffn_post[l])
        return x

    y_prompt = trunk(x_prompt)
    y_sample = trunk(x_sample)
    return (y_prompt, y_sample)


_drawn_inputs = setup_inputs


def setup_inputs(seed=0):
    import zlib

    import numpy as np

    out = dict(_drawn_inputs(seed))
    spreads = {}
    factors = {'q_norm': 8.0, 'k_norm': 8.0, 'conv_b': 8.0, 'mlstm_norm': 2.683}
    for name, (base, spread) in spreads.items():
        noise = np.random.default_rng([zlib.crc32(name.encode()), seed]).standard_normal(out[name].shape)
        drawn = base * np.exp(spread * noise) if base else spread * noise
        out[name] = __import__('jax').numpy.asarray(drawn.astype(out[name].dtype))
    for name, factor in factors.items():
        out[name] = (out[name] * factor).astype(out[name].dtype)
    return out
```

```python
from contextlib import ExitStack

import concourse.bass as bass
from concourse import mybir

F32 = mybir.dt.float32
F32R = mybir.dt.float32r
ACT = mybir.ActivationFunctionType
ALU = mybir.AluOpType
AX_X = mybir.AxisListType.X

P = 128
D = 1024
KD = D // P
SEG_TILES = (4, 8)
NT = sum(SEG_TILES)
TOK = NT * P
CH = 512
NCH = TOK // CH
GRID_W = 64
HEAD = 64
NQ, NKV = 8, 2
QK = (NQ + NKV) * HEAD
QKV = QK + NKV * HEAD
NHEADS_QK = NQ + NKV
MH, MD = 4, 128
MW = MH * MD
FF = 2816
NFF = FF // P
CONV_W = 3
EPS = 1e-6
COL_M = QKV
COL_O = COL_M + 3 * MW
COL_GATE = COL_O + MW
N_GATE = 4 * MH
COL_GA = COL_GATE + N_GATE
NEG = -1.0e30

SEG_OF_CHUNK = [(0, 4), (4, 12), (4, 12)]


def ring(i, c):
    return 2 * i + c, c % 2, i + c // 2


def wait_apart(eng, k, semaphore, value):
    eng.wait_ge(semaphore, value)
    eng.sem_inc(k.waits_apart, 1)


def unit(ap):
    return ap.rearrange("p a n -> p (a n)")


def mm3(pe, out, w_hi, w_lo, x_hi, x_lo, first, last, **kw):
    pe.matmul(out, w_hi, x_hi, start=first, stop=False, **kw)
    pe.matmul(out, w_lo, x_hi, start=False, stop=False, **kw)
    return pe.matmul(out, w_hi, x_lo, start=False, stop=last, **kw)


def norm_and_qkv(nc, k, hT_hi, hT_lo):
    with ExitStack() as ctx:
        def sb(name, shape, dt=F32):
            return ctx.enter_context(nc.sbuf_tensor(name, shape, dt))

        used = []

        def sem(name):
            used.append(ctx.enter_context(nc.semaphore(name)))
            return used[-1]

        wq_hi = sb("wqkv_hi", [P, KD, QKV], F32R)
        wq_lo = sb("wqkv_lo", [P, KD, QKV], F32R)
        gain = sb("mix_gain", [P, D])
        qk_gain = sb("qk_gain", [P, NHEADS_QK, HEAD])
        cos = sb("cos", [P, NT, HEAD // 2])
        sin = sb("sin", [P, NT, HEAD // 2])
        x_t = sb("x_t", [P, 2, D])
        xs = sb("x_scaled", [P, 2, D])
        h_hi = sb("h_hi", [P, KD, P], F32R)
        h_lo = sb("h_lo", [P, KD, P], F32R)
        squares = sb("squares", [P, D])
        qk_sq = sb("qk_sq", [P, NHEADS_QK, HEAD])
        v_st = sb("v_st", [P, NKV * HEAD])
        qk_n = sb("qk_n", [P, NHEADS_QK, HEAD])
        rot_a = sb("rot_a", [P, NHEADS_QK, HEAD // 2])
        rot_b = sb("rot_b", [P, NHEADS_QK, HEAD // 2])
        qk_r = sb("qk_r", [P, NHEADS_QK, HEAD])
        qkT_st = sb("qkT_st", [P, QK // P, P])
        stat = sb("stat", [P, 8])
        qstat = sb("qstat", [P, 4, NHEADS_QK])
        pT = ctx.enter_context(nc.psum_tensor("pT", [P, KD, P], F32))
        pQ = ctx.enter_context(nc.psum_tensor("pQ", [P, 2, D], F32))
        pR = ctx.enter_context(nc.psum_tensor("pR", [P, KD, P], F32))

        const_in = sem("const_in")
        w_in = [sem(f"qkv_w_in{b}") for b in range(2)]
        w_hi_done, w_split = sem("qkv_w_hi_done"), sem("qkv_w_split")
        x_in = [sem(f"x_in{b}") for b in range(2)]
        squared, rooted, rs_ready = sem("squared"), sem("rooted"), sem("rs_ready")
        x_scaled, x_turned = sem("x_scaled_s"), sem("x_turned")
        h_hi_done, h_lo_done, h_kept = sem("h_hi_done"), sem("h_lo_done"), sem("h_kept")
        qkv_done, qk_squared, qk_summed = sem("qkv_done"), sem("qk_squared"), sem("qk_summed")
        qk_rooted, qk_rs, qk_normed, v_copied = sem("qk_rooted"), sem("qk_rs"), sem("qk_normed"), sem("v_copied")
        qk_gained, half_b, half_a, qk_rot = sem("qk_gained"), sem("half_b"), sem("half_a"), sem("qk_rot")
        qk_turned, qkT_copied, v_out, qkT_out = sem("qk_turned"), sem("qkT_copied"), sem("v_out"), sem("qkT_out")
        rot_free = sem("rot_free")
        raw = xs
        start_at_one(nc, used)
        block = ctx.enter_context(nc.Block())
        wv = k.w_in.rearrange("(t p) n -> t p n", p=P)

        @block.sync
        def _(sp):
            for t in range(2):
                sp.dma_start(raw[:, t, 0:QKV], wv[t, :, 0:QKV]).then_inc(w_in[t], 16)
            for t in range(2):
                sp.dma_start(x_t[:, t, :], k.x[t * P:(t + 1) * P, :]).then_inc(x_in[t], 16)
            sp.dma_start(gain[:, :], k.norm_mix_pre.partition_broadcast(P)).then_inc(const_in, 16)
            for h in range(NHEADS_QK):
                g = k.q_norm if h < NQ else k.k_norm
                sp.dma_start(qk_gain[:, h, :], g.partition_broadcast(P)).then_inc(const_in, 16)
            sp.dma_start(cos[:, :, :], k.cos).then_inc(const_in, 16)
            sp.dma_start(sin[:, :, :], k.sin).then_inc(const_in, 16)
            for t in range(2, KD):
                sp.wait_ge(w_split, t)
                sp.dma_start(raw[:, t % 2, 0:QKV], wv[t, :, 0:QKV]).then_inc(w_in[t % 2], 16)
            with sp.Fori(0, (NT - 2) // 2) as i:
                for u in range(2):
                    t, b, _ = ring(i, 2 + u)
                    sp.wait_ge(x_scaled, t)
                    sp.wait_ge(squared, t)
                    sp.dma_start(x_t[:, b, :], k.x[bass.ds(t * P, P), :]).then_inc(x_in[b], 16)

        @block.scalar
        def _(act):
            def statistics(t, b, n):
                act.wait_ge(x_in[b], 16 * (n + 1) + 1)
                act.activation(squares[:, :], x_t[:, b, :], ACT.Square,
                               accum_out=stat[:, b:b + 1]).then_inc(squared, 1)
                act.wait_ge(squared, t + 2)
                act.activation(stat[:, 2 + b:3 + b], stat[:, b:b + 1], ACT.Sqrt, scale=1.0 / D,
                               bias=k.eps[:, 0:1]).then_inc(rooted, 1)

            def keep_hi(t, b, n):
                act.wait_ge(x_turned, t + 2)
                act.wait_ge(qkv_done, t + 1)
                act.wait_ge(h_kept, 2 * t + 1)
                act.activation(h_hi[:, :, :], pT[:, :, :], ACT.Copy).then_inc(h_hi_done, 1)

            def qk_stats(t, b, n):
                act.wait_ge(qkv_done, t + 2)
                act.wait_ge(qk_summed, t + 1)
                act.activation(qk_sq[:, :, :].rearrange("p h d -> p (h d)"), pQ[:, b, 0:QK],
                               ACT.Square).then_inc(qk_squared, 1)
                act.wait_ge(v_out, 16 * t + 1)
                act.activation(v_st[:, :], pQ[:, b, QK:QKV], ACT.Copy).then_inc(v_copied, 1)
                act.wait_ge(qk_summed, t + 2)
                act.activation(qstat[:, 1, :], qstat[:, 0, :], ACT.Sqrt, scale=1.0 / HEAD,
                               bias=k.eps[:, 0:1]).then_inc(qk_rooted, 1)
                act.wait_ge(v_copied, t + 2)
                act.dma_start(k.v[bass.ds(t * P, P), :], v_st[:, :]).then_inc(v_out, 16)

            def keep_qkT(t, b, n):
                act.wait_ge(qk_turned, t + 2)
                act.wait_ge(qkT_out, 16 * t + 1)
                act.activation(qkT_st[:, :, :], pR[:, 0:QK // P, :], ACT.Copy).then_inc(qkT_copied, 1)
                act.wait_ge(qkT_copied, t + 2)
                act.dma_start(k.qkT.rearrange("(a p) t -> p a t", p=P)[:, :, bass.ds(t * P, P)],
                              qkT_st[:, :, :]).then_inc(qkT_out, 16)

            statistics(*ring(0, 0))
            keep_hi(*ring(0, 0))
            statistics(*ring(0, 1))
            with act.Fori(0, (NT - 2) // 2) as i:
                for u in range(2):
                    keep_hi(*ring(i, 1 + u))
                    qk_stats(*ring(i, u))
                    statistics(*ring(i, 2 + u))
                    keep_qkT(*ring(i, u))
            keep_hi(*ring(0, NT - 1))
            qk_stats(*ring(0, NT - 2))
            keep_qkT(*ring(0, NT - 2))
            qk_stats(*ring(0, NT - 1))
            keep_qkT(*ring(0, NT - 1))
            act.wait_ge(v_out, 16 * NT + 1)
            act.wait_ge(qkT_out, 16 * NT + 1)

        @block.vector
        def _(dve):
            dve.wait_ge(const_in, 16 * (1 + NHEADS_QK + 2) + 1)
            for t in range(KD):
                b = t % 2
                dve.wait_ge(w_in[b], 16 * (t // 2 + 1) + 1)
                dve.tensor_copy(wq_hi[:, t, :], raw[:, b, 0:QKV]).then_inc(w_hi_done, 1)
                dve.wait_ge(w_hi_done, t + 2)
                dve.tensor_tensor(wq_lo[:, t, :], raw[:, b, 0:QKV], wq_hi[:, t, :].bitcast(F32),
                                  ALU.subtract).then_inc(w_split, 1)
            dve.wait_ge(w_split, KD + 1)

            def scale(t, b, n, first=False):
                dve.wait_ge(rooted, t + 2)
                dve.reciprocal(stat[:, 4 + b:5 + b], stat[:, 2 + b:3 + b]).then_inc(rs_ready, 1)
                dve.wait_ge(rs_ready, t + 2)
                if not first:
                    dve.wait_ge(x_turned, t)
                dve.scalar_tensor_tensor(out=xs[:, b, :], in0=x_t[:, b, :], scalar=stat[:, 4 + b:5 + b],
                                         in1=gain[:, :], op0=ALU.mult, op1=ALU.mult).then_inc(x_scaled, 1)

            def keep_lo(t, b, n):
                dve.wait_ge(h_hi_done, t + 2)
                dve.tensor_tensor(h_lo[:, :, :], pT[:, :, :], h_hi[:, :, :].bitcast(F32),
                                  ALU.subtract).then_inc(h_lo_done, 1)

            def qk_norm(t, b, n):
                dve.wait_ge(qk_squared, t + 2)
                dve.tensor_reduce(qstat[:, 0, :], qk_sq[:, :, :], AX_X, ALU.add).then_inc(qk_summed, 1)
                dve.wait_ge(qk_rooted, t + 2)
                dve.reciprocal(qstat[:, 2, :], qstat[:, 1, :]).then_inc(qk_rs, 1)
                dve.wait_ge(qk_rs, t + 2)
                dve.wait_ge(rot_free, t + 1)
                dve.tensor_tensor(qk_n[:, :, :], pQ[:, b, 0:QK].rearrange("p (h d) -> p h d", d=HEAD),
                                  qstat[:, 2, :].unsqueeze(2).to_broadcast([P, NHEADS_QK, HEAD]),
                                  ALU.mult).then_inc(qk_normed, 1)

            scale(*ring(0, 0), first=True)
            scale(*ring(0, 1), first=True)
            keep_lo(*ring(0, 0))
            with dve.Fori(0, (NT - 2) // 2) as i:
                for u in range(2):
                    keep_lo(*ring(i, 1 + u))
                    qk_norm(*ring(i, u))
                    scale(*ring(i, 2 + u))
            keep_lo(*ring(0, NT - 1))
            qk_norm(*ring(0, NT - 2))
            qk_norm(*ring(0, NT - 1))

        @block.gpsimd
        def _(pool):
            pool.wait_ge(const_in, 16 * (1 + NHEADS_QK + 2) + 1)

            def keep_h(t, b, n):
                pool.wait_ge(h_hi_done, t + 2)
                pool.tensor_copy(hT_hi[:, :, bass.ds(t * P, P)], h_hi[:, :, :]).then_inc(h_kept, 1)
                pool.wait_ge(h_lo_done, t + 2)
                pool.tensor_copy(hT_lo[:, :, bass.ds(t * P, P)], h_lo[:, :, :]).then_inc(h_kept, 1)

            def rotate(t, b, n):
                pool.wait_ge(qk_normed, t + 2)
                pool.tensor_tensor(qk_n[:, :, :], qk_n[:, :, :], qk_gain[:, :, :], ALU.mult).then_inc(qk_gained, 1)
                pairs = qk_n[:, :, :].rearrange("p h (j e) -> p h j e", e=2)
                turned = qk_r[:, :, :].rearrange("p h (j e) -> p h j e", e=2)
                x0, x1 = pairs[:, :, :, 0], pairs[:, :, :, 1]

                def table(a):
                    return a[:, bass.ds(t, 1), :].to_broadcast([P, NHEADS_QK, HEAD // 2])

                pool.wait_ge(qk_gained, t + 2)
                wait_apart(pool, k, qk_rot, 2 * t + 1)
                pool.tensor_tensor(rot_a[:, :, :], x0, table(cos), ALU.mult).then_inc(half_a, 1)
                pool.tensor_tensor(rot_b[:, :, :], x1, table(sin), ALU.mult).then_inc(half_a, 1)
                pool.wait_ge(half_a, 4 * t + 3)
                pool.wait_ge(qk_turned, t + 1)
                pool.tensor_tensor(turned[:, :, :, 0], rot_a[:, :, :], rot_b[:, :, :],
                                   ALU.subtract).then_inc(qk_rot, 1)
                wait_apart(pool, k, qk_rot, 2 * t + 2)
                pool.tensor_tensor(rot_a[:, :, :], x0, table(sin), ALU.mult).then_inc(half_a, 1)
                pool.tensor_tensor(rot_b[:, :, :], x1, table(cos), ALU.mult).then_inc(rot_free, 1)
                pool.wait_ge(rot_free, t + 2)
                pool.tensor_tensor(turned[:, :, :, 1], rot_a[:, :, :], rot_b[:, :, :],
                                   ALU.add).then_inc(qk_rot, 1)
                pool.sem_inc(half_a, 1)

            keep_h(*ring(0, 0))
            with pool.Fori(0, (NT - 2) // 2) as i:
                for u in range(2):
                    keep_h(*ring(i, 1 + u))
                    rotate(*ring(i, u))
            keep_h(*ring(0, NT - 1))
            rotate(*ring(0, NT - 2))
            rotate(*ring(0, NT - 1))
            pool.wait_ge(h_kept, 2 * NT + 1)

        @block.tensor
        def _(pe):
            def turn_x(t, b, n, first=False):
                pe.wait_ge(x_scaled, t + 2)
                if not first:
                    pe.wait_ge(h_lo_done, t + 1)
                for kt in range(KD):
                    last = pe.transpose(pT[:, kt, :], xs[:, b, kt * P:(kt + 1) * P], k.ident[:, :])
                last.then_inc(x_turned, 1)

            def project(t, b, n, first=False):
                pe.wait_ge(h_lo_done, t + 2)
                if first:
                    pe.wait_ge(w_split, KD + 1)
                else:
                    pe.wait_ge(qk_normed, t)
                    pe.wait_ge(v_copied, t)
                for c0, c1 in ((0, CH), (CH, QKV)):
                    for kt in range(KD):
                        last = mm3(pe, pQ[:, b, c0:c1], h_hi[:, kt, :], h_lo[:, kt, :],
                                   wq_hi[:, kt, c0:c1], wq_lo[:, kt, c0:c1], kt == 0, kt == KD - 1)
                last.then_inc(qkv_done, 1)

            def turn_qk(t, b, n):
                pe.wait_ge(qk_rot, 2 * t + 3)
                pe.wait_ge(qkT_copied, t + 1)
                for a in range(QK // P):
                    last = pe.transpose(pR[:, a, :], qk_r[:, 2 * a:2 * a + 2, :].rearrange("p h d -> p (h d)"),
                                        k.ident[:, :])
                last.then_inc(qk_turned, 1)

            turn_x(*ring(0, 0), first=True)
            project(*ring(0, 0), first=True)
            turn_x(*ring(0, 1))
            project(*ring(0, 1), first=True)
            with pe.Fori(0, (NT - 2) // 2) as i:
                for u in range(2):
                    turn_x(*ring(i, 2 + u))
                    turn_qk(*ring(i, u))
                    project(*ring(i, 2 + u))
            turn_qk(*ring(0, NT - 2))
            turn_qk(*ring(0, NT - 1))
    return used


def input_projection(nc, k, hT_hi, hT_lo):
    with ExitStack() as ctx:
        def sb(name, shape, dt=F32):
            return ctx.enter_context(nc.sbuf_tensor(name, shape, dt))

        used = []

        def sem(name):
            used.append(ctx.enter_context(nc.semaphore(name)))
            return used[-1]

        raw = sb("win_raw", [P, 2, KD, P])
        w_hi = sb("win_hi", [P, 2, KD, P], F32R)
        w_lo = sb("win_lo", [P, 2, KD, P], F32R)
        z_st = sb("z_st", [P, 2, TOK])
        pZ = ctx.enter_context(nc.psum_tensor("pZ", [P, 2, NCH, CH], F32))
        w_in = [sem(f"win_in{b}") for b in range(2)]
        gate_placed, hi_done, lo_done = sem("gate_placed"), sem("win_hi_done"), sem("win_lo_done")
        product, copied = sem("z_product"), sem("z_copied")
        raw_free, bank_free = sem("raw_free"), sem("bank_free")
        z_out = [sem(f"z_out{b}") for b in range(2)]
        start_at_one(nc, used)
        block = ctx.enter_context(nc.Block())
        wv = k.w_in.rearrange("(t p) n -> p t n", p=P)
        zv = k.zT.rearrange("(a p) t -> a p t", p=P)
        runs = [(3 * MH // 2, COL_M, 0, ACT.Copy), (MH // 2, COL_O, 3 * MH, ACT.Sigmoid),
                (KD, COL_GA, 4 * MH, ACT.Sigmoid)]
        n_tiles = 1 + sum(2 * r[0] for r in runs)

        @block.sync
        def _(sp):
            gates = wv[:, :, COL_GATE:COL_GATE + N_GATE]
            sp.wait_ge(gate_placed, 2)
            for q, g in ((0, 0), (2, 1), (1, 2), (3, 3)):
                sp.dma_start(raw[:, 0, :, 32 * q:32 * q + MH], gates[:, :, g * MH:(g + 1) * MH]).then_inc(w_in[0], 16)
            done = 0
            for pairs, col, _, _ in runs:
                with sp.Fori(0, pairs) as i:
                    for u in range(2):
                        f, b, n = ring(i, 1 + done + u)
                        sp.wait_ge(raw_free, f + 2)
                        sp.dma_start(raw[:, b, :, :], wv[:, :, bass.ds(col + (2 * i + u) * P, P)]).then_inc(w_in[b], 16)
                done += 2 * pairs

        @block.vector
        def _(dve):
            dve.memset(raw[:, 0, :, :], 0.0).then_inc(gate_placed, 1)
            dve.sem_inc(raw_free, 2)

            def split(f, b, n):
                dve.wait_ge(w_in[b], (16 * (n + 1) + (48 if b == 0 else 0)) + 1)
                dve.wait_ge(product, NCH * f + 1)
                dve.tensor_copy(w_hi[:, b], raw[:, b]).then_inc(hi_done, 1)
                dve.wait_ge(hi_done, f + 2)
                dve.tensor_tensor(w_lo[:, b], raw[:, b], w_hi[:, b].bitcast(F32), ALU.subtract).then_inc(lo_done, 1)
                dve.wait_ge(lo_done, f + 2)
                dve.sem_inc(raw_free, 1)

            split(*ring(0, 0))
            with dve.Fori(0, (n_tiles - 1) // 2) as i:
                for u in range(2):
                    split(*ring(i, 1 + u))

        @block.tensor
        def _(pe):
            pe.sem_inc(product, NCH)

            def products(f, b, n):
                pe.wait_ge(lo_done, f + 2)
                for c in range(NCH):
                    pe.wait_ge(bank_free, NCH * f + c + 2)
                    for kt in range(KD):
                        last = mm3(pe, pZ[:, b, c, :], w_hi[:, b, kt, :], w_lo[:, b, kt, :],
                                   hT_hi[:, kt, c * CH:(c + 1) * CH], hT_lo[:, kt, c * CH:(c + 1) * CH],
                                   kt == 0, kt == KD - 1)
                    last.then_inc(product, 1)

            products(*ring(0, 0))
            with pe.Fori(0, (n_tiles - 1) // 2) as i:
                for u in range(2):
                    products(*ring(i, 1 + u))

        @block.scalar
        def _(act):
            act.sem_inc(bank_free, 2 * NCH)

            def evacuate(f, b, n, func, dst):
                for c in range(NCH):
                    act.wait_ge(product, NCH * (f + 1) + c + 2)
                    act.activation(dst[:, c * CH:(c + 1) * CH], pZ[:, b, c, :], func).then_inc(bank_free, 1)

            evacuate(*ring(0, 0), ACT.Copy, k.gates)
            done = 0
            for pairs, _, tile0, func in runs:
                with act.Fori(0, pairs) as i:
                    for u in range(2):
                        f, b, n = ring(i, 1 + done + u)
                        act.wait_ge(z_out[b], (16 * (n - (1 if b == 0 else 0))) + 1)
                        evacuate(f, b, n, func, z_st[:, b, :])
                        act.wait_ge(bank_free, NCH * (f + 3) + 1)
                        act.dma_start(zv[bass.ds(tile0 + 2 * i + u, 1)].rearrange("a p t -> (a p) t"),
                                      z_st[:, b, :]).then_inc(z_out[b], 16)
                done += 2 * pairs
            for b in range(2):
                act.wait_ge(z_out[b], 16 * (n_tiles - 1) // 2 + 1)


def gate_scans(nc, k):
    with ExitStack() as ctx:
        def sb(name, shape, dt=F32):
            return ctx.enter_context(nc.sbuf_tensor(name, shape, dt))

        used = []

        def sem(name):
            used.append(ctx.enter_context(nc.semaphore(name)))
            return used[-1]

        R = 64
        bias_i, bias_f = sb("bias_i", [R, 1]), sb("bias_f", [R, 1])
        gi, gf = sb("gi", [R, TOK]), sb("gf", [R, TOK])
        t0, t1 = sb("gate_t0", [R, TOK]), sb("gate_t1", [R, TOK])
        ones = sb("gate_ones", [R, TOK])
        cum, top = sb("gate_cum", [R, TOK]), sb("gate_top", [R, TOK])
        pA = ctx.enter_context(nc.psum_tensor("pGateA", [P, 2, 8, R], F32))
        pM = ctx.enter_context(nc.psum_tensor("pGateM", [P, 2, 8, R], F32))
        zeroed, bias_in, a_step, v_step = sem("bias_zeroed"), sem("bias_in"), sem("gate_act"), sem("gate_dve")
        turned, cols, out = sem("gate_turned"), sem("gate_cols"), sem("gate_out")
        start_at_one(nc, used)
        block = ctx.enter_context(nc.Block())
        segs = ((0, SEG_TILES[0] * P), (SEG_TILES[0] * P, TOK))

        @block.sync
        def _(sp):
            sp.wait_ge(zeroed, 3)
            for q, g, dst in ((0, 0, bias_i), (0, 1, bias_f), (1, 2, bias_i), (1, 3, bias_f)):
                sp.dma_start(dst[32 * q:32 * q + MH, :],
                             k.b_if[g * MH:(g + 1) * MH].rearrange("(p a) -> p a", a=1)).then_inc(bias_in, 16)
            sp.wait_ge(v_step, 8)
            for d in range(2):
                sp.dma_start(k.negA[d * MH:(d + 1) * MH, :], t1[32 * d:32 * d + MH, :]).then_inc(out, 16)
            sp.wait_ge(out, 33)

        @block.scalar
        def _(act):
            act.wait_ge(bias_in, 65)
            act.activation(gi[:, :], k.gates[0:R, :], ACT.Identity, bias=bias_i[:, 0:1]).then_inc(a_step, 1)
            act.activation(gf[:, :], k.gates[R:2 * R, :], ACT.Identity, bias=bias_f[:, 0:1]).then_inc(a_step, 1)
            act.wait_ge(a_step, 3)
            act.activation(t0[:, :], gf[:, :], ACT.Abs).then_inc(a_step, 1)
            act.wait_ge(a_step, 4)
            act.activation(t1[:, :], t0[:, :], ACT.Exp, scale=-1.0).then_inc(a_step, 1)
            act.wait_ge(a_step, 5)
            act.activation(t0[:, :], t1[:, :], ACT.Ln, bias=k.one[0:R, 0:1]).then_inc(a_step, 1)
            act.wait_ge(turned, 3)
            act.wait_ge(cols, 2)
            for half in range(2):
                n = 8 if half == 0 else NT - 8
                for d in range(2):
                    act.activation(k.floor[:, d, 8 * half:8 * half + n, :], pM[:, half, 0:n, 32 * d:32 * d + MH],
                                   ACT.Exp).then_inc(a_step, 1)
            act.wait_ge(a_step, 10)

        @block.vector
        def _(dve):
            dve.memset(bias_i[:, :], 0.0).then_inc(zeroed, 1)
            dve.memset(bias_f[:, :], 0.0).then_inc(zeroed, 1)
            dve.memset(ones[:, :], 1.0).then_inc(v_step, 1)
            dve.wait_ge(a_step, 6)
            dve.scalar_tensor_tensor(out=gf[:, :], in0=gf[:, :], scalar=0.0, in1=t0[:, :],
                                     op0=ALU.min, op1=ALU.subtract).then_inc(v_step, 1)
            dve.wait_ge(v_step, 3)

            def scans(out_t, data0, data1, op0, op1):
                for s0, s1 in segs:
                    dve.tensor_tensor_scan(out_t[0:32, s0:s1], data0[0:32, s0:s1], data1[0:32, s0:s1], 0.0,
                                           op0, op1)
                    rev = slice(s1 - 1, s0 - 1 if s0 else None, -1)
                    last = dve.tensor_tensor_scan(out_t[32:64, rev], data0[32:64, rev], data1[32:64, rev],
                                                  0.0, op0, op1)
                last.then_inc(v_step, 1)

            scans(cum, ones, gf, ALU.mult, ALU.add)
            dve.wait_ge(v_step, 4)
            dve.tensor_tensor(gi[:, :], gi[:, :], cum[:, :], ALU.subtract).then_inc(v_step, 1)
            dve.wait_ge(v_step, 5)
            scans(top, ones, gi, ALU.mult, ALU.max)
            dve.wait_ge(v_step, 6)
            dve.tensor_scalar(t1[:, :], top[:, :], -1.0, None, ALU.mult).then_inc(v_step, 1)
            dve.wait_ge(v_step, 7)
            dve.tensor_tensor(t0[:, :], t1[:, :], cum[:, :], ALU.subtract).then_inc(v_step, 1)
            dve.wait_ge(turned, 3)
            for half in range(2):
                n = 8 if half == 0 else NT - 8
                for d in range(2):
                    last = dve.tensor_copy(k.a_col[:, d, 8 * half:8 * half + n, :],
                                           pA[:, half, 0:n, 32 * d:32 * d + MH])
            last.then_inc(cols, 1)
            dve.wait_ge(cols, 2)

        @block.tensor
        def _(pe):
            pe.wait_ge(v_step, 8)
            for src, dst in ((gi, pA), (t0, pM)):
                for t in range(NT):
                    last = pe.transpose(dst[:, t // 8, t % 8, :], src[:, t * P:(t + 1) * P], k.ident[0:R, 0:R])
                last.then_inc(turned, 1)


def attention(nc, k):
    with ExitStack() as ctx:
        def sb(name, shape, dt=F32):
            return ctx.enter_context(nc.sbuf_tensor(name, shape, dt))

        used = []

        def sem(name):
            used.append(ctx.enter_context(nc.semaphore(name)))
            return used[-1]

        H2 = HEAD
        q_raw, k_raw = sb("q_raw", [P, TOK]), sb("k_raw", [P, TOK])
        v_raw = sb("v_raw", [P, NT, H2])
        q_stack = [sb(f"q_stack{h}", [P, TOK], F32R) for h in range(2)]
        k_hi = sb("k_hi", [P, TOK], F32R)
        k_lo = [sb(f"k_lo{h}", [P, TOK], F32R) for h in range(2)]
        v_both = sb("v_both", [P, NT, 2 * H2], F32R)
        v_high = sb("v_high", [P, NT, 2 * H2], F32R)
        probs = sb("probs", [P, 2, 8 * P])
        pT_hi = sb("pT_hi", [P, 2, 8, CH], F32R)
        pT_lo = sb("pT_lo", [P, 2, 8, CH], F32R)
        o_low = sb("o_low", [H2, CH])
        o_st = sb("o_st", [P, TOK])
        small = sb("att_small", [P, 8])
        pS = ctx.enter_context(nc.psum_tensor("pS", [P, 2, 8 * P], F32))
        pT = ctx.enter_context(nc.psum_tensor("pAT", [P, 2, 4, P], F32))
        pO = ctx.enter_context(nc.psum_tensor("pO", [P, 2, CH], F32))

        zeroed, kv_in, q_in = sem("att_zeroed"), sem("kv_in"), sem("q_in")
        kv_hi, kv_split, q_hi, q_split = sem("kv_hi"), sem("kv_split"), sem("q_hi"), sem("q_split")
        scored, maxed, negated, exped = sem("scored"), sem("maxed"), sem("negated"), sem("exped")
        inverted, normed, turned = sem("inverted"), sem("normed"), sem("turned")
        hi_done, lo_done, weighed = sem("pT_hi_done"), sem("pT_lo_done"), sem("weighed")
        low_copied, o_added, o_out = sem("low_copied"), sem("o_added"), sem("o_out")
        start_at_one(nc, used)
        block = ctx.enter_context(nc.Block())

        GROUPS = [(h, c) for h in range(2) for c in range(NCH)]
        UNITS = [(h, c, qb) for h, c in GROUPS for qb in range(CH // P)]
        KT = {c: SEG_OF_CHUNK[c][1] - SEG_OF_CHUNK[c][0] for c in range(NCH)}
        NU, NG = len(UNITS), len(GROUPS)
        quads = [(u, q) for u, (h, c, qb) in enumerate(UNITS) for q in range(KT[c] // 4)]
        NQD = len(quads)
        quads_before = [sum(1 for x in quads if x[0] < u) for u in range(NU + 1)]

        def pairs(eng, body, per_kv=None):
            with eng.Fori(0, NKV) as g:
                if per_kv:
                    per_kv(g)
                with eng.Fori(0, 2) as j:
                    body(2 * g + j)

        @block.sync
        def _(sp):
            def load_kv(g):
                wait_apart(sp, k, weighed, 2 * NG * g + 1)
                wait_apart(sp, k, kv_split, 4 * g + 1)
                for half in range(2):
                    sp.dma_start(k_raw[half * H2:(half + 1) * H2, :],
                                 k.qkT[bass.ds(NQ * HEAD + g * H2, H2), :]).then_inc(kv_in, 16)
                sp.dma_start(v_raw[:, :, :], k.v[:, bass.ds(g * H2, H2)].rearrange("(t p) d -> p t d", p=P))\
                  .then_inc(kv_in, 16)

            def load_q(n):
                wait_apart(sp, k, q_split, 2 * n + 1)
                sp.dma_start(q_raw[:, :], k.qkT[bass.ds(n * P, P), :]).then_inc(q_in, 16)

            pairs(sp, load_q, load_kv)

        @block.gpsimd
        def _(pool):
            pool.memset(k_lo[0][H2:P, :].bitcast(F32), 0.0).then_inc(zeroed, 1)
            pool.wait_ge(zeroed, 2)
            pool.memset(k_lo[1][0:H2, :].bitcast(F32), 0.0).then_inc(zeroed, 1)
            pool.wait_ge(zeroed, 3)
            pool.memset(v_high[:, :, H2:2 * H2].bitcast(F32), 0.0).then_inc(zeroed, 1)
            pool.wait_ge(zeroed, 4)

        @block.scalar
        def _(act):
            def split_kv(g):
                act.wait_ge(kv_in, 48 * (g + 1) + 1)
                act.wait_ge(weighed, 2 * NG * g + 1)
                act.activation(k_hi[:, :], k_raw[:, :], ACT.Copy).then_inc(kv_hi, 1)
                act.activation(v_both[:, :, 0:H2], v_raw[:, :, :], ACT.Copy).then_inc(kv_hi, 1)
                act.activation(v_high[:, :, 0:H2], v_raw[:, :, :], ACT.Copy).then_inc(kv_hi, 1)

            def exp(n, u):
                h, c, qb = UNITS[u]
                b = u % 2
                act.wait_ge(negated, n * NU + u + 2)
                act.wait_ge(turned, (n * NQD + (quads_before[u - 1] if u >= 2 else 0)) + 1)
                act.activation(probs[:, b, 0:KT[c] * P], pS[:, b, 0:KT[c] * P], ACT.Exp, scale=HEAD ** -0.5,
                               bias=small[:, 2 + b:3 + b], accum_out=small[:, 4 + b:5 + b]).then_inc(exped, 1)

            def keep_hi(n, u):
                h, c, qb = UNITS[u]
                g = u // 4
                for q in range(KT[c] // 4):
                    at = quads_before[u] + q
                    act.wait_ge(turned, n * NQD + at + 2)
                    act.wait_ge(weighed, n * NG + max(g - 1, 0) + 1)
                    act.activation(pT_hi[:, g % 2, 4 * q:4 * q + 4, qb * P:(qb + 1) * P], pT[:, at % 2, :, :],
                                   ACT.Copy).then_inc(hi_done, 1)

            def low_half(n, g):
                act.wait_ge(weighed, n * NG + g + 2)
                act.wait_ge(o_added, n * NG + g + 1)
                act.activation(o_low[:, :], pO[H2:P, g % 2, :], ACT.Copy).then_inc(low_copied, 1)

            def pair(n):
                act.wait_ge(q_in, 16 * (n + 1) + 1)
                act.wait_ge(weighed, n * NG + 1)
                act.activation(q_stack[0][0:H2, :], q_raw[0:H2, :], ACT.Copy).then_inc(q_hi, 1)
                act.activation(q_stack[1][H2:P, :], q_raw[H2:P, :], ACT.Copy).then_inc(q_hi, 1)
                exp(n, 0)
                for u in range(NU):
                    if u + 1 < NU:
                        exp(n, u + 1)
                    keep_hi(n, u)
                    if u % 4 == 1 and u > 4:
                        low_half(n, u // 4 - 1)
                low_half(n, NG - 1)
                act.wait_ge(o_added, (n + 1) * NG + 1)
                act.dma_start(k.aT[bass.ds(n * P, P), :], o_st[:, :]).then_inc(o_out, 16)

            pairs(act, pair, split_kv)
            act.wait_ge(o_out, 16 * 4 + 1)

        @block.vector
        def _(dve):
            dve.wait_ge(zeroed, 4)

            def split_kv(g):
                dve.wait_ge(kv_hi, 3 * g + 4)
                dve.tensor_tensor(k_lo[0][0:H2, :], k_raw[0:H2, :], k_hi[0:H2, :].bitcast(F32),
                                  ALU.subtract).then_inc(kv_split, 1)
                dve.tensor_tensor(k_lo[1][H2:P, :], k_raw[H2:P, :], k_hi[H2:P, :].bitcast(F32),
                                  ALU.subtract).then_inc(kv_split, 1)
                dve.tensor_tensor(v_both[:, :, H2:2 * H2], v_raw[:, :, :], v_both[:, :, 0:H2].bitcast(F32),
                                  ALU.subtract).then_inc(kv_split, 2)

            def row_max(n, u):
                h, c, qb = UNITS[u]
                b = u % 2
                dve.wait_ge(scored, n * NU + u + 2)
                dve.tensor_reduce(small[:, b:b + 1], pS[:, b, 0:KT[c] * P], AX_X, ALU.max).then_inc(maxed, 1)
                dve.wait_ge(maxed, n * NU + u + 2)
                dve.wait_ge(exped, n * NU + max(u - 1, 0) + 1)
                dve.tensor_scalar(small[:, 2 + b:3 + b], small[:, b:b + 1], -HEAD ** -0.5, None,
                                  ALU.mult).then_inc(negated, 1)

            def normalise(n, u):
                b = u % 2
                """Rows of P times the inverse of their sums."""
                h, c, qb = UNITS[u]
                dve.wait_ge(exped, n * NU + u + 2)
                dve.wait_ge(normed, n * NU + max(u - 1, 0) + 1)
                dve.reciprocal(small[:, 6 + b:7 + b], small[:, 4 + b:5 + b]).then_inc(inverted, 1)
                dve.wait_ge(inverted, n * NU + u + 2)
                dve.tensor_scalar(probs[:, b, 0:KT[c] * P], probs[:, b, 0:KT[c] * P], small[:, 6 + b:7 + b],
                                  None, ALU.mult).then_inc(normed, 1)

            def keep_lo(n, u):
                h, c, qb = UNITS[u]
                g = u // 4
                for q in range(KT[c] // 4):
                    at = quads_before[u] + q
                    dve.wait_ge(hi_done, n * NQD + at + 2)
                    dve.tensor_tensor(pT_lo[:, g % 2, 4 * q:4 * q + 4, qb * P:(qb + 1) * P], pT[:, at % 2, :, :],
                                      pT_hi[:, g % 2, 4 * q:4 * q + 4, qb * P:(qb + 1) * P].bitcast(F32),
                                      ALU.subtract).then_inc(lo_done, 1)

            def add(n, g):
                h, c = GROUPS[g]
                dve.wait_ge(low_copied, n * NG + g + 2)
                if g == 0:
                    dve.wait_ge(o_out, 16 * n + 1)
                dve.tensor_tensor(o_st[h * H2:(h + 1) * H2, c * CH:(c + 1) * CH], pO[0:H2, g % 2, :], o_low[:, :],
                                  ALU.add).then_inc(o_added, 1)

            def pair(n):
                dve.wait_ge(q_hi, 2 * (n + 1) + 1)
                dve.tensor_tensor(q_stack[0][H2:P, :], q_raw[0:H2, :], q_stack[0][0:H2, :].bitcast(F32),
                                  ALU.subtract).then_inc(q_split, 1)
                dve.tensor_tensor(q_stack[1][0:H2, :], q_raw[H2:P, :], q_stack[1][H2:P, :].bitcast(F32),
                                  ALU.subtract).then_inc(q_split, 1)
                row_max(n, 0)
                for u in range(NU):
                    normalise(n, u)
                    if u + 1 < NU:
                        row_max(n, u + 1)
                    keep_lo(n, u)
                    if u % 4 == 1 and u > 4:
                        add(n, u // 4 - 1)
                add(n, NG - 1)

            pairs(dve, pair, split_kv)

        @block.tensor
        def _(pe):
            def scores(n, u):
                h, c, qb = UNITS[u]
                b = u % 2
                k0 = SEG_OF_CHUNK[c][0] * P
                q0 = c * CH + qb * P
                pe.wait_ge(exped, n * NU + max(u - 1, 0) + 1)
                for s in range(KT[c] * P // CH):
                    keys = slice(k0 + s * CH, k0 + (s + 1) * CH)
                    out = pS[:, b, s * CH:(s + 1) * CH]
                    pe.matmul(out, q_stack[h][:, q0:q0 + P], k_hi[:, keys], start=True, stop=False)
                    last = pe.matmul(out, q_stack[h][:, q0:q0 + P], k_lo[h][:, keys], start=False, stop=True)
                last.then_inc(scored, 1)

            def turn(n, u):
                h, c, qb = UNITS[u]
                pe.wait_ge(normed, n * NU + u + 2)
                for q in range(KT[c] // 4):
                    at = quads_before[u] + q
                    pe.wait_ge(lo_done, n * NQD + max(at - 1, 0) + 1)
                    for i in range(4):
                        kt = 4 * q + i
                        last = pe.transpose(pT[:, at % 2, i, :], probs[:, u % 2, kt * P:(kt + 1) * P], k.ident[:, :])
                    last.then_inc(turned, 1)

            def weigh(n, g):
                h, c = GROUPS[g]
                t0 = SEG_OF_CHUNK[c][0]
                pe.wait_ge(lo_done, n * NQD + quads_before[4 * g + 4] + 1)
                pe.wait_ge(o_added, n * NG + max(g - 1, 0) + 1)
                for i in range(KT[c]):
                    pe.matmul(pO[:, g % 2, :], v_both[:, t0 + i, :], pT_hi[:, g % 2, i, :],
                              start=(i == 0), stop=False)
                    last = pe.matmul(pO[:, g % 2, :], v_high[:, t0 + i, :], pT_lo[:, g % 2, i, :],
                                     start=False, stop=(i == KT[c] - 1))
                last.then_inc(weighed, 1)

            def wait_kv(g):
                wait_apart(pe, k, kv_split, 4 * g + 4 + 1)

            def pair(n):
                pe.wait_ge(q_split, 2 * (n + 1) + 1)
                scores(n, 0)
                for u in range(NU):
                    if u + 1 < NU:
                        scores(n, u + 1)
                    turn(n, u)
                    if u % 4 == 0 and u > 0:
                        weigh(n, u // 4 - 1)
                weigh(n, NG - 1)

            pairs(pe, pair, wait_kv)


def mlstm(nc, k):
    with ExitStack() as ctx:
        def sb(name, shape, dt=F32):
            return ctx.enter_context(nc.sbuf_tensor(name, shape, dt))

        used = []

        def sem(name):
            used.append(ctx.enter_context(nc.semaphore(name)))
            return used[-1]

        VW = MD + 2
        q_raw, k_raw, v_raw = sb("mq_raw", [P, TOK]), sb("mk_raw", [P, TOK]), sb("mv_raw", [P, TOK])
        negA = sb("negA_rows", [P, 2, TOK])
        negA_m = sb("negA_masked", [P, 2, TOK])
        q_hi, q_lo = sb("mq_hi", [P, TOK], F32R), sb("mq_lo", [P, TOK], F32R)
        k_hi, k_lo = sb("mk_hi", [P, TOK], F32R), sb("mk_lo", [P, TOK], F32R)
        v_hi, v_lo = sb("mv_hi", [P, NT, VW], F32R), sb("mv_lo", [P, NT, MD], F32R)
        decay = sb("decay", [P, 2, CH])
        w_all = sb("w_all", [P, 2, CH])
        w_hi, w_lo = sb("mw_hi", [P, 2, CH], F32R), sb("mw_lo", [P, 2, CH], F32R)
        h_num = sb("h_num", [P, 2, 4, VW])
        floor_c = sb("floor_c", [P, 3, 2, 4])
        part = sb("h_part", [P, 2, 4, MD])
        a_head = sb("a_head", [P, 2, NT])
        pS = ctx.enter_context(nc.psum_tensor("pMS", [P, 2, CH], F32))
        pW = ctx.enter_context(nc.psum_tensor("pMW", [P, 2, 4, 256], F32))
        pV = ctx.enter_context(nc.psum_tensor("pMV", [P, 2, 4, MD], F32))

        fixed, head_in, hi_qk, split = sem("m_fixed"), sem("head_in"), sem("m_hi"), sem("m_split")
        masked, v_turned, v_hi_done, v_split = sem("masked"), sem("v_turned"), sem("v_hi_done"), sem("v_split")
        scored, decayed, multiplied = sem("m_scored"), sem("decayed"), sem("multiplied")
        hi_done, lo_done, weighed, summed = sem("w_hi_done"), sem("w_lo_done"), sem("m_weighed"), sem("m_summed")
        copied_f, copied_b, steps = sem("copied_f"), sem("copied_b"), sem("m_steps")
        scaled, added, a_ready = sem("m_scaled"), sem("m_added"), sem("a_ready")
        start_at_one(nc, used)
        block = ctx.enter_context(nc.Block())

        STEPS = [(c, i) for c in range(NCH) for i in range(*SEG_OF_CHUNK[c])]
        ITEMS = []
        for s, (c, i) in enumerate(STEPS):
            r = i - 4 * c
            if r <= 3:
                ITEMS.append((s, 0, max(r, 0), 4, r if r >= 0 else None))
            if r >= 0:
                ITEMS.append((s, 1, 0, min(r, 3) + 1, r if r <= 3 else None))
        NS, NI = len(STEPS), len(ITEMS)
        first_item = [min(m for m, x in enumerate(ITEMS) if x[0] == s) for s in range(NS)] + [NI]
        last_of_chunk = [max(m for m, x in enumerate(ITEMS) if STEPS[x[0]][0] == c) for c in range(NCH)]
        zrow = k.zT.rearrange("(a p) t -> a p t", p=P)

        @block.sync
        def _(sp):
            with sp.Fori(0, MH) as n:
                wait_apart(sp, k, split, 2 * n + 1)
                wait_apart(sp, k, v_turned, 3 * n + 1)
                sp.wait_ge(decayed, NI * n + 1)
                for dst, a in ((q_raw, n), (k_raw, MH + n), (v_raw, 2 * MH + n)):
                    sp.dma_start(dst[:, :], zrow[bass.ds(a, 1)].rearrange("a p t -> (a p) t")).then_inc(head_in, 16)
                for d in range(2):
                    sp.dma_start(negA[:, d, :], k.negA[bass.ds(d * MH + n, 1), :]
                                 .rearrange("a t -> (a t)").partition_broadcast(P)).then_inc(head_in, 16)

        @block.gpsimd
        def _(pool):
            pool.memset(v_hi[:, :, MD:MD + 1].bitcast(F32), 1.0).then_inc(fixed, 1)
            pool.memset(v_hi[:, :, MD + 1:VW].bitcast(F32), 0.0).then_inc(fixed, 1)
            with pool.Fori(0, MH) as n:
                pool.wait_ge(head_in, 80 * (n + 1) + 1)
                for d in range(2):
                    pool.tensor_tensor(negA_m[:, d, :].rearrange("p (t s) -> p t s", s=P),
                                       negA[:, d, :].rearrange("p (t s) -> p t s", s=P),
                                       k.mask[:, d:d + 1, :].to_broadcast([P, NT, P]), ALU.add).then_inc(masked, 1)
                for c in range(NCH):
                    pool.wait_ge(steps, 3 * (NCH * n + c) + 4)
                    pool.wait_ge(added, NCH * n + c + 1)
                    for d in range(2):
                        pool.tensor_tensor(part[:, d, :, :], h_num[:, d, :, 0:MD],
                                           floor_c[:, 2, d, :].unsqueeze(2).to_broadcast([P, 4, MD]),
                                           ALU.mult).then_inc(scaled, 1)
                    pool.wait_ge(scaled, 2 * (NCH * n + c) + 3)
                    pool.tensor_tensor(k.h_sum[:, 4 * c:4 * c + 4, bass.ds(n, 1), :]
                                       .rearrange("p t a d -> p t (a d)"),
                                       part[:, 0, :, :], part[:, 1, :, :], ALU.add).then_inc(added, 1)
            pool.wait_ge(added, NCH * MH + 1)

        @block.scalar
        def _(act):
            with act.Fori(0, MH) as n:
                act.wait_ge(head_in, 80 * (n + 1) + 1)
                act.wait_ge(weighed, NI * n + 1)
                act.activation(q_hi[:, :], q_raw[:, :], ACT.Copy).then_inc(hi_qk, 1)
                act.activation(k_hi[:, :], k_raw[:, :], ACT.Copy, scale=MD ** -0.5).then_inc(hi_qk, 1)
                for q in range(3):
                    act.wait_ge(v_turned, 3 * n + q + 2)
                    act.activation(v_hi[:, 4 * q:4 * q + 4, 0:MD], pV[:, q % 2, :, :], ACT.Copy).then_inc(v_hi_done, 1)

                def decays(m):
                    s, d, b0, b1, diag = ITEMS[m]
                    c, i = STEPS[s]
                    act.wait_ge(multiplied, NI * n + max(m - 1, 0) + 1)
                    bias = a_head[:, d, i:i + 1]
                    for lo, hi, rows in ((b0, diag if diag is not None else b0, negA),
                                         (diag if diag is not None else b0, diag + 1 if diag is not None else b0, negA_m),
                                         (diag + 1 if diag is not None else b0, b1, negA)):
                        if lo < hi:
                            last = act.activation(decay[:, m % 2, lo * P:hi * P],
                                                  rows[:, d, c * CH + lo * P:c * CH + hi * P], ACT.Exp, bias=bias)
                    last.then_inc(decayed, 1)

                def keep_hi(m):
                    s, d, b0, b1, _ = ITEMS[m]
                    act.wait_ge(multiplied, NI * n + m + 2)
                    act.wait_ge(weighed, NI * n + max(m - 1, 0) + 1)
                    act.activation(w_hi[:, m % 2, b0 * P:b1 * P], w_all[:, m % 2, b0 * P:b1 * P],
                                   ACT.Copy).then_inc(hi_done, 1)

                act.wait_ge(masked, 2 * (n + 1) + 1)
                act.wait_ge(a_ready, n + 2)
                decays(0)
                for m in range(NI):
                    if m + 1 < NI:
                        decays(m + 1)
                    keep_hi(m)
                    for c in range(NCH):
                        if m == min(last_of_chunk[c] + 1, NI - 1):
                            act.wait_ge(weighed, NI * n + last_of_chunk[c] + 2)
                            act.wait_ge(scaled, 2 * (NCH * n + c) + 1)
                            act.activation(h_num[:, 0, :, :], pW[:, 0, :, 0:VW], ACT.Copy).then_inc(copied_f, 1)

        @block.vector
        def _(dve):
            with dve.Fori(0, MH) as n:
                dve.wait_ge(decayed, NI * n + 1)
                dve.tensor_scalar(a_head[:, :, :], k.a_col[:, :, :, bass.ds(n, 1)].rearrange("p d t a -> p d (t a)"),
                                  1.0, None, ALU.mult).then_inc(a_ready, 1)
                dve.wait_ge(hi_qk, 2 * (n + 1) + 1)
                dve.tensor_tensor(q_lo[:, :], q_raw[:, :], q_hi[:, :].bitcast(F32), ALU.subtract).then_inc(split, 1)
                dve.scalar_tensor_tensor(out=k_lo[:, :], in0=k_raw[:, :], scalar=MD ** -0.5,
                                         in1=k_hi[:, :].bitcast(F32), op0=ALU.mult, op1=ALU.subtract).then_inc(split, 1)
                for q in range(3):
                    dve.wait_ge(v_hi_done, 3 * n + q + 2)
                    dve.tensor_tensor(v_lo[:, 4 * q:4 * q + 4, :], pV[:, q % 2, :, :],
                                      v_hi[:, 4 * q:4 * q + 4, 0:MD].bitcast(F32), ALU.subtract).then_inc(v_split, 1)

                def multiply(m):
                    s, d, b0, b1, _ = ITEMS[m]
                    dve.wait_ge(decayed, NI * n + m + 2)
                    dve.wait_ge(scored, NS * n + s + 2)
                    dve.wait_ge(lo_done, NI * n + max(m - 1, 0) + 1)
                    dve.tensor_tensor(w_all[:, m % 2, b0 * P:b1 * P], decay[:, m % 2, b0 * P:b1 * P],
                                      pS[:, s % 2, b0 * P:b1 * P], ALU.mult).then_inc(multiplied, 1)

                def keep_lo(m):
                    s, d, b0, b1, _ = ITEMS[m]
                    dve.wait_ge(hi_done, NI * n + m + 2)
                    dve.tensor_tensor(w_lo[:, m % 2, b0 * P:b1 * P], w_all[:, m % 2, b0 * P:b1 * P],
                                      w_hi[:, m % 2, b0 * P:b1 * P].bitcast(F32), ALU.subtract).then_inc(lo_done, 1)

                def denominators(c):
                    at = NCH * n + c
                    dve.wait_ge(weighed, NI * n + last_of_chunk[c] + 2)
                    dve.wait_ge(scaled, 2 * at + 1)
                    dve.tensor_copy(h_num[:, 1, :, :], pW[:, 1, :, 0:VW]).then_inc(copied_b, 1)
                    dve.wait_ge(copied_f, at + 2)
                    dve.wait_ge(copied_b, at + 2)
                    den = h_num[:, :, :, MD]
                    dve.scalar_tensor_tensor(out=floor_c[:, 0, :, :], in0=den, scalar=-1.0, in1=den,
                                             op0=ALU.mult, op1=ALU.max).then_inc(steps, 1)
                    dve.wait_ge(steps, 3 * at + 2)
                    dve.tensor_tensor(floor_c[:, 1, :, :], floor_c[:, 0, :, :],
                                      k.floor[:, :, 4 * c:4 * c + 4, bass.ds(n, 1)].rearrange("p d t a -> p d (t a)"),
                                      ALU.max).then_inc(steps, 1)
                    dve.wait_ge(steps, 3 * at + 3)
                    dve.reciprocal(floor_c[:, 2, :, :], floor_c[:, 1, :, :]).then_inc(steps, 1)

                multiply(0)
                for m in range(NI):
                    if m + 1 < NI:
                        multiply(m + 1)
                    keep_lo(m)
                    for c in range(NCH):
                        if m == min(last_of_chunk[c] + 1, NI - 1):
                            denominators(c)

        @block.tensor
        def _(pe):
            pe.wait_ge(fixed, 3)
            with pe.Fori(0, MH) as n:
                pe.wait_ge(head_in, 80 * (n + 1) + 1)
                for q in range(3):
                    pe.wait_ge(v_split, 3 * n + max(q - 1, 0) + 1)
                    for a in range(4):
                        t = 4 * q + a
                        last = pe.transpose(pV[:, q % 2, a, :], v_raw[:, t * P:(t + 1) * P], k.ident[:, :])
                    last.then_inc(v_turned, 1)

                def scores(s):
                    c, i = STEPS[s]
                    pe.wait_ge(multiplied, (NI * n + (first_item[s - 1] if s >= 2 else 0)) + 1)
                    mm3(pe, pS[:, s % 2, :], k_hi[:, i * P:(i + 1) * P], k_lo[:, i * P:(i + 1) * P],
                        q_hi[:, c * CH:(c + 1) * CH], q_lo[:, c * CH:(c + 1) * CH], True, True).then_inc(scored, 1)

                def weigh(m, begun):
                    s, d, b0, b1, _ = ITEMS[m]
                    c, i = STEPS[s]
                    pe.wait_ge(lo_done, NI * n + m + 2)
                    if s == 0 or STEPS[s - 1][0] != c:
                        pe.wait_ge(copied_f, NCH * n + c + 1)
                        pe.wait_ge(copied_b, NCH * n + c + 1)
                        if m == first_item[s]:
                            begun.clear()
                    for b in range(b0, b1):
                        out = pW[:, d, b, :]
                        start = (d, b // 2) not in begun
                        begun.add((d, b // 2))
                        blk = slice(b * P, (b + 1) * P)
                        pe.matmul(out[:, 0:VW], w_hi[:, m % 2, blk], v_hi[:, i, :], start=start, stop=False,
                                  skip_group_check=True)
                        pe.matmul(out[:, 0:VW], w_lo[:, m % 2, blk], v_hi[:, i, :], start=False, stop=False,
                                  skip_group_check=True)
                        last = pe.matmul(out[:, 0:MD], w_hi[:, m % 2, blk], v_lo[:, i, :], start=False, stop=True,
                                         skip_group_check=True)
                    last.then_inc(weighed, 1)

                pe.wait_ge(split, 2 * (n + 1) + 1)
                pe.wait_ge(v_split, 3 * (n + 1) + 1)
                begun = set()
                scores(0)
                for s in range(NS):
                    if s + 1 < NS:
                        scores(s + 1)
                    for m in range(first_item[s], first_item[s + 1]):
                        weigh(m, begun)


def mlstm_norm(nc, k):
    with ExitStack() as ctx:
        def sb(name, shape, dt=F32):
            return ctx.enter_context(nc.sbuf_tensor(name, shape, dt))

        used = []

        def sem(name):
            used.append(ctx.enter_context(nc.semaphore(name)))
            return used[-1]

        gain = sb("m_gain", [P, MH, MD])
        sq = sb("m_sq", [P, 2, MH, MD])
        hn = sb("m_hn", [P, 2, MH, MD])
        sig_o = sb("sig_o", [P, 2, MH, P])
        mT_st = sb("mT_st", [P, 2, MH, P])
        stat = sb("m_stat", [P, 2, 3, MH])
        pT = ctx.enter_context(nc.psum_tensor("pNT", [P, 2, MH, P], F32))
        gain_in, o_in = sem("m_gain_in"), [sem(f"o_in{b}") for b in range(2)]
        squared, summed, rooted, inverted = sem("n_squared"), sem("n_summed"), sem("n_rooted"), sem("n_inverted")
        scaled, gained, turned, gated = sem("n_scaled"), sem("n_gained"), sem("n_turned"), sem("n_gated")
        out = [sem(f"mT_out{b}") for b in range(2)]
        free = sem("n_slots")
        start_at_one(nc, used)
        block = ctx.enter_context(nc.Block())
        ov = k.zT.rearrange("(a p) t -> p a t", p=P)[:, 3 * MH:4 * MH, :]

        @block.sync
        def _(sp):
            sp.dma_start(gain[:, :, :].rearrange("p h d -> p (h d)"), k.mlstm_norm.partition_broadcast(P)).then_inc(gain_in, 16)
            with sp.Fori(0, NT // 2) as i:
                for u in range(2):
                    t, b, n = ring(i, u)
                    sp.wait_ge(free, t + 2)
                    sp.dma_start(sig_o[:, b, :, :], ov[:, :, bass.ds(t * P, P)]).then_inc(o_in[b], 16)

        @block.scalar
        def _(act):
            with act.Fori(0, NT // 2) as i:
                for u in range(2):
                    t, b, n = ring(i, u)
                    act.wait_ge(free, t + 2)
                    act.activation(unit(sq[:, b:b + 1].rearrange("p a h d -> p a (h d)")),
                                   k.h_sum[:, bass.ds(t, 1), :, :].rearrange("p a h d -> p (a h d)"),
                                   ACT.Square).then_inc(squared, 1)
                    act.wait_ge(summed, t + 2)
                    act.activation(stat[:, b, 1, :], stat[:, b, 0, :], ACT.Sqrt, scale=1.0 / MD,
                                   bias=k.eps[:, 0:1]).then_inc(rooted, 1)
                    act.wait_ge(gated, t + 2)
                    act.dma_start(k.mT.rearrange("(a p) t -> p a t", p=P)[:, :, bass.ds(t * P, P)],
                                  mT_st[:, b, :, :]).then_inc(out[b], 16)
            for b in range(2):
                act.wait_ge(out[b], 16 * (NT // 2) + 1)

        @block.gpsimd
        def _(pool):
            pool.wait_ge(gain_in, 17)
            with pool.Fori(0, NT // 2) as i:
                for u in range(2):
                    t, b, n = ring(i, u)
                    pool.wait_ge(scaled, t + 2)
                    pool.tensor_tensor(hn[:, b], hn[:, b], gain[:, :, :], ALU.mult).then_inc(gained, 1)

        @block.vector
        def _(dve):
            dve.sem_inc(free, 2)
            with dve.Fori(0, NT // 2) as i:
                for u in range(2):
                    t, b, n = ring(i, u)
                    dve.wait_ge(squared, t + 2)
                    dve.tensor_reduce(stat[:, b, 0, :], sq[:, b], AX_X, ALU.add).then_inc(summed, 1)
                    dve.wait_ge(rooted, t + 2)
                    dve.reciprocal(stat[:, b, 2, :], stat[:, b, 1, :]).then_inc(inverted, 1)
                    dve.wait_ge(inverted, t + 2)
                    dve.wait_ge(free, t + 2)
                    dve.tensor_tensor(hn[:, b], k.h_sum[:, bass.ds(t, 1), :, :].rearrange("p a h d -> p (a h) d"),
                                      stat[:, b, 2, :].unsqueeze(2).to_broadcast([P, MH, MD]),
                                      ALU.mult).then_inc(scaled, 1)
                    dve.wait_ge(turned, t + 2)
                    dve.wait_ge(o_in[b], 16 * (n + 1) + 1)
                    dve.wait_ge(out[b], 16 * n + 1)
                    dve.tensor_tensor(mT_st[:, b], pT[:, b], sig_o[:, b], ALU.mult).then_inc(gated, 1)
                    dve.wait_ge(gated, t + 2)
                    dve.sem_inc(free, 1)

        @block.tensor
        def _(pe):
            with pe.Fori(0, NT // 2) as i:
                for u in range(2):
                    t, b, n = ring(i, u)
                    pe.wait_ge(gained, t + 2)
                    pe.wait_ge(free, t + 2)
                    for h in range(MH):
                        last = pe.transpose(pT[:, b, h, :], hn[:, b, h, :], k.ident[:, :])
                    last.then_inc(turned, 1)


def merge(nc, k):
    with ExitStack() as ctx:
        def sb(name, shape, dt=F32):
            return ctx.enter_context(nc.sbuf_tensor(name, shape, dt))

        used = []

        def sem(name):
            used.append(ctx.enter_context(nc.semaphore(name)))
            return used[-1]

        KB = MW // P
        b_raw = sb("branch_raw", [P, 2, TOK])
        b_hi, b_lo = sb("branch_hi", [P, 2 * KB, TOK], F32R), sb("branch_lo", [P, 2 * KB, TOK], F32R)
        raw = sb("wbo_raw", [P, 2, 2 * KB, P])
        w_hi, w_lo = sb("wbo_hi", [P, 2, 2 * KB, P], F32R), sb("wbo_lo", [P, 2, 2 * KB, P], F32R)
        sig = sb("sig_g", [P, 2, 2, TOK])
        gated = sb("gated", [P, 2, CH])
        m_st = sb("merged_st", [P, 2, TOK])
        pB = ctx.enter_context(nc.psum_tensor("pB", [P, 2, 2, CH], F32))
        b_in = [sem(f"branch_in{b}") for b in range(2)]
        b_hi_done, b_split = sem("b_hi_done"), sem("b_split")
        w_in, sig_in = [sem(f"wbo_in{b}") for b in range(2)], [sem(f"sig_in{b}") for b in range(2)]
        hi_done, split = sem("wbo_hi_done"), sem("wbo_split")
        product, mixed, added, slot_free = sem("b_product"), sem("mixed"), sem("m_added2"), sem("wbo_slots")
        out = [sem(f"merged_out{b}") for b in range(2)]
        start_at_one(nc, used)
        block = ctx.enter_context(nc.Block())
        branches = [k.aT.rearrange("(a p) t -> a p t", p=P), k.mT.rearrange("(a p) t -> a p t", p=P)]
        zv = k.zT.rearrange("(a p) t -> a p t", p=P)

        @block.sync
        def _(sp):
            def weights(f, b):
                for w, part in ((k.w_attn_o, 0), (k.w_mlstm_o, 1)):
                    sp.dma_start(raw[:, b, part * KB:(part + 1) * KB, :],
                                 w.rearrange("(t p) n -> p t n", p=P)[:, :, bass.ds(f * P, P)]).then_inc(w_in[b], 16)
                for g in range(2):
                    sp.dma_start(sig[:, b, g, :], zv[bass.ds((4 * MH + g * KD) + f, 1)]
                                 .rearrange("a p t -> (a p) t")).then_inc(sig_in[b], 16)

            for a in range(2 * KB):
                if a >= 2:
                    sp.wait_ge(b_split, a)
                sp.dma_start(b_raw[:, a % 2, :], branches[a // KB][a % KB]).then_inc(b_in[a % 2], 16)
            with sp.Fori(0, KD // 2) as i:
                for u in range(2):
                    f, b, n = ring(i, u)
                    sp.wait_ge(slot_free, f + 2)
                    weights(f, b)

        @block.scalar
        def _(act):
            for a in range(2 * KB):
                act.wait_ge(b_in[a % 2], 16 * (a // 2 + 1) + 1)
                act.activation(b_hi[:, a, :], b_raw[:, a % 2, :], ACT.Copy).then_inc(b_hi_done, 1)
            with act.Fori(0, KD // 2) as i:
                for u in range(2):
                    f, b, n = ring(i, u)
                    act.wait_ge(added, NCH * f + NCH + 1)
                    act.dma_start(k.mergedT.rearrange("(a p) t -> a p t", p=P)[bass.ds(f, 1)]
                                  .rearrange("a p t -> (a p) t"), m_st[:, b, :]).then_inc(out[b], 16)
            for b in range(2):
                act.wait_ge(out[b], 16 * (KD // 2) + 1)

        @block.vector
        def _(dve):
            for a in range(2 * KB):
                dve.wait_ge(b_hi_done, a + 2)
                dve.tensor_tensor(b_lo[:, a, :], b_raw[:, a % 2, :], b_hi[:, a, :].bitcast(F32),
                                  ALU.subtract).then_inc(b_split, 1)

            def split_w(f, b, n):
                dve.wait_ge(w_in[b], 32 * (n + 1) + 1)
                dve.wait_ge(slot_free, f + 2)
                dve.tensor_copy(w_hi[:, b], raw[:, b]).then_inc(hi_done, 1)
                dve.wait_ge(hi_done, f + 2)
                dve.tensor_tensor(w_lo[:, b], raw[:, b], w_hi[:, b].bitcast(F32), ALU.subtract).then_inc(split, 1)

            def mix(f, b, n):
                dve.wait_ge(sig_in[b], 32 * (n + 1) + 1)
                dve.wait_ge(out[b], 16 * n + 1)
                for c in range(NCH):
                    at = NCH * f + c
                    s = (NCH * b + c) % 2
                    cols = slice(c * CH, (c + 1) * CH)
                    dve.wait_ge(product, at + 2)
                    dve.wait_ge(added, at + 1)
                    dve.tensor_tensor(m_st[:, b, cols], pB[:, s, 0, :], sig[:, b, 0, cols], ALU.mult).then_inc(mixed, 1)
                    dve.tensor_tensor(gated[:, s, :], pB[:, s, 1, :], sig[:, b, 1, cols], ALU.mult).then_inc(mixed, 1)
                dve.wait_ge(mixed, 2 * NCH * f + 2 * NCH + 3)
                dve.sem_inc(slot_free, 1)

            dve.sem_inc(slot_free, 2)
            dve.sem_inc(mixed, 2)
            split_w(*ring(0, 0))
            with dve.Fori(0, KD // 2 - 1) as i:
                for u in range(2):
                    split_w(*ring(i, u + 1))
                    mix(*ring(i, u))
            split_w(*ring(0, KD - 1))
            mix(*ring(0, KD - 2))
            mix(*ring(0, KD - 1))

        @block.gpsimd
        def _(pool):
            with pool.Fori(0, KD // 2) as i:
                for u in range(2):
                    f, b, n = ring(i, u)
                    for c in range(NCH):
                        at = NCH * f + c
                        s = (NCH * b + c) % 2
                        cols = slice(c * CH, (c + 1) * CH)
                        pool.wait_ge(mixed, 2 * at + 5)
                        pool.tensor_tensor(m_st[:, b, cols], m_st[:, b, cols], gated[:, s, :],
                                           ALU.add).then_inc(added, 1)

        @block.tensor
        def _(pe):
            pe.wait_ge(b_split, 2 * KB + 1)
            with pe.Fori(0, KD // 2) as i:
                for u in range(2):
                    f, b, n = ring(i, u)
                    pe.wait_ge(split, f + 2)
                    for c in range(NCH):
                        at = NCH * f + c
                        s = (NCH * b + c) % 2
                        pe.wait_ge(mixed, 2 * at + 1)
                        for g in range(2):
                            for kt in range(KB):
                                a = g * KB + kt
                                last = mm3(pe, pB[:, s, g, :], w_hi[:, b, a, :], w_lo[:, b, a, :],
                                           b_hi[:, a, c * CH:(c + 1) * CH], b_lo[:, a, c * CH:(c + 1) * CH],
                                           kt == 0, kt == KB - 1)
                        last.then_inc(product, 1)


def out_projection(nc, k, h2_hi, h2_lo):
    with ExitStack() as ctx:
        def sb(name, shape, dt=F32):
            return ctx.enter_context(nc.sbuf_tensor(name, shape, dt))

        used = []

        def sem(name):
            used.append(ctx.enter_context(nc.semaphore(name)))
            return used[-1]

        wo_hi, wo_lo = sb("wo_hi", [P, KD, D], F32R), sb("wo_lo", [P, KD, D], F32R)
        raw = sb("o_raw", [P, 2, D])
        m_hi, m_lo = sb("mg_hi", [P, 2, KD, P], F32R), sb("mg_lo", [P, 2, KD, P], F32R)
        x_t = sb("xr_t", [P, 2, D])
        row = sb("o_row", [P, D])
        post, pre = sb("post_gain", [P, D]), sb("pre_gain", [P, D])
        stat = sb("o_stat", [P, 8])
        pY = ctx.enter_context(nc.psum_tensor("pY", [P, 2, D], F32))
        pT = ctx.enter_context(nc.psum_tensor("pHT", [P, KD, P], F32))
        gain_in, raw_in, x_in = sem("o_gain_in"), [sem(f"o_raw_in{b}") for b in range(2)], [sem(f"xr_in{b}") for b in range(2)]
        hi_done, split, product = sem("o_hi_done"), sem("o_split"), sem("o_product")
        a_stat, v_rs, normed, x1_done, h_scaled = sem("o_stat_s"), sem("o_rs"), sem("o_normed"), sem("x1_done"), sem("h2_scaled")
        turned, h_hi_done, h_lo_done = sem("h2_turned"), sem("h2_hi_done"), sem("h2_lo_done")
        x1_out = [sem(f"x1_out{b}") for b in range(2)]
        start_at_one(nc, used)
        block = ctx.enter_context(nc.Block())
        wv = k.w_out.rearrange("(t p) n -> t p n", p=P)
        mv = k.mergedT.rearrange("(a p) t -> p a t", p=P)

        @block.sync
        def _(sp):
            for g, dst in ((k.norm_mix_post, post), (k.norm_ffn_pre, pre)):
                sp.dma_start(dst[:, :], g.partition_broadcast(P)).then_inc(gain_in, 16)
            for t in range(KD):
                if t >= 2:
                    sp.wait_ge(split, t)
                sp.dma_start(raw[:, t % 2, :], wv[t]).then_inc(raw_in[t % 2], 16)
            with sp.Fori(0, NT // 2) as i:
                for u in range(2):
                    t, b, n = ring(i, u)
                    sp.wait_ge(split, KD + t)
                    sp.dma_start(raw[:, b, :].rearrange("p (a t) -> p a t", t=P), mv[:, :, bass.ds(t * P, P)])\
                      .then_inc(raw_in[b], 16)
                    wait_apart(sp, k, x1_out[b], 16 * n + 1)
                    sp.wait_ge(h_scaled, t + 1)
                    sp.dma_start(x_t[:, b, :], k.x[bass.ds(t * P, P), :]).then_inc(x_in[b], 16)

        @block.scalar
        def _(act):
            with act.Fori(0, NT // 2) as i:
                for u in range(2):
                    t, b, n = ring(i, u)
                    act.wait_ge(product, t + 2)
                    act.wait_ge(turned, t + 1)
                    act.activation(row[:, :], pY[:, b, :], ACT.Square, accum_out=stat[:, 0:1]).then_inc(a_stat, 1)
                    act.wait_ge(a_stat, 4 * t + 2)
                    act.activation(stat[:, 1:2], stat[:, 0:1], ACT.Sqrt, scale=1.0 / D, bias=k.eps[:, 0:1]).then_inc(a_stat, 1)
                    act.wait_ge(x1_done, t + 2)
                    act.dma_start(k.x1[bass.ds(t * P, P), :], x_t[:, b, :]).then_inc(x1_out[b], 16)
                    act.activation(row[:, :], x_t[:, b, :], ACT.Square, accum_out=stat[:, 3:4]).then_inc(a_stat, 1)
                    act.wait_ge(a_stat, 4 * t + 4)
                    act.activation(stat[:, 4:5], stat[:, 3:4], ACT.Sqrt, scale=1.0 / D, bias=k.eps[:, 0:1]).then_inc(a_stat, 1)
                    act.wait_ge(turned, t + 2)
                    act.activation(h2_hi[:, :, bass.ds(t * P, P)], pT[:, :, :], ACT.Copy).then_inc(h_hi_done, 1)
            for b in range(2):
                act.wait_ge(x1_out[b], 16 * (NT // 2) + 1)

        @block.vector
        def _(dve):
            for t in range(KD):
                b = t % 2
                dve.wait_ge(raw_in[b], 16 * (t // 2 + 1) + 1)
                dve.tensor_copy(wo_hi[:, t, :], raw[:, b, :]).then_inc(hi_done, 1)
                dve.wait_ge(hi_done, t + 2)
                dve.tensor_tensor(wo_lo[:, t, :], raw[:, b, :], wo_hi[:, t, :].bitcast(F32), ALU.subtract).then_inc(split, 1)
            dve.wait_ge(gain_in, 33)
            dve.sem_inc(h_scaled, 1)

            def split_m(t, b, n, first=False):
                dve.wait_ge(raw_in[b], 16 * (KD // 2 + n + 1) + 1)
                if not first:
                    dve.wait_ge(product, t)
                rows = raw[:, b, :].rearrange("p (a t) -> p a t", t=P)
                dve.tensor_copy(m_hi[:, b], rows).then_inc(hi_done, 1)
                dve.wait_ge(hi_done, KD + t + 2)
                dve.tensor_tensor(m_lo[:, b], rows, m_hi[:, b].bitcast(F32), ALU.subtract).then_inc(split, 1)

            def post_norm(t, b, n):
                dve.wait_ge(a_stat, 4 * t + 3)
                dve.reciprocal(stat[:, 2:3], stat[:, 1:2]).then_inc(v_rs, 1)
                dve.wait_ge(v_rs, 2 * t + 2)
                dve.scalar_tensor_tensor(out=row[:, :], in0=pY[:, b, :], scalar=stat[:, 2:3], in1=post[:, :],
                                         op0=ALU.mult, op1=ALU.mult).then_inc(normed, 1)
                dve.wait_ge(normed, t + 2)
                dve.wait_ge(x_in[b], 16 * (n + 1) + 1)
                dve.tensor_tensor(x_t[:, b, :], x_t[:, b, :], row[:, :], ALU.add).then_inc(x1_done, 1)
                dve.wait_ge(a_stat, 4 * t + 5)
                dve.reciprocal(stat[:, 5:6], stat[:, 4:5]).then_inc(v_rs, 1)
                dve.wait_ge(v_rs, 2 * t + 3)
                dve.scalar_tensor_tensor(out=row[:, :], in0=x_t[:, b, :], scalar=stat[:, 5:6], in1=pre[:, :],
                                         op0=ALU.mult, op1=ALU.mult).then_inc(h_scaled, 1)

            def keep_lo(t, b, n):
                dve.wait_ge(h_hi_done, t + 2)
                cols = bass.ds(t * P, P)
                dve.tensor_tensor(h2_lo[:, :, cols], pT[:, :, :], h2_hi[:, :, cols].bitcast(F32),
                                  ALU.subtract).then_inc(h_lo_done, 1)

            split_m(*ring(0, 0), first=True)
            split_m(*ring(0, 1), first=True)
            with dve.Fori(0, NT // 2 - 1) as i:
                for u in range(2):
                    post_norm(*ring(i, u))
                    split_m(*ring(i, u + 2))
                    keep_lo(*ring(i, u))
            for t in (NT - 2, NT - 1):
                post_norm(*ring(0, t))
                keep_lo(*ring(0, t))

        @block.tensor
        def _(pe):
            def products(t, b, n, first=False):
                pe.wait_ge(split, KD + t + 2)
                if not first:
                    pe.wait_ge(normed, t)
                for h in range(D // CH):
                    for kt in range(KD):
                        last = mm3(pe, pY[:, b, h * CH:(h + 1) * CH], m_hi[:, b, kt, :], m_lo[:, b, kt, :],
                                   wo_hi[:, kt, h * CH:(h + 1) * CH], wo_lo[:, kt, h * CH:(h + 1) * CH],
                                   kt == 0, kt == KD - 1)
                last.then_inc(product, 1)

            def turn(t, b, n):
                pe.wait_ge(h_scaled, t + 3)
                pe.wait_ge(h_lo_done, t + 1)
                for kt in range(KD):
                    last = pe.transpose(pT[:, kt, :], row[:, kt * P:(kt + 1) * P], k.ident[:, :])
                last.then_inc(turned, 1)

            products(*ring(0, 0), first=True)
            products(*ring(0, 1), first=True)
            with pe.Fori(0, NT // 2 - 1) as i:
                for u in range(2):
                    turn(*ring(i, u))
                    products(*ring(i, u + 2))
            turn(*ring(0, NT - 2))
            turn(*ring(0, NT - 1))


def ffn(nc, k, h2_hi, h2_lo, y_sum):
    with ExitStack() as ctx:
        def sb(name, shape, dt=F32):
            return ctx.enter_context(nc.sbuf_tensor(name, shape, dt))

        used = []

        def sem(name):
            used.append(ctx.enter_context(nc.semaphore(name)))
            return used[-1]

        act_hi, act_lo = sb("act_hi", [P, TOK], F32R), sb("act_lo", [P, TOK], F32R)
        raw = sb("ffn_raw", [P, 2, D])
        g_hi, g_lo = sb("wg_hi", [P, KD, P], F32R), sb("wg_lo", [P, KD, P], F32R)
        v_hi, v_lo = sb("wv_hi", [P, KD, P], F32R), sb("wv_lo", [P, KD, P], F32R)
        d_hi, d_lo = sb("wd_hi", [P, D], F32R), sb("wd_lo", [P, D], F32R)
        GP = TOK + 4
        gate = sb("gate_pad", [P, GP])
        conv = sb("conv", [P, CH])
        gelu = sb("gelu", [P, CH])
        taps = sb("taps", [P, CONV_W, NFF])
        conv_b = sb("conv_b", [P, NFF])
        pG = ctx.enter_context(nc.psum_tensor("pG", [P, NCH, CH], F32))
        pV = ctx.enter_context(nc.psum_tensor("pVal", [P, NCH, CH], F32))
        pD = ctx.enter_context(nc.psum_tensor("pD", [P, 2, CH], F32))
        taps_in, padded = sem("taps_in"), sem("padded")
        raw_in = [sem(f"ffn_in{b}") for b in range(2)]
        whi, wsplit = sem("ffn_whi"), sem("ffn_wsplit")
        gated, gate_copied, vald, downed = sem("gate_done"), sem("gate_copied"), sem("val_done"), sem("down_done")
        conv_s, gelu_done, act_f32, act_h, act_l, summed = (sem("conv_steps"), sem("gelu_done"), sem("act_f32"),
                                                            sem("act_h"), sem("act_l"), sem("y_summed"))
        start_at_one(nc, used)
        block = ctx.enter_context(nc.Block())
        up = k.w_up.rearrange("(t p) n -> p t n", p=P)
        down = k.w_down.rearrange("(f p) n -> f p n", p=P)
        PAD_AT = [1, 3 + CH, 3 + 2 * CH]
        NEEDS = [1, 3, 3]
        NDT = NT * (D // CH)
        last_f = NFF - 1

        @block.sync
        def _(sp):
            sp.dma_start(taps[:, :, :], k.conv_w).then_inc(taps_in, 16)
            sp.dma_start(conv_b[:, :], k.conv_b).then_inc(taps_in, 16)

            def load(at, b, src, first=False):
                if not first:
                    sp.wait_ge(wsplit, at)
                sp.dma_start(raw[:, b, :] if src is None else src[0](raw[:, b, :]), src[1]).then_inc(raw_in[b], 16)

            def square(a):
                return a.rearrange("p (t n) -> p t n", n=P)

            def three(f, odd, first=False):
                at = 3 * f
                load(at, odd, (square, up[:, :, bass.ds(f * P, P)]), first)
                load(at + 1, 1 - odd, (square, up[:, :, bass.ds(FF + f * P, P)]), first)
                load(at + 2, odd, (lambda a: a, down[bass.ds(f, 1)].rearrange("a p n -> (a p) n")))

            three(0, 0, first=True)
            three(1, 1)
            with sp.Fori(1, NFF // 2) as i:
                three(2 * i, 0)
                three(2 * i + 1, 1)

        @block.vector
        def _(dve):
            for a in (0, 1 + CH, 2 + CH, GP - 1):
                dve.memset(gate[:, a:a + 1], 0.0).then_inc(padded, 1)
            dve.wait_ge(taps_in, 33)
            dve.wait_ge(padded, 5)

            def split(at, b, n, hi, lo, used, count):
                dve.wait_ge(raw_in[b], 16 * (n + 1) + 1)
                dve.wait_ge(used, count + 1)
                flat = raw[:, b, :]
                dve.tensor_copy(hi, flat).then_inc(whi, 1)
                dve.wait_ge(whi, at + 2)
                dve.tensor_tensor(lo, flat, hi.bitcast(F32), ALU.subtract).then_inc(wsplit, 1)

            def flat(a):
                return a[:, :, :].rearrange("p t n -> p (t n)")

            def place(i, odd, j):
                c = 3 * odd + j
                return 6 * i + c, c % 2, 3 * i + c // 2

            def split_gate(i, odd):
                split(*place(i, odd, 0), flat(g_hi), flat(g_lo), gated, NCH * (2 * i + odd))

            def split_val(i, odd):
                split(*place(i, odd, 1), flat(v_hi), flat(v_lo), vald, NCH * (2 * i + odd))

            def split_down(i, odd):
                split(*place(i, odd, 2), d_hi[:, :], d_lo[:, :], downed, NDT * (2 * i + odd))

            def activate(f):
                for c in range(NCH):
                    at = NCH * f + c
                    dve.wait_ge(gate_copied, NCH * f + NEEDS[c] + 1)
                    dve.wait_ge(gelu_done, at + 1)
                    a = PAD_AT[c]

                    def tap(w):
                        return taps[:, w, bass.ds(f, 1)] if not isinstance(f, int) else taps[:, w, f:f + 1]

                    dve.tensor_scalar(conv[:, :], gate[:, a - 1:a - 1 + CH], tap(0), None, ALU.mult).then_inc(conv_s, 1)
                    for w in (1, 2):
                        dve.wait_ge(conv_s, 3 * at + w + 1)
                        dve.scalar_tensor_tensor(out=conv[:, :], in0=gate[:, a - 1 + w:a - 1 + w + CH], scalar=tap(w),
                                                 in1=conv[:, :], op0=ALU.mult, op1=ALU.add).then_inc(conv_s, 1)
                    dve.wait_ge(gelu_done, at + 2)
                    dve.wait_ge(vald, at + 2)
                    dve.tensor_tensor(gelu[:, :], gelu[:, :], pV[:, c, :], ALU.mult).then_inc(act_f32, 1)
                    dve.wait_ge(act_h, at + 2)
                    cols = slice(c * CH, (c + 1) * CH)
                    dve.tensor_tensor(act_lo[:, cols], gelu[:, :], act_hi[:, cols].bitcast(F32),
                                      ALU.subtract).then_inc(act_l, 1)

            def add_down(f, first=False):
                for t in range(NT):
                    for h in range(D // CH):
                        at = NDT * f + 2 * t + h
                        dve.wait_ge(downed, at + 2)
                        cols = slice(h * CH, (h + 1) * CH)
                        if first:
                            dve.tensor_copy(y_sum[:, t, cols], pD[:, h, :]).then_inc(summed, 1)
                        else:
                            dve.wait_ge(summed, NDT * f + 1)
                            dve.tensor_tensor(y_sum[:, t, cols], y_sum[:, t, cols], pD[:, h, :],
                                              ALU.add).then_inc(summed, 1)

            def step(i, odd, last=False):
                split_val(i, odd)
                add_down(2 * i + odd - 1)
                split_down(i, odd)
                if not last:
                    split_gate(i, odd + 1)
                activate(2 * i + odd)

            split_gate(0, 0)
            split_val(0, 0)
            split_down(0, 0)
            split_gate(0, 1)
            activate(0)
            split_val(0, 1)
            add_down(0, first=True)
            split_down(0, 1)
            split_gate(0, 2)
            activate(1)
            with dve.Fori(1, NFF // 2 - 1) as i:
                step(i, 0)
                step(i, 1)
            step(NFF // 2 - 1, 0)
            step(NFF // 2 - 1, 1, last=True)
            add_down(last_f)

        @block.scalar
        def _(act):
            act.wait_ge(padded, 5)
            act.wait_ge(taps_in, 33)

            def copy_gate(f):
                for c in range(NCH):
                    act.wait_ge(gated, NCH * f + c + 2)
                    act.wait_ge(conv_s, 3 * NCH * f + 1)
                    act.activation(gate[:, PAD_AT[c]:PAD_AT[c] + CH], pG[:, c, :], ACT.Copy).then_inc(gate_copied, 1)

            def gelus(f):
                for c in range(NCH):
                    at = NCH * f + c
                    wait_apart(act, k, conv_s, 3 * at + 3 + 1)
                    wait_apart(act, k, act_l, at + 1)
                    b = conv_b[:, bass.ds(f, 1)] if not isinstance(f, int) else conv_b[:, f:f + 1]
                    act.activation(gelu[:, :], conv[:, :], ACT.Gelu_apprx_tanh, bias=b).then_inc(gelu_done, 1)
                    act.wait_ge(act_f32, at + 2)
                    act.wait_ge(downed, NDT * f + 1)
                    act.activation(act_hi[:, c * CH:(c + 1) * CH], gelu[:, :], ACT.Copy).then_inc(act_h, 1)

            with act.Fori(0, NFF) as f:
                copy_gate(f)
                gelus(f)

        @block.tensor
        def _(pe):
            def ups(f, at_split, w_hi, w_lo, bank, done, free, count, inc):
                pe.wait_ge(wsplit, at_split + 2)
                for c in range(NCH):
                    pe.wait_ge(free, count + 1)
                    for kt in range(KD):
                        last = mm3(pe, bank[:, c, :], w_hi[:, kt, :], w_lo[:, kt, :],
                                   h2_hi[:, kt, c * CH:(c + 1) * CH], h2_lo[:, kt, c * CH:(c + 1) * CH],
                                   kt == 0, kt == KD - 1)
                    last.then_inc(done, 1)

            def gate_products(f):
                ups(f, 3 * f, g_hi, g_lo, pG, gated, gate_copied, NCH * f, 1)

            def val_products(f):
                ups(f, 3 * f + 1, v_hi, v_lo, pV, vald, act_f32, NCH * f, 1)

            def down_products(f, first=False):
                pe.wait_ge(wsplit, 3 * f + 4)
                pe.wait_ge(act_l, NCH * f + NCH + 1)
                for t in range(NT):
                    for h in range(D // CH):
                        if not (first and t == 0):
                            pe.wait_ge(summed, NDT * f + 2 * t + h)
                        cols = slice(h * CH, (h + 1) * CH)
                        mm3(pe, pD[:, h, :], act_hi[:, t * P:(t + 1) * P], act_lo[:, t * P:(t + 1) * P],
                            d_hi[:, cols], d_lo[:, cols], True, True).then_inc(downed, 1)

            gate_products(0)
            val_products(0)
            gate_products(1)
            down_products(0, first=True)
            val_products(1)
            with pe.Fori(2, NFF) as f:
                gate_products(f)
                down_products(f - 1)
                val_products(f)
            down_products(last_f)


def final_norm(nc, k, y_sum):
    with ExitStack() as ctx:
        def sb(name, shape, dt=F32):
            return ctx.enter_context(nc.sbuf_tensor(name, shape, dt))

        used = []

        def sem(name):
            used.append(ctx.enter_context(nc.semaphore(name)))
            return used[-1]

        gain, x_t, y_t = sb("f_gain", [P, D]), sb("f_x1", [P, 2, D]), sb("f_y", [P, 2, D])
        squares, stat = sb("f_sq", [P, D]), sb("f_stat", [P, 8])
        gain_in, x_in = sem("f_gain_in"), [sem(f"f_x1_in{b}") for b in range(2)]
        squared, rooted, inverted, scaled, added = sem("f_squared"), sem("f_rooted"), sem("f_inverted"), sem("f_scaled"), sem("f_added")
        out = [sem(f"y_out{b}") for b in range(2)]
        start_at_one(nc, used)
        block = ctx.enter_context(nc.Block())

        def row(t):
            return y_sum[:, bass.ds(t, 1), :].rearrange("p a n -> p (a n)")

        @block.sync
        def _(sp):
            sp.dma_start(gain[:, :], k.norm_ffn_post.partition_broadcast(P)).then_inc(gain_in, 16)
            with sp.Fori(0, NT // 2) as i:
                for u in range(2):
                    t, b, n = ring(i, u)
                    sp.wait_ge(added, t + 1)
                    sp.dma_start(x_t[:, b, :], k.x1[bass.ds(t * P, P), :]).then_inc(x_in[b], 16)

        @block.scalar
        def _(act):
            with act.Fori(0, NT // 2) as i:
                for u in range(2):
                    t, b, n = ring(i, u)
                    act.wait_ge(inverted, t + 1)
                    act.wait_ge(squared, t + 1)
                    act.activation(squares[:, :], row(t), ACT.Square, accum_out=stat[:, b:b + 1]).then_inc(squared, 1)
                    act.wait_ge(squared, t + 2)
                    act.activation(stat[:, 2 + b:3 + b], stat[:, b:b + 1], ACT.Sqrt, scale=1.0 / D,
                                   bias=k.eps[:, 0:1]).then_inc(rooted, 1)
                    act.wait_ge(added, t + 3)
                    act.dma_start(k.y[bass.ds(t * P, P), :], y_t[:, b, :]).then_inc(out[b], 16)
            for b in range(2):
                act.wait_ge(out[b], 16 * (NT // 2) + 1)

        @block.vector
        def _(dve):
            dve.wait_ge(gain_in, 17)
            with dve.Fori(0, NT // 2) as i:
                for u in range(2):
                    t, b, n = ring(i, u)
                    dve.wait_ge(rooted, t + 2)
                    dve.reciprocal(stat[:, 4 + b:5 + b], stat[:, 2 + b:3 + b]).then_inc(inverted, 1)
                    dve.wait_ge(inverted, t + 2)
                    dve.wait_ge(out[b], 16 * n + 1)
                    dve.scalar_tensor_tensor(out=y_t[:, b, :], in0=row(t), scalar=stat[:, 4 + b:5 + b], in1=gain[:, :],
                                             op0=ALU.mult, op1=ALU.mult).then_inc(scaled, 1)

        @block.gpsimd
        def _(pool):
            pool.sem_inc(added, 1)
            with pool.Fori(0, NT // 2) as i:
                for u in range(2):
                    t, b, n = ring(i, u)
                    pool.wait_ge(scaled, t + 2)
                    pool.wait_ge(x_in[b], 16 * (n + 1) + 1)
                    pool.tensor_tensor(y_t[:, b, :], y_t[:, b, :], x_t[:, b, :], ALU.add).then_inc(added, 1)


class Names:
    pass


def start_at_one(nc, semaphores):
    with nc.Block() as block:
        @block.gpsimd
        def _(pool):
            for s in semaphores:
                pool.sem_inc(s, 1)


def clear(nc, semaphores):
    with nc.Block() as block:
        @block.gpsimd
        def _(pool):
            for s in semaphores:
                pool.sem_clear(s)


def constants(nc, k):
    made = k.made
    with nc.Block() as block:
        @block.gpsimd
        def _(pool):
            pool.memset(k.eps[:, :], EPS).then_inc(made, 1)
            pool.memset(k.one[:, :], 1.0).then_inc(made, 1)
            pool.memset(k.ident[:, :], 0.0).then_inc(made, 1)
            pool.memset(k.mask[:, :, :], 0.0).then_inc(made, 1)
            pool.wait_ge(made, 4)
            pool.affine_select(out=k.ident[:, :], in_=k.ident[:, :], compare_op=ALU.not_equal, fill=1.0, base=0,
                               pattern=[[-1, P]], channel_multiplier=1).then_inc(made, 1)
            pool.affine_select(out=k.mask[:, 0, :], in_=k.mask[:, 0, :], compare_op=ALU.is_ge, fill=NEG, base=0,
                               pattern=[[1, P]], channel_multiplier=-1).then_inc(made, 1)
            pool.affine_select(out=k.mask[:, 1, :], in_=k.mask[:, 1, :], compare_op=ALU.is_ge, fill=NEG, base=0,
                               pattern=[[-1, P]], channel_multiplier=1).then_inc(made, 1)
            pool.wait_ge(made, 7)


def encoder_block(nc, x, norm_mix_pre, w_in, b_if, q_norm, k_norm, mlstm_norm_w, w_attn_o, w_mlstm_o, w_out,
                  norm_mix_post, norm_ffn_pre, w_up, conv_w, conv_b, w_down, norm_ffn_post, cos, sin, y):
    k = Names()
    k.x, k.norm_mix_pre, k.w_in, k.b_if, k.q_norm, k.k_norm = x, norm_mix_pre, w_in, b_if, q_norm, k_norm
    k.mlstm_norm, k.w_attn_o, k.w_mlstm_o, k.w_out = mlstm_norm_w, w_attn_o, w_mlstm_o, w_out
    k.norm_mix_post, k.norm_ffn_pre, k.w_up, k.conv_w, k.conv_b = norm_mix_post, norm_ffn_pre, w_up, conv_w, conv_b
    k.w_down, k.norm_ffn_post, k.cos, k.sin, k.y = w_down, norm_ffn_post, cos, sin, y

    def scratch(name, shape):
        return nc.dram_tensor(name, shape, F32).ap()

    k.v = scratch("v_scratch", (TOK, NKV * HEAD))
    k.qkT = scratch("qkT_scratch", (QK, TOK))
    k.zT = scratch("zT_scratch", (4 * MW + 2 * D, TOK))
    k.negA = scratch("negA_scratch", (2 * MH, TOK))
    k.aT, k.mT = scratch("aT_scratch", (MW, TOK)), scratch("mT_scratch", (MW, TOK))
    k.mergedT, k.x1 = scratch("mergedT_scratch", (D, TOK)), scratch("x1_scratch", (TOK, D))

    with ExitStack() as ctx:
        def sb(stack, name, shape, dt=F32):
            return stack.enter_context(nc.sbuf_tensor(name, shape, dt))

        k.ident, k.mask = sb(ctx, "ident", [P, P]), sb(ctx, "mask", [P, 2, P])
        k.eps, k.one = sb(ctx, "eps", [P, 1]), sb(ctx, "one", [P, 1])
        k.made = ctx.enter_context(nc.semaphore("constants_made"))
        k.waits_apart = ctx.enter_context(nc.semaphore("waits_apart"))
        constants(nc, k)
        with ExitStack() as mix:
            k.a_col = sb(mix, "a_col", [P, 2, NT, MH])
            k.floor = sb(mix, "floor", [P, 2, NT, MH])
            with ExitStack() as proj:
                k.gates = sb(proj, "gates", [P, TOK])
                with ExitStack() as first:
                    hT_hi, hT_lo = (sb(first, f"hT_{s}", [P, KD, TOK], F32R) for s in ("hi", "lo"))
                    clear(nc, norm_and_qkv(nc, k, hT_hi, hT_lo))
                    input_projection(nc, k, hT_hi, hT_lo)
                gate_scans(nc, k)
            attention(nc, k)
            k.h_sum = sb(mix, "h_sum", [P, NT, MH, MD])
            mlstm(nc, k)
            mlstm_norm(nc, k)
        merge(nc, k)
        with ExitStack() as second:
            h2_hi, h2_lo = (sb(second, f"h2T_{s}", [P, KD, TOK], F32R) for s in ("hi", "lo"))
            out_projection(nc, k, h2_hi, h2_lo)
            y_sum = sb(second, "y_sum", [P, NT, D])
            ffn(nc, k, h2_hi, h2_lo, y_sum)
            final_norm(nc, k, y_sum)


def rotary_tables():
    import numpy as np

    pairs = HEAD // 4
    freq = np.float32(10000.0) ** (-np.arange(pairs, dtype=np.float32) / np.float32(pairs))
    pos = np.concatenate([np.arange(n * P) for n in SEG_TILES])
    angle = np.concatenate([(pos // GRID_W).astype(np.float32)[:, None] * freq,
                            (pos % GRID_W).astype(np.float32)[:, None] * freq], axis=1)
    table = angle.reshape(NT, P, HEAD // 2).transpose(1, 0, 2)
    return np.ascontiguousarray(np.cos(table)), np.ascontiguousarray(np.sin(table))


_WEIGHTS = ["norm_mix_pre", "w_in", "b_if", "q_norm", "k_norm", "mlstm_norm", "w_attn_o", "w_mlstm_o", "w_out",
            "norm_mix_post", "norm_ffn_pre", "w_up", "conv_w", "conv_b", "w_down", "norm_ffn_post"]


def kernel(**inputs):
    import numpy as np
    import concourse.bacc as bacc
    from concourse.bass_utils import run_bass_kernel_spmd

    x = np.concatenate([np.asarray(inputs[n])[0] for n in ("x_prompt", "x_sample")], axis=0)
    arrays = {"in_x": np.ascontiguousarray(x)}
    for name in _WEIGHTS:
        arrays[f"in_{name}"] = np.ascontiguousarray(np.asarray(inputs[name])[0])
    for name in ("in_conv_w", "in_conv_b"):
        a = arrays[name].reshape(-1, NFF, P)
        arrays[name] = np.ascontiguousarray(a.transpose(2, 0, 1) if name == "in_conv_w" else a[0].T)
    arrays["in_cos"], arrays["in_sin"] = rotary_tables()
    nc = bacc.Bacc("TRN2", target_bir_lowering=False, num_devices=1)
    args = [nc.dram_tensor(n, a.shape, mybir.dt.from_np(a.dtype), kind="ExternalInput").ap()
            for n, a in arrays.items()]
    args.append(nc.dram_tensor("out_y", (TOK, D), F32, kind="ExternalOutput").ap())
    encoder_block(nc, *args)
    y = run_bass_kernel_spmd(nc, [arrays], core_ids=[0]).results[0]["out_y"]
    n = SEG_TILES[0] * P
    return y[None, :n], y[None, n:]
```

```python
from contextlib import ExitStack

import concourse.bass as bass
from concourse import mybir

F32 = mybir.dt.float32
F32R = mybir.dt.float32r
ACT = mybir.ActivationFunctionType
ALU = mybir.AluOpType
AX_X = mybir.AxisListType.X

P = 128
D = 1024
KD = D // P
SEG_TILES = (4, 8)
NT = sum(SEG_TILES)
TOK = NT * P
CH = 512
NCH = TOK // CH
GRID_W = 64
HEAD = 64
NQ, NKV = 8, 2
QK = (NQ + NKV) * HEAD
QKV = QK + NKV * HEAD
NHEADS_QK = NQ + NKV
MH, MD = 4, 128
MW = MH * MD
FF = 2816
NFF = FF // P
CONV_W = 3
EPS = 1e-6
COL_M = QKV
COL_O = COL_M + 3 * MW
COL_GATE = COL_O + MW
N_GATE = 4 * MH
COL_GA = COL_GATE + N_GATE
Q_SCALE = -HEAD ** -0.5
NEG = -1.0e30

SEG_OF_CHUNK = [(0, 4), (4, 12), (4, 12)]


def ring(i, c):
    return 2 * i + c, c % 2, i + c // 2


def wait_apart(eng, k, semaphore, value):
    eng.wait_ge(semaphore, value)
    eng.sem_inc(k.waits_apart, 1)


def mm3(pe, out, w_hi, w_lo, x_hi, x_lo, first, last, **kw):
    pe.matmul(out, w_hi, x_hi, start=first, stop=False, **kw)
    pe.matmul(out, w_lo, x_hi, start=False, stop=False, **kw)
    return pe.matmul(out, w_hi, x_lo, start=False, stop=last, **kw)


def norm_and_qkv(nc, k, hT_hi, hT_lo):
    with ExitStack() as ctx:
        def sb(name, shape, dt=F32):
            return ctx.enter_context(nc.sbuf_tensor(name, shape, dt))

        used = []

        def sem(name):
            used.append(ctx.enter_context(nc.semaphore(name)))
            return used[-1]

        wq_hi = sb("wqkv_hi", [P, KD, QKV], F32R)
        wq_lo = sb("wqkv_lo", [P, KD, QKV], F32R)
        gain = sb("mix_gain", [P, D])
        qk_gain = sb("qk_gain", [P, NHEADS_QK, HEAD])
        cos = sb("cos", [P, NT, HEAD // 2])
        sin = sb("sin", [P, NT, HEAD // 2])
        x_t = sb("x_t", [P, 2, D])
        xs = sb("x_scaled", [P, 2, D])
        h_hi = [sb(f"h_hi{b}", [P, KD, P], F32R) for b in range(2)]
        h_lo = [sb(f"h_lo{b}", [P, KD, P], F32R) for b in range(2)]
        qk_sq = sb("qk_sq", [P, NHEADS_QK, HEAD])
        v_st = sb("v_st", [P, NKV * HEAD])
        qk_n = sb("qk_n", [P, NHEADS_QK, HEAD])
        rot_a = sb("rot_a", [P, NHEADS_QK, HEAD // 2])
        rot_b = sb("rot_b", [P, NHEADS_QK, HEAD // 2])
        qk_r = sb("qk_r", [P, NHEADS_QK, HEAD])
        qkT_st = sb("qkT_st", [P, QK // P, P])
        stat = sb("stat", [P, 8])
        qstat = sb("qstat", [P, 4, NHEADS_QK])
        pT = ctx.enter_context(nc.psum_tensor("pT", [P, KD, P], F32))
        pQ = ctx.enter_context(nc.psum_tensor("pQ", [P, 2, D], F32))
        pR = ctx.enter_context(nc.psum_tensor("pR", [P, KD, P], F32))

        gain_in, const_in = sem("mix_gain_in"), sem("const_in")
        w_in = [sem(f"qkv_w_in{b}") for b in range(2)]
        w_hi_done, w_split = sem("qkv_w_hi_done"), sem("qkv_w_split")
        x_in = [sem(f"x_in{b}") for b in range(2)]
        squared, rooted, rs_ready = sem("squared"), sem("rooted"), sem("rs_ready")
        x_scaled, x_turned = sem("x_scaled_s"), sem("x_turned")
        h_hi_done, h_lo_done, h_kept = sem("h_hi_done"), sem("h_lo_done"), sem("h_kept")
        qkv_done, qk_squared, qk_summed = sem("qkv_done"), sem("qk_squared"), sem("qk_summed")
        qk_rooted, qk_rs, qk_normed, v_copied = sem("qk_rooted"), sem("qk_rs"), sem("qk_normed"), sem("v_copied")
        qk_gained, half_b, half_a, qk_rot = sem("qk_gained"), sem("half_b"), sem("half_a"), sem("qk_rot")
        qk_turned, qkT_copied, v_out, qkT_out = sem("qk_turned"), sem("qkT_copied"), sem("v_out"), sem("qkT_out")
        rot_free, gain_scaled = sem("rot_free"), sem("q_gain_scaled")
        raw = k.gates[:, :].rearrange("p (b n) -> p b n", n=QKV)
        start_at_one(nc, used)
        block = ctx.enter_context(nc.Block())
        wv = k.w_in.rearrange("(t p) n -> t p n", p=P)

        def steps(eng, step):
            step(lambda d: ring(0, d), 0)
            with eng.Fori(0, (NT - 4) // 2) as i:
                for u in range(2):
                    step(lambda d: ring(i, 1 + u + d), None)
            for t in range(NT - 3, NT):
                step(lambda d: ring(0, t + d), t)

        def there(t, d):
            return t is None or 0 <= t + d < NT

        @block.sync
        def _(sp):
            for t in range(2):
                sp.dma_start(x_t[:, t, :], k.x[t * P:(t + 1) * P, :]).then_inc(x_in[t], 16)
                sp.dma_start(raw[:, t, :], wv[t, :, 0:QKV]).then_inc(w_in[t], 16)
            for t in range(2, KD):
                sp.wait_ge(w_split, t)
                sp.dma_start(raw[:, t % 2, :], wv[t, :, 0:QKV]).then_inc(w_in[t % 2], 16)
            with sp.Fori(0, (NT - 2) // 2) as i:
                for u in range(2):
                    t, b, _ = ring(i, 2 + u)
                    sp.wait_ge(x_scaled, t)
                    sp.wait_ge(squared, t)
                    sp.dma_start(x_t[:, b, :], k.x[bass.ds(t * P, P), :]).then_inc(x_in[b], 16)

        @block.scalar
        def _(act):
            def statistics(t, b, n, first=False):
                act.wait_ge(x_in[b], 16 * (n + 1) + 1)
                if not first:
                    act.wait_ge(x_turned, t)
                act.activation(xs[:, b, :], x_t[:, b, :], ACT.Square,
                               accum_out=stat[:, b:b + 1]).then_inc(squared, 1)
                act.wait_ge(squared, t + 2)
                act.activation(stat[:, 2 + b:3 + b], stat[:, b:b + 1], ACT.Sqrt, scale=1.0 / D,
                               bias=k.eps[:, 0:1]).then_inc(rooted, 1)

            def keep_hi(t, b, n, first=False):
                act.wait_ge(x_turned, t + 2)
                if not first:
                    act.wait_ge(qkv_done, t)
                    act.wait_ge(h_kept, 2 * t - 1)
                act.activation(h_hi[b][:, :, :], pT[:, :, :], ACT.Copy).then_inc(h_hi_done, 1)

            def qk_stats(t, b, n):
                act.wait_ge(qkv_done, t + 2)
                act.wait_ge(qk_summed, t + 1)
                act.activation(qk_sq[:, :, :].rearrange("p h d -> p (h d)"), pQ[:, b, 0:QK],
                               ACT.Square).then_inc(qk_squared, 1)
                act.wait_ge(v_out, 16 * t + 1)
                act.activation(v_st[:, :], pQ[:, b, QK:QKV], ACT.Copy).then_inc(v_copied, 1)
                act.wait_ge(qk_summed, t + 2)
                act.activation(qstat[:, 1, :], qstat[:, 0, :], ACT.Sqrt, scale=1.0 / HEAD,
                               bias=k.eps[:, 0:1]).then_inc(qk_rooted, 1)
                act.wait_ge(v_copied, t + 2)
                act.dma_start(k.v[bass.ds(t * P, P), :], v_st[:, :]).then_inc(v_out, 16)

            def keep_qkT(t, b, n):
                act.wait_ge(qk_turned, t + 2)
                act.wait_ge(qkT_out, 16 * t + 1)
                act.activation(qkT_st[:, :, :], pR[:, 0:QK // P, :], ACT.Copy).then_inc(qkT_copied, 1)
                act.wait_ge(qkT_copied, t + 2)
                act.dma_start(k.qkT.rearrange("(a p) t -> p a t", p=P)[:, :, bass.ds(t * P, P)],
                              qkT_st[:, :, :]).then_inc(qkT_out, 16)

            act.dma_start(gain[:, :], k.norm_mix_pre.partition_broadcast(P)).then_inc(gain_in, 16)
            for h in range(NHEADS_QK):
                g = k.q_norm if h < NQ else k.k_norm
                act.dma_start(qk_gain[:, h, :], g.partition_broadcast(P)).then_inc(const_in, 16)
            act.dma_start(cos[:, :, :], k.cos).then_inc(const_in, 16)
            act.dma_start(sin[:, :, :], k.sin).then_inc(const_in, 16)
            statistics(*ring(0, 0), first=True)
            statistics(*ring(0, 1), first=True)
            keep_hi(*ring(0, 0), first=True)
            keep_hi(*ring(0, 1), first=True)
            statistics(*ring(0, 2))

            def step(tile, t):
                if there(t, 2):
                    keep_hi(*tile(2))
                qk_stats(*tile(0))
                if there(t, 3):
                    statistics(*tile(3))
                if there(t, -1):
                    keep_qkT(*tile(-1))

            steps(act, step)
            keep_qkT(*ring(0, NT - 1))
            act.wait_ge(v_out, 16 * NT + 1)
            act.wait_ge(qkT_out, 16 * NT + 1)

        @block.vector
        def _(dve):
            def split_w(t):
                b = t % 2
                dve.wait_ge(w_in[b], 16 * (t // 2 + 1) + 1)
                dve.tensor_copy(wq_hi[:, t, :], raw[:, b, :]).then_inc(w_hi_done, 1)
                dve.wait_ge(w_hi_done, t + 2)
                dve.tensor_tensor(wq_lo[:, t, :], raw[:, b, :], wq_hi[:, t, :].bitcast(F32),
                                  ALU.subtract).then_inc(w_split, 1)

            def scale(t, b, n, first=False):
                dve.wait_ge(rooted, t + 2)
                dve.reciprocal(stat[:, 4 + b:5 + b], stat[:, 2 + b:3 + b]).then_inc(rs_ready, 1)
                dve.wait_ge(rs_ready, t + 2)
                if not first:
                    dve.wait_ge(x_turned, t)
                dve.scalar_tensor_tensor(out=xs[:, b, :], in0=x_t[:, b, :], scalar=stat[:, 4 + b:5 + b],
                                         in1=gain[:, :], op0=ALU.mult, op1=ALU.mult).then_inc(x_scaled, 1)

            def keep_lo(t, b, n):
                dve.wait_ge(h_hi_done, t + 2)
                dve.tensor_tensor(h_lo[b][:, :, :], pT[:, :, :], h_hi[b][:, :, :].bitcast(F32),
                                  ALU.subtract).then_inc(h_lo_done, 1)

            def keep_h(t, b, n):
                dve.wait_ge(h_lo_done, t + 2)
                dve.tensor_copy(hT_hi[:, :, bass.ds(t * P, P)], h_hi[b][:, :, :]).then_inc(h_kept, 1)
                dve.tensor_copy(hT_lo[:, :, bass.ds(t * P, P)], h_lo[b][:, :, :]).then_inc(h_kept, 1)

            def qk_norm(t, b, n):
                dve.wait_ge(qk_squared, t + 2)
                dve.tensor_reduce(qstat[:, 0, :], qk_sq[:, :, :], AX_X, ALU.add).then_inc(qk_summed, 1)
                dve.wait_ge(qk_rooted, t + 2)
                dve.reciprocal(qstat[:, 2, :], qstat[:, 1, :]).then_inc(qk_rs, 1)
                dve.wait_ge(qk_rs, t + 2)
                dve.wait_ge(rot_free, t + 1)
                dve.tensor_tensor(qk_n[:, :, :], pQ[:, b, 0:QK].rearrange("p (h d) -> p h d", d=HEAD),
                                  qstat[:, 2, :].unsqueeze(2).to_broadcast([P, NHEADS_QK, HEAD]),
                                  ALU.mult).then_inc(qk_normed, 1)
                dve.wait_ge(qk_normed, t + 2)
                dve.tensor_tensor(qk_n[:, :, :], qk_n[:, :, :], qk_gain[:, :, :], ALU.mult).then_inc(qk_gained, 1)

            split_w(0)
            dve.wait_ge(gain_in, 17)
            scale(*ring(0, 0), first=True)
            split_w(1)
            scale(*ring(0, 1), first=True)
            split_w(2)
            keep_lo(*ring(0, 0))
            split_w(3)
            keep_lo(*ring(0, 1))
            for t in range(4, KD):
                split_w(t)
            scale(*ring(0, 2))
            keep_h(*ring(0, 0))
            keep_h(*ring(0, 1))
            dve.wait_ge(const_in, 16 * (NHEADS_QK + 2) + 1)
            dve.tensor_scalar(qk_gain[:, 0:NQ, :], qk_gain[:, 0:NQ, :], Q_SCALE, None, ALU.mult).then_inc(gain_scaled, 1)
            dve.wait_ge(gain_scaled, 2)

            def step(tile, t):
                qk_norm(*tile(0))
                if there(t, 2):
                    keep_lo(*tile(2))
                    keep_h(*tile(2))
                if there(t, 3):
                    scale(*tile(3))

            steps(dve, step)
            dve.wait_ge(h_kept, 2 * NT + 1)

        @block.gpsimd
        def _(pool):
            pool.wait_ge(const_in, 16 * (NHEADS_QK + 2) + 1)

            def rotate(t, b, n):
                pairs = qk_n[:, :, :].rearrange("p h (j e) -> p h j e", e=2)
                turned = qk_r[:, :, :].rearrange("p h (j e) -> p h j e", e=2)
                x0, x1 = pairs[:, :, :, 0], pairs[:, :, :, 1]

                def table(a):
                    return a[:, bass.ds(t, 1), :].to_broadcast([P, NHEADS_QK, HEAD // 2])

                pool.wait_ge(qk_gained, t + 2)
                wait_apart(pool, k, qk_rot, 2 * t + 1)
                pool.tensor_tensor(rot_a[:, :, :], x0, table(cos), ALU.mult).then_inc(half_a, 1)
                pool.tensor_tensor(rot_b[:, :, :], x1, table(sin), ALU.mult).then_inc(half_a, 1)
                pool.wait_ge(half_a, 4 * t + 3)
                pool.wait_ge(qk_turned, t + 1)
                pool.tensor_tensor(turned[:, :, :, 0], rot_a[:, :, :], rot_b[:, :, :],
                                   ALU.subtract).then_inc(qk_rot, 1)
                wait_apart(pool, k, qk_rot, 2 * t + 2)
                pool.tensor_tensor(rot_a[:, :, :], x0, table(sin), ALU.mult).then_inc(half_a, 1)
                pool.tensor_tensor(rot_b[:, :, :], x1, table(cos), ALU.mult).then_inc(rot_free, 1)
                pool.wait_ge(rot_free, t + 2)
                pool.tensor_tensor(turned[:, :, :, 1], rot_a[:, :, :], rot_b[:, :, :],
                                   ALU.add).then_inc(qk_rot, 1)
                pool.sem_inc(half_a, 1)

            with pool.Fori(0, NT // 2) as i:
                for u in range(2):
                    rotate(*ring(i, u))

        @block.tensor
        def _(pe):
            def turn_x(t, b, n, first=False):
                pe.wait_ge(x_scaled, t + 2)
                if not first:
                    pe.wait_ge(h_lo_done, t + 1)
                for kt in range(KD):
                    last = pe.transpose(pT[:, kt, :], xs[:, b, kt * P:(kt + 1) * P], k.ident[:, :])
                last.then_inc(x_turned, 1)

            def project(t, b, n, first=False, free=False):
                pe.wait_ge(h_lo_done, t + 2)
                if not (first or free):
                    pe.wait_ge(qk_normed, t)
                    pe.wait_ge(v_copied, t)
                for c0, c1 in ((0, CH), (CH, QKV)):
                    for kt in range(KD):
                        if first:
                            pe.wait_ge(w_split, kt + 2)
                        last = mm3(pe, pQ[:, b, c0:c1], h_hi[b][:, kt, :], h_lo[b][:, kt, :],
                                   wq_hi[:, kt, c0:c1], wq_lo[:, kt, c0:c1], kt == 0, kt == KD - 1)
                last.then_inc(qkv_done, 1)

            def turn_qk(t, b, n):
                pe.wait_ge(qk_rot, 2 * t + 3)
                pe.wait_ge(qkT_copied, t + 1)
                for a in range(QK // P):
                    last = pe.transpose(pR[:, a, :], qk_r[:, 2 * a:2 * a + 2, :].rearrange("p h d -> p (h d)"),
                                        k.ident[:, :])
                last.then_inc(qk_turned, 1)

            turn_x(*ring(0, 0), first=True)
            turn_x(*ring(0, 1))
            project(*ring(0, 0), first=True)

            def step(tile, t):
                if there(t, 2):
                    turn_x(*tile(2))
                if there(t, -1):
                    turn_qk(*tile(-1))
                if there(t, 1):
                    project(*tile(1), free=t == 0)

            steps(pe, step)
            turn_qk(*ring(0, NT - 1))
    return used


def input_projection(nc, k, hT_hi, hT_lo):
    with ExitStack() as ctx:
        def sb(name, shape, dt=F32):
            return ctx.enter_context(nc.sbuf_tensor(name, shape, dt))

        used = []

        def sem(name):
            used.append(ctx.enter_context(nc.semaphore(name)))
            return used[-1]

        raw = sb("win_raw", [P, 2, KD, P])
        w_hi = sb("win_hi", [P, 2, KD, P], F32R)
        w_lo = sb("win_lo", [P, 2, KD, P], F32R)
        z_st = sb("z_st", [P, 2, TOK])
        pZ = ctx.enter_context(nc.psum_tensor("pZ", [P, 2, NCH, CH], F32))
        w_in = [sem(f"win_in{b}") for b in range(2)]
        gate_placed, hi_done, lo_done = sem("gate_placed"), sem("win_hi_done"), sem("win_lo_done")
        product = sem("z_product")
        raw_free, bank_free = sem("raw_free"), sem("bank_free")
        z_out = [sem(f"z_out{b}") for b in range(2)]

        R = 64
        bias_i, bias_f = sb("bias_i", [R, 1]), sb("bias_f", [R, 1])
        gi, gf = sb("gi", [R, TOK]), sb("gf", [R, TOK])
        t0, t1 = sb("gate_t0", [R, TOK]), sb("gate_t1", [R, TOK])
        ones = sb("gate_ones", [R, TOK])
        cum, top = sb("gate_cum", [R, TOK]), sb("gate_top", [R, TOK])
        pG = ctx.enter_context(nc.psum_tensor("pGate", [P, 2, 8, R], F32))
        zeroed, bias_in, a_step, v_step = sem("bias_zeroed"), sem("bias_in"), sem("gate_act"), sem("gate_dve")
        turned, cols, scans_out = sem("gate_turned"), sem("gate_cols"), sem("gate_out")
        segs = ((0, SEG_TILES[0] * P), (SEG_TILES[0] * P, TOK))
        halves = ((0, 0, 8), (1, 8, NT))
        start_at_one(nc, used)
        block = ctx.enter_context(nc.Block())
        wv = k.w_in.rearrange("(t p) n -> p t n", p=P)
        zv = k.zT.rearrange("(a p) t -> a p t", p=P)
        half = 3 * MH // 4
        runs = [(half, COL_M, 0, ACT.Copy), (half, COL_M + 2 * half * P, 2 * half, ACT.Copy),
                (MH // 2, COL_O, 3 * MH, ACT.Sigmoid),
                (KD // 2, COL_GA, 4 * MH, ACT.Sigmoid), (KD // 2, COL_GA + KD * P, 4 * MH + KD, ACT.Sigmoid)]
        n_tiles = 1 + sum(2 * r[0] for r in runs)

        @block.sync
        def _(sp):
            gates = wv[:, :, COL_GATE:COL_GATE + N_GATE]
            sp.wait_ge(gate_placed, 2)
            for q, g in ((0, 0), (2, 1), (1, 2), (3, 3)):
                sp.dma_start(raw[:, 0, :, 32 * q:32 * q + MH], gates[:, :, g * MH:(g + 1) * MH]).then_inc(w_in[0], 16)
            sp.wait_ge(zeroed, 3)
            for q, g, dst in ((0, 0, bias_i), (0, 1, bias_f), (1, 2, bias_i), (1, 3, bias_f)):
                sp.dma_start(dst[32 * q:32 * q + MH, :],
                             k.b_if[g * MH:(g + 1) * MH].rearrange("(p a) -> p a", a=1)).then_inc(bias_in, 16)
            done = 0
            for r, (pairs, col, _, _) in enumerate(runs):
                if r == 4:
                    sp.wait_ge(v_step, 8)
                    for d in range(2):
                        sp.dma_start(k.negA[d * MH:(d + 1) * MH, :], t1[32 * d:32 * d + MH, :]).then_inc(scans_out, 16)
                with sp.Fori(0, pairs) as i:
                    for u in range(2):
                        f, b, n = ring(i, 1 + done + u)
                        sp.wait_ge(raw_free, f + 2)
                        sp.dma_start(raw[:, b, :, :], wv[:, :, bass.ds(col + (2 * i + u) * P, P)]).then_inc(w_in[b], 16)
                done += 2 * pairs
            sp.wait_ge(scans_out, 33)

        @block.vector
        def _(dve):
            dve.memset(raw[:, 0, :, :], 0.0).then_inc(gate_placed, 1)
            dve.sem_inc(raw_free, 2)

            def split(f, b, n):
                dve.wait_ge(w_in[b], (16 * (n + 1) + (48 if b == 0 else 0)) + 1)
                dve.wait_ge(product, NCH * f + 1)
                dve.tensor_copy(w_hi[:, b], raw[:, b]).then_inc(hi_done, 1)
                dve.wait_ge(hi_done, f + 2)
                dve.tensor_tensor(w_lo[:, b], raw[:, b], w_hi[:, b].bitcast(F32), ALU.subtract).then_inc(lo_done, 1)
                dve.wait_ge(lo_done, f + 2)
                dve.sem_inc(raw_free, 1)

            def scans(out_t, data0, data1, op0, op1):
                for s0, s1 in segs:
                    dve.tensor_tensor_scan(out_t[0:32, s0:s1], data0[0:32, s0:s1], data1[0:32, s0:s1], 0.0,
                                           op0, op1)
                    rev = slice(s1 - 1, s0 - 1 if s0 else None, -1)
                    last = dve.tensor_tensor_scan(out_t[32:64, rev], data0[32:64, rev], data1[32:64, rev],
                                                  0.0, op0, op1)
                last.then_inc(v_step, 1)

            def forget_sums():
                dve.wait_ge(a_step, 6)
                dve.scalar_tensor_tensor(out=gf[:, :], in0=gf[:, :], scalar=0.0, in1=t0[:, :],
                                         op0=ALU.min, op1=ALU.subtract).then_inc(v_step, 1)
                dve.wait_ge(v_step, 3)
                scans(cum, ones, gf, ALU.mult, ALU.add)

            def running_maxima():
                dve.wait_ge(v_step, 4)
                dve.tensor_tensor(gi[:, :], gi[:, :], cum[:, :], ALU.subtract).then_inc(v_step, 1)
                dve.wait_ge(v_step, 5)
                scans(top, ones, gi, ALU.mult, ALU.max)
                dve.wait_ge(v_step, 6)
                dve.tensor_scalar(t1[:, :], top[:, :], -1.0, None, ALU.mult).then_inc(v_step, 1)
                dve.wait_ge(v_step, 7)
                dve.tensor_tensor(t0[:, :], t1[:, :], cum[:, :], ALU.subtract).then_inc(v_step, 1)

            def a_columns():
                dve.wait_ge(turned, 2)
                for bank, n0, n1 in halves:
                    for d in range(2):
                        last = dve.tensor_copy(k.a_col[:, d, n0:n1, :], pG[:, bank, 0:n1 - n0, 32 * d:32 * d + MH])
                last.then_inc(cols, 1)

            dve.memset(bias_i[:, :], 0.0).then_inc(zeroed, 1)
            dve.memset(bias_f[:, :], 0.0).then_inc(zeroed, 1)
            dve.memset(ones[:, :], 1.0).then_inc(v_step, 1)
            split(*ring(0, 0))
            done = 0
            for r, (pairs, _, _, _) in enumerate(runs):
                if r == 2:
                    forget_sums()
                elif r == 3:
                    running_maxima()
                with dve.Fori(0, pairs) as i:
                    for u in range(2):
                        split(*ring(i, 1 + done + u))
                done += 2 * pairs
            a_columns()
            dve.wait_ge(cols, 2)

        @block.tensor
        def _(pe):
            pe.sem_inc(product, NCH)

            def products(f, b, n):
                pe.wait_ge(lo_done, f + 2)
                for c in range(NCH):
                    pe.wait_ge(bank_free, NCH * f + c + 2)
                    for kt in range(KD):
                        last = mm3(pe, pZ[:, b, c, :], w_hi[:, b, kt, :], w_lo[:, b, kt, :],
                                   hT_hi[:, kt, c * CH:(c + 1) * CH], hT_lo[:, kt, c * CH:(c + 1) * CH],
                                   kt == 0, kt == KD - 1)
                    last.then_inc(product, 1)

            def turn(src):
                for bank, n0, n1 in halves:
                    for t in range(n0, n1):
                        last = pe.transpose(pG[:, bank, t - n0, :], src[:, t * P:(t + 1) * P], k.ident[0:R, 0:R])
                last.then_inc(turned, 1)

            products(*ring(0, 0))
            done = 0
            for r, (pairs, _, _, _) in enumerate(runs):
                if r == 4:
                    pe.wait_ge(v_step, 8)
                    turn(gi)
                with pe.Fori(0, pairs) as i:
                    for u in range(2):
                        products(*ring(i, 1 + done + u))
                done += 2 * pairs
            pe.wait_ge(cols, 2)
            turn(t0)

        @block.scalar
        def _(act):
            act.sem_inc(bank_free, 2 * NCH)

            def evacuate(f, b, n, func, dst):
                for c in range(NCH):
                    act.wait_ge(product, NCH * (f + 1) + c + 2)
                    act.activation(dst[:, c * CH:(c + 1) * CH], pZ[:, b, c, :], func).then_inc(bank_free, 1)

            def log_sigmoid_parts():
                act.wait_ge(bias_in, 65)
                act.wait_ge(bank_free, 3 * NCH + 1)
                act.activation(gi[:, :], k.gates[0:R, :], ACT.Identity, bias=bias_i[:, 0:1]).then_inc(a_step, 1)
                act.activation(gf[:, :], k.gates[R:2 * R, :], ACT.Identity, bias=bias_f[:, 0:1]).then_inc(a_step, 1)
                act.wait_ge(a_step, 3)
                act.activation(t0[:, :], gf[:, :], ACT.Abs).then_inc(a_step, 1)
                act.wait_ge(a_step, 4)
                act.activation(t1[:, :], t0[:, :], ACT.Exp, scale=-1.0).then_inc(a_step, 1)
                act.wait_ge(a_step, 5)
                act.activation(t0[:, :], t1[:, :], ACT.Ln, bias=k.one[0:R, 0:1]).then_inc(a_step, 1)

            evacuate(*ring(0, 0), ACT.Copy, k.gates)
            done = 0
            for r, (pairs, _, tile0, func) in enumerate(runs):
                if r == 1:
                    log_sigmoid_parts()
                with act.Fori(0, pairs) as i:
                    for u in range(2):
                        f, b, n = ring(i, 1 + done + u)
                        act.wait_ge(z_out[b], (16 * (n - (1 if b == 0 else 0))) + 1)
                        evacuate(f, b, n, func, z_st[:, b, :])
                        act.wait_ge(bank_free, NCH * (f + 3) + 1)
                        act.dma_start(zv[bass.ds(tile0 + 2 * i + u, 1)].rearrange("a p t -> (a p) t"),
                                      z_st[:, b, :]).then_inc(z_out[b], 16)
                done += 2 * pairs
            for b in range(2):
                act.wait_ge(z_out[b], 16 * (n_tiles - 1) // 2 + 1)
            act.wait_ge(turned, 3)
            for bank, n0, n1 in halves:
                for d in range(2):
                    act.activation(k.floor[:, d, n0:n1, :], pG[:, bank, 0:n1 - n0, 32 * d:32 * d + MH],
                                   ACT.Exp).then_inc(a_step, 1)
            act.wait_ge(a_step, 10)
    return used


def attention(nc, k):
    with ExitStack() as ctx:
        def sb(name, shape, dt=F32):
            return ctx.enter_context(nc.sbuf_tensor(name, shape, dt))

        used = []

        def sem(name):
            used.append(ctx.enter_context(nc.semaphore(name)))
            return used[-1]

        H2 = HEAD
        q_raw, k_raw = sb("q_raw", [P, TOK]), sb("k_raw", [P, TOK])
        v_raw = sb("v_raw", [P, NT, H2])
        q_stack = [sb(f"q_stack{h}", [P, TOK], F32R) for h in range(2)]
        k_hi = sb("k_hi", [P, TOK], F32R)
        k_lo = [sb(f"k_lo{h}", [P, TOK], F32R) for h in range(2)]
        v_both = sb("v_both", [P, NT, 2 * H2], F32R)
        v_high = sb("v_high", [P, NT, 2 * H2], F32R)
        probs = sb("probs", [P, 2, 8 * P])
        pT_hi = sb("pT_hi", [P, 2, 8, CH], F32R)
        pT_lo = sb("pT_lo", [P, 2, 8, CH], F32R)
        o_parts = sb("o_parts", [H2, 2, 2, CH])
        small = sb("att_small", [P, 8])
        pS = ctx.enter_context(nc.psum_tensor("pS", [P, 2, 8 * P], F32))
        pT = ctx.enter_context(nc.psum_tensor("pAT", [P, 2, 4, P], F32))
        pO = ctx.enter_context(nc.psum_tensor("pO", [P, 2, CH], F32))

        zeroed, k_in, v_in, q_in = sem("att_zeroed"), sem("k_in"), sem("v_in"), sem("q_in")
        k_hi_done, v_hi_done = sem("k_hi_done"), sem("v_hi_done")
        k_split, v_split = [sem(f"k_split{h}") for h in range(2)], sem("v_split")
        q_hi, q_split = [sem(f"q_hi{h}") for h in range(2)], [sem(f"q_split{h}") for h in range(2)]
        scored, maxed, exped = sem("scored"), sem("maxed"), sem("exped")
        inverted, normed, turned = sem("inverted"), sem("normed"), sem("turned")
        hi_done, lo_done, weighed = sem("pT_hi_done"), sem("pT_lo_done"), sem("weighed")
        o_copied, o_added = sem("o_copied"), sem("o_added")
        start_at_one(nc, used)
        block = ctx.enter_context(nc.Block())

        GROUPS = [(h, c) for h in range(2) for c in range(NCH)]
        UNITS = [(h, c, qb) for h, c in GROUPS for qb in range(CH // P)]
        KT = {c: SEG_OF_CHUNK[c][1] - SEG_OF_CHUNK[c][0] for c in range(NCH)}
        NU, NG = len(UNITS), len(GROUPS)
        quads = [(u, q) for u, (h, c, qb) in enumerate(UNITS) for q in range(KT[c] // 4)]
        NQD = len(quads)
        quads_before = [sum(1 for x in quads if x[0] < u) for u in range(NU + 1)]

        def q_low(eng, h):
            top, low = slice(h * H2, (h + 1) * H2), slice((1 - h) * H2, (2 - h) * H2)
            eng.tensor_tensor(q_stack[h][low, :], q_raw[top, :], q_stack[h][top, :].bitcast(F32),
                              ALU.subtract).then_inc(q_split[h], 1)

        def pairs(eng, body, per_kv=None):
            with eng.Fori(0, NKV) as g:
                if per_kv:
                    per_kv(g)
                with eng.Fori(0, 2) as j:
                    body(2 * g + j, g)

        @block.sync
        def _(sp):
            def load_k(g):
                for h in range(2):
                    wait_apart(sp, k, k_split[h], g + 1)
                for half in range(2):
                    sp.dma_start(k_raw[half * H2:(half + 1) * H2, :],
                                 k.qkT[bass.ds(NQ * HEAD + g * H2, H2), :]).then_inc(k_in, 16)

            def load_q(n, g):
                for h in range(2):
                    wait_apart(sp, k, q_split[h], n + 1)
                sp.dma_start(q_raw[:, :], k.qkT[bass.ds(n * P, P), :]).then_inc(q_in, 16)

            def load_v(g):
                wait_apart(sp, k, v_split, 2 * g + 1)
                sp.dma_start(v_raw[:, :, :], k.v[:, bass.ds(g * H2, H2)].rearrange("(t p) d -> p t d", p=P))\
                  .then_inc(v_in, 16)

            with sp.Fori(0, NKV) as g:
                load_k(g)
                load_q(2 * g, g)
                load_v(g)
                load_q(2 * g + 1, g)

        @block.gpsimd
        def _(pool):
            pool.memset(k_lo[0][H2:P, :].bitcast(F32), 0.0).then_inc(zeroed, 1)
            pool.wait_ge(zeroed, 2)
            pool.memset(k_lo[1][0:H2, :].bitcast(F32), 0.0).then_inc(zeroed, 1)
            pool.wait_ge(zeroed, 3)
            pool.memset(v_high[:, :, H2:2 * H2].bitcast(F32), 0.0).then_inc(zeroed, 1)
            pool.wait_ge(zeroed, 4)

            def split_kv(g):
                wait_apart(pool, k, v_hi_done, g + 2)
                wait_apart(pool, k, o_added, 2 * NG * g + 1)
                pool.tensor_copy(v_high[:, :, 0:H2], v_both[:, :, 0:H2]).then_inc(v_split, 1)
                pool.tensor_tensor(v_both[:, :, H2:2 * H2], v_raw[:, :, :], v_both[:, :, 0:H2].bitcast(F32),
                                   ALU.subtract).then_inc(v_split, 1)
                wait_apart(pool, k, k_hi_done, g + 2)
                wait_apart(pool, k, v_split, 2 * g + 3)
                pool.tensor_tensor(k_lo[1][H2:P, :], k_raw[H2:P, :], k_hi[H2:P, :].bitcast(F32),
                                   ALU.subtract).then_inc(k_split[1], 1)

            def pair(n, g):
                wait_apart(pool, k, k_split[1], g + 2)
                wait_apart(pool, k, o_added, n * NG + 1)
                wait_apart(pool, k, q_hi[1], n + 2)
                q_low(pool, 1)
                wait_apart(pool, k, q_split[1], n + 2)
                for group, (h, c) in enumerate(GROUPS):
                    wait_apart(pool, k, o_copied, 2 * (n * NG + group) + 3)
                    pool.tensor_tensor(k.a_T[h * H2:(h + 1) * H2, bass.ds(n, 1), c * CH:(c + 1) * CH]
                                       .rearrange("p a t -> p (a t)"), o_parts[:, group % 2, 0, :],
                                       o_parts[:, group % 2, 1, :], ALU.add).then_inc(o_added, 1)

            pairs(pool, pair, split_kv)
            pool.wait_ge(o_added, 4 * NG + 1)

        @block.scalar
        def _(act):
            def keep_k_hi(g):
                act.wait_ge(k_in, 32 * (g + 1) + 1)
                act.wait_ge(weighed, 2 * NG * g + 1)
                act.activation(k_hi[:, :], k_raw[:, :], ACT.Copy).then_inc(k_hi_done, 1)

            def keep_v_hi(g):
                act.wait_ge(v_in, 16 * (g + 1) + 1)
                act.activation(v_both[:, :, 0:H2], v_raw[:, :, :], ACT.Copy).then_inc(v_hi_done, 1)

            def keep_q_hi(n, h):
                rows = slice(h * H2, (h + 1) * H2)
                act.wait_ge(q_in, 16 * (n + 1) + 1)
                act.wait_ge(weighed, n * NG + 1)
                act.activation(q_stack[h][rows, :], q_raw[rows, :], ACT.Copy).then_inc(q_hi[h], 1)

            def exp(n, u):
                h, c, qb = UNITS[u]
                b = u % 2
                act.wait_ge(maxed, n * NU + u + 2)
                act.wait_ge(turned, (n * NQD + (quads_before[u - 1] if u >= 2 else 0)) + 1)
                act.activation(probs[:, b, 0:KT[c] * P], pS[:, b, 0:KT[c] * P], ACT.Exp, scale=-1.0,
                               bias=small[:, 2 + b:3 + b], accum_out=small[:, 4 + b:5 + b]).then_inc(exped, 1)

            def keep_hi(n, u):
                h, c, qb = UNITS[u]
                g = u // 4
                for q in range(KT[c] // 4):
                    at = quads_before[u] + q
                    act.wait_ge(turned, n * NQD + at + 2)
                    act.wait_ge(weighed, n * NG + max(g - 1, 0) + 1)
                    act.activation(pT_hi[:, g % 2, 4 * q:4 * q + 4, qb * P:(qb + 1) * P], pT[:, at % 2, :, :],
                                   ACT.Copy).then_inc(hi_done, 1)

            def keep_o(n, g):
                act.wait_ge(weighed, n * NG + g + 2)
                act.wait_ge(o_added, n * NG + max(g - 1, 0) + 1)
                act.activation(o_parts[:, g % 2, 0, :], pO[0:H2, g % 2, :], ACT.Copy).then_inc(o_copied, 1)
                act.activation(o_parts[:, g % 2, 1, :], pO[H2:P, g % 2, :], ACT.Copy).then_inc(o_copied, 1)

            def pair(n, g):
                for h in range(2):
                    keep_q_hi(n, h)
                exp(n, 0)
                exp(n, 1)
                for u in range(1, NU):
                    keep_hi(n, u - 1)
                    if u + 1 < NU:
                        exp(n, u + 1)
                    if u % 4 == 1 and u > 8:
                        keep_o(n, u // 4 - 2)
                keep_hi(n, NU - 1)
                keep_o(n, NG - 2)
                keep_o(n, NG - 1)

            def kv_hi(g):
                keep_k_hi(g)
                keep_v_hi(g)

            pairs(act, pair, kv_hi)

        @block.vector
        def _(dve):
            dve.wait_ge(zeroed, 4)

            def split_k(g):
                dve.wait_ge(k_hi_done, g + 2)
                dve.tensor_tensor(k_lo[0][0:H2, :], k_raw[0:H2, :], k_hi[0:H2, :].bitcast(F32),
                                  ALU.subtract).then_inc(k_split[0], 1)

            def split_q(n, h):
                dve.wait_ge(q_hi[h], n + 2)
                q_low(dve, h)

            def row_max(n, u):
                h, c, qb = UNITS[u]
                b = u % 2
                dve.wait_ge(scored, n * NU + u + 2)
                dve.wait_ge(exped, n * NU + max(u - 1, 0) + 1)
                dve.tensor_reduce(small[:, 2 + b:3 + b], pS[:, b, 0:KT[c] * P], AX_X, ALU.min).then_inc(maxed, 1)

            def invert(n, u):
                b = u % 2
                dve.wait_ge(exped, n * NU + u + 2)
                dve.wait_ge(normed, n * NU + max(u - 1, 0) + 1)
                dve.reciprocal(small[:, 6 + b:7 + b], small[:, 4 + b:5 + b]).then_inc(inverted, 1)

            def normalise(n, u):
                b = u % 2
                h, c, qb = UNITS[u]
                dve.wait_ge(inverted, n * NU + u + 2)
                dve.tensor_scalar(probs[:, b, 0:KT[c] * P], probs[:, b, 0:KT[c] * P], small[:, 6 + b:7 + b],
                                  None, ALU.mult).then_inc(normed, 1)

            def keep_lo(n, u):
                h, c, qb = UNITS[u]
                g = u // 4
                for q in range(KT[c] // 4):
                    at = quads_before[u] + q
                    dve.wait_ge(hi_done, n * NQD + at + 2)
                    dve.tensor_tensor(pT_lo[:, g % 2, 4 * q:4 * q + 4, qb * P:(qb + 1) * P], pT[:, at % 2, :, :],
                                      pT_hi[:, g % 2, 4 * q:4 * q + 4, qb * P:(qb + 1) * P].bitcast(F32),
                                      ALU.subtract).then_inc(lo_done, 1)

            def pair(n, g):
                split_q(n, 0)
                row_max(n, 0)
                for u in range(NU):
                    if u + 1 < NU:
                        row_max(n, u + 1)
                    invert(n, u)
                    normalise(n, u)
                    if u:
                        keep_lo(n, u - 1)
                keep_lo(n, NU - 1)

            pairs(dve, pair, split_k)

        @block.tensor
        def _(pe):
            def scores(n, u, kv):
                h, c, qb = UNITS[u]
                b = u % 2
                k0 = SEG_OF_CHUNK[c][0] * P
                q0 = c * CH + qb * P
                if u % (NU // 2) == 0:
                    pe.wait_ge(q_split[h], n + 2)
                    pe.wait_ge(k_split[h], kv + 2)
                pe.wait_ge(exped, n * NU + max(u - 1, 0) + 1)
                for s in range(KT[c] * P // CH):
                    keys = slice(k0 + s * CH, k0 + (s + 1) * CH)
                    out = pS[:, b, s * CH:(s + 1) * CH]
                    pe.matmul(out, q_stack[h][:, q0:q0 + P], k_hi[:, keys], start=True, stop=False)
                    last = pe.matmul(out, q_stack[h][:, q0:q0 + P], k_lo[h][:, keys], start=False, stop=True)
                last.then_inc(scored, 1)

            def turn(n, u):
                h, c, qb = UNITS[u]
                pe.wait_ge(normed, n * NU + u + 2)
                for q in range(KT[c] // 4):
                    at = quads_before[u] + q
                    pe.wait_ge(lo_done, n * NQD + max(at - 1, 0) + 1)
                    for i in range(4):
                        kt = 4 * q + i
                        last = pe.transpose(pT[:, at % 2, i, :], probs[:, u % 2, kt * P:(kt + 1) * P], k.ident[:, :])
                    last.then_inc(turned, 1)

            def weigh(n, g, quarter, kv):
                h, c = GROUPS[g]
                t0 = SEG_OF_CHUNK[c][0]
                if g == 0 and quarter == 0:
                    pe.wait_ge(v_split, 2 * kv + 3)
                if quarter == 0:
                    pe.wait_ge(lo_done, n * NQD + quads_before[4 * g + 4] + 1)
                    pe.wait_ge(o_copied, 2 * (n * NG + max(g - 1, 0)) + 1)
                for i in range(quarter * KT[c] // 4, (quarter + 1) * KT[c] // 4):
                    pe.matmul(pO[:, g % 2, :], v_both[:, t0 + i, :], pT_hi[:, g % 2, i, :],
                              start=(i == 0), stop=False)
                    last = pe.matmul(pO[:, g % 2, :], v_high[:, t0 + i, :], pT_lo[:, g % 2, i, :],
                                     start=False, stop=(i == KT[c] - 1))
                if quarter == 3:
                    last.then_inc(weighed, 1)

            def pair(n, kv):
                scores(n, 0, kv)
                scores(n, 1, kv)
                for u in range(NU):
                    if u + 2 < NU:
                        scores(n, u + 2, kv)
                    turn(n, u)
                    if u >= 4:
                        weigh(n, u // 4 - 1, u % 4, kv)
                for quarter in range(4):
                    weigh(n, NG - 1, quarter, kv)

            pairs(pe, pair)


def mlstm(nc, k):
    with ExitStack() as ctx:
        def sb(name, shape, dt=F32):
            return ctx.enter_context(nc.sbuf_tensor(name, shape, dt))

        used = []

        def sem(name):
            used.append(ctx.enter_context(nc.semaphore(name)))
            return used[-1]

        RING, MRING = 3, 4
        q_raw, k_raw, v_raw = sb("mq_raw", [P, TOK]), sb("mk_raw", [P, TOK]), sb("mv_raw", [P, TOK])
        negA = sb("negA_rows", [P, 2, TOK])
        negA_m = sb("negA_masked", [P, MRING, P])
        q_hi, q_lo = sb("mq_hi", [P, TOK], F32R), sb("mq_lo", [P, TOK], F32R)
        k_hi, k_lo = sb("mk_hi", [P, TOK], F32R), sb("mk_lo", [P, TOK], F32R)
        v_hi, v_lo = sb("mv_hi", [P, NT, MD], F32R), sb("mv_lo", [P, NT, MD], F32R)
        ones = sb("m_ones", [P, P], F32R)
        decay = sb("decay", [P, RING, CH])
        w_all = sb("w_all", [P, RING, CH])
        w_hi, w_lo = sb("mw_hi", [P, RING, CH], F32R), sb("mw_lo", [P, RING, CH], F32R)
        num = sb("h_num", [P, 2, CH])
        picked = sb("den_picked", [P, 8, P])
        floor_c = sb("floor_c", [P, 4, 2, 4])
        part = sb("h_part", [P, 2, 4, MD])
        a_head = sb("a_head", [P, 2, NT])
        pS = ctx.enter_context(nc.psum_tensor("pMS", [P, 2, CH], F32))
        pN = ctx.enter_context(nc.psum_tensor("pMN", [P, 2, CH], F32))
        pD = ctx.enter_context(nc.psum_tensor("pMD", [P, 2, CH], F32))
        pV = ctx.enter_context(nc.psum_tensor("pMV", [P, 2, 4, MD], F32))

        fixed, masked = sem("m_fixed"), sem("masked")

        def by_chunk(name):
            return [sem(f"{name}{c}") for c in range(NCH)]

        head_in, hi_qk, split = by_chunk("head_in"), by_chunk("m_hi"), by_chunk("m_split")
        v_turned, v_hi_done, v_split = by_chunk("v_turned"), by_chunk("v_hi_done"), by_chunk("v_split")
        a_ready = by_chunk("a_ready")
        scored, decayed, multiplied = sem("m_scored"), sem("decayed"), sem("multiplied")
        hi_done, lo_done, weighed = sem("w_hi_done"), sem("w_lo_done"), sem("m_weighed")
        copied_f, copied_b, steps = sem("copied_f"), sem("copied_b"), sem("m_steps")
        den_picked, h_turned = sem("den_picked_s"), sem("h_turned")
        scaled, added = sem("m_scaled"), sem("m_added")
        start_at_one(nc, used)
        block = ctx.enter_context(nc.Block())

        STEPS = [(c, i) for c in range(NCH) for i in range(*SEG_OF_CHUNK[c])]
        ITEMS = []
        for s, (c, i) in enumerate(STEPS):
            r = i - 4 * c
            if r <= 3:
                ITEMS.append((s, 0, max(r, 0), 4, r if r >= 0 else None))
            if r >= 0:
                ITEMS.append((s, 1, 0, min(r, 3) + 1, r if r <= 3 else None))
        NS, NI = len(STEPS), len(ITEMS)
        first_item = [min(m for m, x in enumerate(ITEMS) if x[0] == s) for s in range(NS)] + [NI]
        last_of_chunk = [max(m for m, x in enumerate(ITEMS) if STEPS[x[0]][0] == c) for c in range(NCH)]
        DIAG = [m for m, x in enumerate(ITEMS) if x[4] is not None]
        ND = len(DIAG)
        masked_by_chunk = [sum(1 for m in DIAG if m <= last_of_chunk[c]) for c in range(NCH)]
        first_of_chunk = [0] + [x + 1 for x in last_of_chunk[:-1]]
        PREP = [first_item[first_item.index(first_of_chunk[1]) + 4], 2, 5]
        prep_step = [max(s for s in range(NS) if first_item[s] <= PREP[c]) for c in range(NCH)]

        def cut(c):
            return slice(c * CH, (c + 1) * CH)

        def heads(eng, head):
            with eng.Fori(0, MH - 1) as n:
                head(n, False)
            head(MH - 1, True)

        def prepared_at(m, n, last, prepare):
            for c in range(1, NCH):
                if m == PREP[c]:
                    prepare(n, c)
            if m == PREP[0] and not last:
                prepare(n + 1, 0)

        zrow = k.zT.rearrange("(a p) t -> a p t", p=P)

        @block.sync
        def _(sp):
            def load(n, c):
                if not isinstance(n, int) or n:
                    wait_apart(sp, k, split[c], 2 * n + 1)
                    wait_apart(sp, k, v_turned[c], n + 1)
                for dst, a in ((q_raw, n), (k_raw, MH + n), (v_raw, 2 * MH + n)):
                    sp.dma_start(dst[:, cut(c)], zrow[bass.ds(a, 1), :, cut(c)].rearrange("a p t -> (a p) t"))\
                      .then_inc(head_in[c], 16)
                if not isinstance(n, int) or n:
                    wait_apart(sp, k, decayed, NI * (n - 1) + last_of_chunk[c] + 2)
                    wait_apart(sp, k, masked, ND * (n - 1) + masked_by_chunk[c] + 1)
                for d in range(2):
                    sp.dma_start(negA[:, d, cut(c)], k.negA[bass.ds(d * MH + n, 1), cut(c)]
                                 .rearrange("a t -> (a t)").partition_broadcast(P)).then_inc(head_in[c], 16)

            for c in range(NCH):
                load(0, c)
            with sp.Fori(1, MH) as n:
                for c in range(NCH):
                    load(n, c)

        @block.gpsimd
        def _(pool):
            pool.memset(ones[:, :].bitcast(F32), 1.0).then_inc(fixed, 1)
            with pool.Fori(0, MH) as n:
                for j, m in enumerate(DIAG):
                    s, d, _, _, b = ITEMS[m]
                    t0 = (4 * STEPS[s][0] + b) * P
                    if m == first_of_chunk[STEPS[s][0]]:
                        pool.wait_ge(head_in[STEPS[s][0]], 80 * (n + 1) + 1)
                    wait_apart(pool, k, decayed, (NI * n + (DIAG[j - MRING] + 1 if j >= MRING else 0)) + 1)
                    pool.tensor_tensor(negA_m[:, j % MRING, :], negA[:, d, t0:t0 + P], k.mask[:, d, :],
                                       ALU.add).then_inc(masked, 1)
            pool.wait_ge(fixed, 2)

        @block.scalar
        def _(act):
            def prepare(n, c):
                act.wait_ge(head_in[c], 80 * (n + 1) + 1)
                if not isinstance(n, int) or n:
                    act.wait_ge(weighed, NI * (n - 1) + (last_of_chunk[0] + 1 if c == 0 else NI) + 1)
                act.activation(k_hi[:, cut(c)], k_raw[:, cut(c)], ACT.Copy, scale=MD ** -0.5).then_inc(hi_qk[c], 1)
                act.activation(q_hi[:, cut(c)], q_raw[:, cut(c)], ACT.Copy).then_inc(hi_qk[c], 1)
                act.wait_ge(v_turned[c], n + 2)
                act.activation(v_hi[:, 4 * c:4 * c + 4, :], pV[:, 0, :, :], ACT.Copy).then_inc(v_hi_done[c], 1)

            def head(n, last):
                def decays(m):
                    s, d, b0, b1, diag = ITEMS[m]
                    c, i = STEPS[s]
                    act.wait_ge(multiplied, NI * n + max(m - RING + 1, 0) + 1)
                    bias = a_head[:, d, i:i + 1]
                    if m == first_of_chunk[c]:
                        for part in (0,) if c == 0 else (1, 2):
                            act.wait_ge(a_ready[part], n + 2)
                        act.wait_ge(head_in[c], 80 * (n + 1) + 1)
                    if diag is not None:
                        j = DIAG.index(m)
                        act.wait_ge(masked, ND * n + j + 2)
                        last = act.activation(decay[:, m % RING, diag * P:(diag + 1) * P], negA_m[:, j % MRING, :],
                                              ACT.Exp, bias=bias)
                    for lo, hi in ((b0, b1),) if diag is None else ((b0, diag), (diag + 1, b1)):
                        if lo < hi:
                            last = act.activation(decay[:, m % RING, lo * P:hi * P],
                                                  negA[:, d, c * CH + lo * P:c * CH + hi * P], ACT.Exp, bias=bias)
                    last.then_inc(decayed, 1)

                def keep_hi(m):
                    s, d, b0, b1, _ = ITEMS[m]
                    act.wait_ge(multiplied, NI * n + m + 2)
                    act.wait_ge(weighed, NI * n + max(m - RING + 1, 0) + 1)
                    act.activation(w_hi[:, m % RING, b0 * P:b1 * P], w_all[:, m % RING, b0 * P:b1 * P],
                                   ACT.Copy).then_inc(hi_done, 1)

                decays(0)
                for m in range(NI):
                    prepared_at(m, n, last, prepare)
                    if m + 1 < NI:
                        decays(m + 1)
                    keep_hi(m)
                    for c in range(NCH):
                        if m == min(last_of_chunk[c] + 1, NI - 1):
                            act.wait_ge(weighed, NI * n + last_of_chunk[c] + 2)
                            act.wait_ge(h_turned, NCH * n + c + 1)
                            act.activation(num[:, 0, :], pN[:, 0, :], ACT.Copy).then_inc(copied_f, 1)

            prepare(0, 0)
            heads(act, head)

        @block.vector
        def _(dve):
            def prepare(n, c):
                if not isinstance(n, int) or n:
                    dve.wait_ge(decayed, NI * (n - 1) + (last_of_chunk[0] + 1 if c == 0 else NI) + 1)
                tiles = slice(4 * c, 4 * c + 4)
                head = bass.ds(n, 1)
                dve.tensor_scalar(a_head[:, :, tiles], k.a_col[:, :, tiles, head].rearrange("p d t a -> p d (t a)"),
                                  1.0, None, ALU.mult).then_inc(a_ready[c], 1)
                dve.wait_ge(hi_qk[c], 2 * (n + 1) + 1)
                dve.scalar_tensor_tensor(out=k_lo[:, cut(c)], in0=k_raw[:, cut(c)], scalar=MD ** -0.5,
                                         in1=k_hi[:, cut(c)].bitcast(F32), op0=ALU.mult,
                                         op1=ALU.subtract).then_inc(split[c], 1)
                dve.tensor_tensor(q_lo[:, cut(c)], q_raw[:, cut(c)], q_hi[:, cut(c)].bitcast(F32),
                                  ALU.subtract).then_inc(split[c], 1)
                dve.wait_ge(v_hi_done[c], n + 2)
                dve.tensor_tensor(v_lo[:, tiles, :], pV[:, 0, :, :], v_hi[:, tiles, :].bitcast(F32),
                                  ALU.subtract).then_inc(v_split[c], 1)

            def head(n, last):
                def multiply(m):
                    s, d, b0, b1, _ = ITEMS[m]
                    dve.wait_ge(decayed, NI * n + m + 2)
                    dve.wait_ge(scored, NS * n + s + 2)
                    dve.wait_ge(lo_done, NI * n + max(m - RING + 1, 0) + 1)
                    dve.tensor_tensor(w_all[:, m % RING, b0 * P:b1 * P], decay[:, m % RING, b0 * P:b1 * P],
                                      pS[:, s % 2, b0 * P:b1 * P], ALU.mult).then_inc(multiplied, 1)

                def keep_lo(m):
                    s, d, b0, b1, _ = ITEMS[m]
                    dve.wait_ge(hi_done, NI * n + m + 2)
                    dve.tensor_tensor(w_lo[:, m % RING, b0 * P:b1 * P], w_all[:, m % RING, b0 * P:b1 * P],
                                      w_hi[:, m % RING, b0 * P:b1 * P].bitcast(F32), ALU.subtract).then_inc(lo_done, 1)

                def denominators(c):
                    at = NCH * n + c
                    dve.wait_ge(weighed, NI * n + last_of_chunk[c] + 2)
                    dve.wait_ge(h_turned, at + 1)
                    dve.tensor_copy(num[:, 1, :], pN[:, 1, :]).then_inc(copied_b, 1)
                    dve.wait_ge(den_picked, 2 * at + 1)
                    dve.tensor_tensor(picked[:, :, :], pD[:, :, :].rearrange("p d (b t) -> p (d b) t", t=P),
                                      k.ident[:, :].rearrange("p (a t) -> p a t", a=1).to_broadcast([P, 8, P]),
                                      ALU.mult).then_inc(den_picked, 1)
                    dve.wait_ge(den_picked, 2 * at + 2)
                    den = floor_c[:, 3, :, :]
                    dve.tensor_reduce(den.rearrange("p d b -> p (d b)"), picked[:, :, :], AX_X,
                                      ALU.add).then_inc(den_picked, 1)
                    dve.wait_ge(den_picked, 2 * at + 3)
                    dve.scalar_tensor_tensor(out=floor_c[:, 0, :, :], in0=den, scalar=-1.0, in1=den,
                                             op0=ALU.mult, op1=ALU.max).then_inc(steps, 1)
                    dve.wait_ge(steps, 3 * at + 2)
                    dve.tensor_tensor(floor_c[:, 1, :, :], floor_c[:, 0, :, :],
                                      k.floor[:, :, 4 * c:4 * c + 4, bass.ds(n, 1)].rearrange("p d t a -> p d (t a)"),
                                      ALU.max).then_inc(steps, 1)
                    dve.wait_ge(steps, 3 * at + 3)
                    dve.reciprocal(floor_c[:, 2, :, :], floor_c[:, 1, :, :]).then_inc(steps, 1)

                def divide(c):
                    at = NCH * n + c
                    dve.wait_ge(steps, 3 * at + 4)
                    dve.wait_ge(h_turned, at + 2)
                    dve.wait_ge(added, at + 1)
                    for d in range(2):
                        dve.tensor_tensor(part[:, d, :, :], pV[:, d, :, :],
                                          floor_c[:, 2, d, :].unsqueeze(2).to_broadcast([P, 4, MD]),
                                          ALU.mult).then_inc(scaled, 1)
                    dve.wait_ge(scaled, 2 * at + 3)
                    dve.tensor_tensor(k.h_sum[:, 4 * c:4 * c + 4, bass.ds(n, 1), :]
                                      .rearrange("p t a d -> p t (a d)"),
                                      part[:, 0, :, :], part[:, 1, :, :], ALU.add).then_inc(added, 1)

                multiply(0)
                for m in range(NI):
                    prepared_at(m, n, last, prepare)
                    if m + 1 < NI:
                        multiply(m + 1)
                    keep_lo(m)
                    for c in range(NCH):
                        if m == min(last_of_chunk[c] + 1, NI - 1):
                            denominators(c)
                        if m == min(last_of_chunk[c] + 4, NI - 1):
                            divide(c)

            prepare(0, 0)
            heads(dve, head)
            dve.wait_ge(added, NCH * MH + 1)

        @block.tensor
        def _(pe):
            pe.wait_ge(fixed, 2)
            def prepare(n, c):
                pe.wait_ge(head_in[c], 80 * (n + 1) + 1)
                if c:
                    pe.wait_ge(v_split[c - 1], n + 2)
                if not isinstance(n, int) or n:
                    pe.wait_ge(scaled, 2 * NCH * (n - 1) + (2 if c == 0 else 2 * NCH) + 1)
                for a in range(4):
                    t = 4 * c + a
                    last = pe.transpose(pV[:, 0, a, :], v_raw[:, t * P:(t + 1) * P], k.ident[:, :])
                last.then_inc(v_turned[c], 1)

            def head(n, last_head):
                def scores(s):
                    c, i = STEPS[s]
                    if s == 0 or STEPS[s - 1][0] != c:
                        for part in (0,) if c == 0 else (1, 2):
                            pe.wait_ge(split[part], 2 * (n + 1) + 1)
                    pe.wait_ge(multiplied, (NI * n + (first_item[s - 1] if s >= 2 else 0)) + 1)
                    mm3(pe, pS[:, s % 2, :], k_hi[:, i * P:(i + 1) * P], k_lo[:, i * P:(i + 1) * P],
                        q_hi[:, c * CH:(c + 1) * CH], q_lo[:, c * CH:(c + 1) * CH], True, True).then_inc(scored, 1)

                def weigh(m, begun):
                    s, d, b0, b1, _ = ITEMS[m]
                    c, i = STEPS[s]
                    pe.wait_ge(lo_done, NI * n + m + 2)
                    if m == first_of_chunk[c]:
                        for part in (0,) if c == 0 else (1, 2):
                            pe.wait_ge(v_split[part], n + 2)
                    if d not in begun:
                        pe.wait_ge(copied_b if d else copied_f, NCH * n + c + 1)
                        pe.wait_ge(den_picked, 2 * (NCH * n + c) + 1)
                    cols = slice(b0 * P, b1 * P)
                    hi, lo = w_hi[:, m % RING, cols], w_lo[:, m % RING, cols]
                    first = d not in begun
                    begun.add(d)
                    free = dict(skip_group_check=True)
                    pe.matmul(pN[:, d, cols], v_hi[:, i, :], hi, start=first, stop=False, **free)
                    pe.matmul(pN[:, d, cols], v_hi[:, i, :], lo, start=False, stop=False, **free)
                    pe.matmul(pN[:, d, cols], v_lo[:, i, :], hi, start=False, stop=True, **free)
                    pe.matmul(pD[:, d, cols], ones[:, :], hi, start=first, stop=False, **free)
                    pe.matmul(pD[:, d, cols], ones[:, :], lo, start=False, stop=True, **free).then_inc(weighed, 1)

                def turn_back(c):
                    at = NCH * n + c
                    pe.wait_ge(copied_f, at + 2)
                    pe.wait_ge(copied_b, at + 2)
                    pe.wait_ge(scaled, 2 * at + 1)
                    if c == 0:
                        pe.wait_ge(v_split[2], n + 2)
                    elif not last_head:
                        pe.wait_ge(v_split[0], n + 3)
                    for d in range(2):
                        for b in range(4):
                            last = pe.transpose(pV[:, d, b, :], num[:, d, b * P:(b + 1) * P], k.ident[:, :])
                    last.then_inc(h_turned, 1)

                scores(0)
                scores(1)
                for s in range(NS):
                    c = STEPS[s][0]
                    for part in range(NCH):
                        if s == prep_step[part] and not (part == 0 and last_head):
                            prepare(n + (part == 0), part)
                    if s + 2 < NS:
                        scores(s + 2)
                    if s == 0 or STEPS[s - 1][0] != c:
                        begun = set()
                    for m in range(first_item[s], first_item[s + 1]):
                        weigh(m, begun)
                        if c and m == last_of_chunk[c - 1] + 1:
                            turn_back(c - 1)
                turn_back(NCH - 1)

            prepare(0, 0)
            heads(pe, head)


def mlstm_norm(nc, k):
    with ExitStack() as ctx:
        def sb(name, shape, dt=F32):
            return ctx.enter_context(nc.sbuf_tensor(name, shape, dt))

        def sem(name):
            return ctx.enter_context(nc.semaphore(name))

        gain = sb("m_gain", [P, MH])
        sq = sb("m_sq", [P, 2, NT, MD])
        hn = sb("m_hn", [P, 2, NT, MD])
        sig_o = sb("sig_o", [P, 2, TOK])
        mT_st = sb("mT_st", [P, 2, TOK])
        stat = sb("m_stat", [P, 2, 3, NT])
        pT = ctx.enter_context(nc.psum_tensor("pNT", [P, 2, NT, P], F32))
        gain_in, o_in = sem("m_gain_in"), [sem(f"o_in{b}") for b in range(2)]
        squared, summed, rooted, inverted = sem("n_squared"), sem("n_summed"), sem("n_rooted"), sem("n_inverted")
        scaled, turned, gated = sem("n_scaled"), sem("n_turned"), sem("n_gated")
        a_hi_done, a_split, m_hi_done, m_split = sem("a_hi_done"), sem("a_split"), sem("mT_hi_done"), sem("mT_split")
        block = ctx.enter_context(nc.Block())

        @block.sync
        def _(sp):
            for h in range(MH):
                sp.dma_start(gain[:, h:h + 1], k.mlstm_norm[h * MD:(h + 1) * MD].rearrange("(p a) -> p a", a=1))\
                  .then_inc(gain_in, 16)
            for h in range(MH):
                if h >= 2:
                    sp.wait_ge(gated, h - 1)
                sp.dma_start(sig_o[:, h % 2, :], k.zT[(3 * MH + h) * P:(3 * MH + h + 1) * P, :]).then_inc(o_in[h % 2], 16)

        @block.scalar
        def _(act):
            def m_hi(h):
                act.wait_ge(gated, h + 1)
                act.activation(k.b_hi[:, MH + h, :], mT_st[:, h % 2, :], ACT.Copy).then_inc(m_hi_done, 1)

            for h in range(MH):
                if h >= 2:
                    act.wait_ge(summed, h - 1)
                act.activation(sq[:, h % 2, :, :], k.h_sum[:, :, h, :], ACT.Square).then_inc(squared, 1)
            for h in range(MH):
                act.wait_ge(summed, h + 1)
                if h >= 2:
                    act.wait_ge(inverted, h - 1)
                act.activation(stat[:, h % 2, 1, :], stat[:, h % 2, 0, :], ACT.Sqrt, scale=1.0 / MD,
                               bias=k.eps[:, 0:1]).then_inc(rooted, 1)
                act.activation(k.b_hi[:, h, :], k.a_T[:, h, :], ACT.Copy).then_inc(a_hi_done, 1)
                if h:
                    m_hi(h - 1)
            m_hi(MH - 1)

        @block.gpsimd
        def _(pool):
            for a in range(MW // P):
                pool.wait_ge(a_hi_done, a + 1)
                pool.tensor_tensor(k.b_lo[:, a, :], k.a_T[:, a, :], k.b_hi[:, a, :].bitcast(F32),
                                   ALU.subtract).then_inc(a_split, 1)
            pool.wait_ge(a_split, MW // P)

        @block.vector
        def _(dve):
            def sums(h):
                dve.wait_ge(squared, h + 1)
                if h >= 2:
                    dve.wait_ge(rooted, h - 1)
                dve.tensor_reduce(stat[:, h % 2, 0, :], sq[:, h % 2, :, :], AX_X, ALU.add).then_inc(summed, 1)

            def scale(h):
                dve.wait_ge(rooted, h + 1)
                if h >= 2:
                    dve.wait_ge(scaled, h - 1)
                dve.reciprocal(stat[:, h % 2, 2, :], stat[:, h % 2, 1, :]).then_inc(inverted, 1)
                dve.wait_ge(inverted, h + 1)
                if h >= 2:
                    dve.wait_ge(turned, h - 1)
                dve.tensor_tensor(hn[:, h % 2, :, :], k.h_sum[:, :, h, :],
                                  stat[:, h % 2, 2, :].unsqueeze(2).to_broadcast([P, NT, MD]),
                                  ALU.mult).then_inc(scaled, 1)

            def gate(h):
                dve.wait_ge(turned, h + 1)
                dve.wait_ge(o_in[h % 2], 16 * (h // 2 + 1))
                if h >= 2:
                    dve.wait_ge(m_split, h - 1)
                dve.scalar_tensor_tensor(out=mT_st[:, h % 2, :], in0=pT[:, h % 2, :, :].rearrange("p t d -> p (t d)"),
                                         scalar=gain[:, h:h + 1], in1=sig_o[:, h % 2, :],
                                         op0=ALU.mult, op1=ALU.mult).then_inc(gated, 1)

            def m_lo(h):
                dve.wait_ge(m_hi_done, h + 1)
                dve.tensor_tensor(k.b_lo[:, MH + h, :], mT_st[:, h % 2, :], k.b_hi[:, MH + h, :].bitcast(F32),
                                  ALU.subtract).then_inc(m_split, 1)

            dve.wait_ge(gain_in, 16 * MH)
            sums(0)
            for h in range(MH):
                if h + 1 < MH:
                    sums(h + 1)
                scale(h)
                if h:
                    gate(h - 1)
                if h >= 2:
                    m_lo(h - 2)
            gate(MH - 1)
            m_lo(MH - 2)
            m_lo(MH - 1)

        @block.tensor
        def _(pe):
            for h in range(MH):
                pe.wait_ge(scaled, h + 1)
                if h >= 2:
                    pe.wait_ge(gated, h - 1)
                for t in range(NT):
                    last = pe.transpose(pT[:, h % 2, t, :], hn[:, h % 2, t, :], k.ident[:, :])
                last.then_inc(turned, 1)


def merge(nc, k):
    with ExitStack() as ctx:
        def sb(name, shape, dt=F32):
            return ctx.enter_context(nc.sbuf_tensor(name, shape, dt))

        used = []

        def sem(name):
            used.append(ctx.enter_context(nc.semaphore(name)))
            return used[-1]

        KB = MW // P
        b_hi, b_lo = k.b_hi, k.b_lo
        raw = sb("wbo_raw", [P, 2, 2 * KB, P])
        w_hi, w_lo = sb("wbo_hi", [P, 2, 2 * KB, P], F32R), sb("wbo_lo", [P, 2, 2 * KB, P], F32R)
        sig = k.a_T[:, :, :].rearrange("p (b g) t -> p b g t", b=2)
        m_st = k.h_sum[:, 0:6, :, :].rearrange("p (b t) h d -> p b (t h d)", b=2)
        gated = sb("gated", [P, 2, CH])
        pB = ctx.enter_context(nc.psum_tensor("pB", [P, 2, 2, CH], F32))
        w_in, sig_in = [sem(f"wbo_in{b}") for b in range(2)], [sem(f"sig_in{b}") for b in range(2)]
        hi_done, split = sem("wbo_hi_done"), sem("wbo_split")
        product, mixed, added, slot_free = sem("b_product"), sem("mixed"), sem("m_added2"), sem("wbo_slots")
        out = [sem(f"merged_out{b}") for b in range(2)]
        start_at_one(nc, used)
        block = ctx.enter_context(nc.Block())
        zv = k.zT.rearrange("(a p) t -> a p t", p=P)

        @block.sync
        def _(sp):
            def weights(f, b):
                for w, part in ((k.w_attn_o, 0), (k.w_mlstm_o, 1)):
                    sp.dma_start(raw[:, b, part * KB:(part + 1) * KB, :],
                                 w.rearrange("(t p) n -> p t n", p=P)[:, :, bass.ds(f * P, P)]).then_inc(w_in[b], 16)
                for g in range(2):
                    sp.dma_start(sig[:, b, g, :], zv[bass.ds((4 * MH + g * KD) + f, 1)]
                                 .rearrange("a p t -> (a p) t")).then_inc(sig_in[b], 16)

            with sp.Fori(0, KD // 2) as i:
                for u in range(2):
                    f, b, n = ring(i, u)
                    sp.wait_ge(slot_free, f + 2)
                    weights(f, b)

        @block.scalar
        def _(act):
            with act.Fori(0, KD // 2) as i:
                for u in range(2):
                    f, b, n = ring(i, u)
                    act.wait_ge(added, NCH * f + NCH + 1)
                    act.dma_start(k.mergedT.rearrange("(a p) t -> a p t", p=P)[bass.ds(f, 1)]
                                  .rearrange("a p t -> (a p) t"), m_st[:, b, :]).then_inc(out[b], 16)
            for b in range(2):
                act.wait_ge(out[b], 16 * (KD // 2) + 1)

        @block.vector
        def _(dve):
            def split_w(f, b, n):
                dve.wait_ge(w_in[b], 32 * (n + 1) + 1)
                dve.wait_ge(slot_free, f + 2)
                dve.tensor_copy(w_hi[:, b], raw[:, b]).then_inc(hi_done, 1)
                dve.wait_ge(hi_done, f + 2)
                dve.tensor_tensor(w_lo[:, b], raw[:, b], w_hi[:, b].bitcast(F32), ALU.subtract).then_inc(split, 1)

            def mix(f, b, n):
                dve.wait_ge(sig_in[b], 32 * (n + 1) + 1)
                dve.wait_ge(out[b], 16 * n + 1)
                for c in range(NCH):
                    at = NCH * f + c
                    s = (NCH * b + c) % 2
                    cols = slice(c * CH, (c + 1) * CH)
                    dve.wait_ge(product, at + 2)
                    dve.wait_ge(added, at + 1)
                    dve.tensor_tensor(m_st[:, b, cols], pB[:, s, 0, :], sig[:, b, 0, cols], ALU.mult).then_inc(mixed, 1)
                    dve.tensor_tensor(gated[:, s, :], pB[:, s, 1, :], sig[:, b, 1, cols], ALU.mult).then_inc(mixed, 1)
                dve.wait_ge(mixed, 2 * NCH * f + 2 * NCH + 3)
                dve.sem_inc(slot_free, 1)

            dve.sem_inc(slot_free, 2)
            dve.sem_inc(mixed, 2)
            split_w(*ring(0, 0))
            with dve.Fori(0, KD // 2 - 1) as i:
                for u in range(2):
                    split_w(*ring(i, u + 1))
                    mix(*ring(i, u))
            split_w(*ring(0, KD - 1))
            mix(*ring(0, KD - 2))
            mix(*ring(0, KD - 1))

        @block.gpsimd
        def _(pool):
            with pool.Fori(0, KD // 2) as i:
                for u in range(2):
                    f, b, n = ring(i, u)
                    for c in range(NCH):
                        at = NCH * f + c
                        s = (NCH * b + c) % 2
                        cols = slice(c * CH, (c + 1) * CH)
                        pool.wait_ge(mixed, 2 * at + 5)
                        pool.tensor_tensor(m_st[:, b, cols], m_st[:, b, cols], gated[:, s, :],
                                           ALU.add).then_inc(added, 1)

        @block.tensor
        def _(pe):
            with pe.Fori(0, KD // 2) as i:
                for u in range(2):
                    f, b, n = ring(i, u)
                    pe.wait_ge(split, f + 2)
                    for c in range(NCH):
                        at = NCH * f + c
                        s = (NCH * b + c) % 2
                        pe.wait_ge(mixed, 2 * at + 1)
                        for g in range(2):
                            for kt in range(KB):
                                a = g * KB + kt
                                last = mm3(pe, pB[:, s, g, :], w_hi[:, b, a, :], w_lo[:, b, a, :],
                                           b_hi[:, a, c * CH:(c + 1) * CH], b_lo[:, a, c * CH:(c + 1) * CH],
                                           kt == 0, kt == KB - 1)
                        last.then_inc(product, 1)


def out_projection(nc, k, h2_hi, h2_lo):
    with ExitStack() as ctx:
        def sb(name, shape, dt=F32):
            return ctx.enter_context(nc.sbuf_tensor(name, shape, dt))

        used = []

        def sem(name):
            used.append(ctx.enter_context(nc.semaphore(name)))
            return used[-1]

        wo_hi, wo_lo = sb("wo_hi", [P, KD, D], F32R), sb("wo_lo", [P, KD, D], F32R)
        raw = sb("o_raw", [P, 2, D])
        m_hi, m_lo = sb("mg_hi", [P, 2, KD, P], F32R), sb("mg_lo", [P, 2, KD, P], F32R)
        x_t = sb("xr_t", [P, 2, D])
        w_raw = x_t[:, :, :].rearrange("p b (s n) -> p (b s) n", n=CH)
        HALVES = [(h, kt) for h in range(D // CH) for kt in range(KD)]
        row = sb("o_row", [P, D])
        post, pre = sb("post_gain", [P, D]), sb("pre_gain", [P, D])
        stat = sb("o_stat", [P, 8])
        pY = ctx.enter_context(nc.psum_tensor("pY", [P, 2, D], F32))
        pT = ctx.enter_context(nc.psum_tensor("pHT", [P, KD, P], F32))
        pN = ctx.enter_context(nc.psum_tensor("pNormed", [P, D], F32))
        gain_in, raw_in, x_in = sem("o_gain_in"), [sem(f"o_raw_in{b}") for b in range(2)], [sem(f"xr_in{b}") for b in range(2)]
        w_in, w_hi_done, w_split = [sem(f"wo_in{b}") for b in range(4)], sem("wo_hi_done"), sem("wo_split")
        hi_done, split, product = sem("o_hi_done"), sem("o_split"), sem("o_product")
        a_stat, v_rs, normed, x1_done, h_scaled = sem("o_stat_s"), sem("o_rs"), sem("o_normed"), sem("x1_done"), sem("h2_scaled")
        turned, h_hi_done, h_lo_done = sem("h2_turned"), sem("h2_hi_done"), sem("h2_lo_done")
        x1_out = [sem(f"x1_out{b}") for b in range(2)]
        start_at_one(nc, used)
        block = ctx.enter_context(nc.Block())
        wv = k.w_out.rearrange("(t p) n -> t p n", p=P)
        mv = k.mergedT.rearrange("(a p) t -> p a t", p=P)

        @block.sync
        def _(sp):
            def load_m(t, b):
                sp.dma_start(raw[:, b, :].rearrange("p (a t) -> p a t", t=P), mv[:, :, bass.ds(t * P, P)])\
                  .then_inc(raw_in[b], 16)

            for w, (h, kt) in enumerate(HALVES):
                if w >= 4:
                    sp.wait_ge(w_split, w - 2)
                sp.dma_start(w_raw[:, w % 4, :], wv[kt, :, h * CH:(h + 1) * CH]).then_inc(w_in[w % 4], 16)
                if w < 2:
                    load_m(w, w)
                if w == KD:
                    for g, dst in ((k.norm_mix_post, post), (k.norm_ffn_pre, pre)):
                        sp.dma_start(dst[:, :], g.partition_broadcast(P)).then_inc(gain_in, 16)
            sp.wait_ge(w_split, len(HALVES) + 1)
            for t in range(2):
                sp.dma_start(x_t[:, t, :], k.x[t * P:(t + 1) * P, :]).then_inc(x_in[t], 16)
            with sp.Fori(1, NT // 2) as i:
                for u in range(2):
                    t, b, n = ring(i, u)
                    sp.wait_ge(split, t)
                    load_m(t, b)
                    wait_apart(sp, k, x1_out[b], 16 * n + 1)
                    sp.wait_ge(h_scaled, t + 1)
                    sp.dma_start(x_t[:, b, :], k.x[bass.ds(t * P, P), :]).then_inc(x_in[b], 16)

        @block.scalar
        def _(act):
            def post_root(t, b, n):
                act.wait_ge(product, t + 2)
                act.wait_ge(x1_done, t + 1)
                act.activation(pN[:, :], pY[:, b, :], ACT.Square, accum_out=stat[:, 0:1]).then_inc(a_stat, 1)
                act.wait_ge(a_stat, 4 * t + 2)
                act.activation(stat[:, 1:2], stat[:, 0:1], ACT.Sqrt, scale=1.0 / D, bias=k.eps[:, 0:1]).then_inc(a_stat, 1)

            def pre_root(t, b, n):
                act.wait_ge(x1_done, t + 2)
                act.dma_start(k.x1[bass.ds(t * P, P), :], x_t[:, b, :]).then_inc(x1_out[b], 16)
                act.activation(pN[:, :], x_t[:, b, :], ACT.Square, accum_out=stat[:, 3:4]).then_inc(a_stat, 1)
                act.wait_ge(a_stat, 4 * t + 4)
                act.activation(stat[:, 4:5], stat[:, 3:4], ACT.Sqrt, scale=1.0 / D, bias=k.eps[:, 0:1]).then_inc(a_stat, 1)

            def keep_hi(t, b, n):
                act.wait_ge(turned, t + 2)
                act.activation(h2_hi[:, :, bass.ds(t * P, P)], pT[:, :, :], ACT.Copy).then_inc(h_hi_done, 1)

            post_root(*ring(0, 0))
            with act.Fori(0, NT // 2 - 1) as i:
                for u in range(2):
                    pre_root(*ring(i, u))
                    post_root(*ring(i, u + 1))
                    keep_hi(*ring(i, u))
            pre_root(*ring(0, NT - 2))
            post_root(*ring(0, NT - 1))
            keep_hi(*ring(0, NT - 2))
            pre_root(*ring(0, NT - 1))
            keep_hi(*ring(0, NT - 1))
            for b in range(2):
                act.wait_ge(x1_out[b], 16 * (NT // 2) + 1)

        @block.vector
        def _(dve):
            def split_w(w):
                h, kt = HALVES[w]
                hi, lo = (x[:, kt, h * CH:(h + 1) * CH] for x in (wo_hi, wo_lo))
                dve.wait_ge(w_in[w % 4], 16 * (w // 4 + 1) + 1)
                dve.tensor_copy(hi, w_raw[:, w % 4, :]).then_inc(w_hi_done, 1)
                dve.wait_ge(w_hi_done, w + 2)
                dve.tensor_tensor(lo, w_raw[:, w % 4, :], hi.bitcast(F32), ALU.subtract).then_inc(w_split, 1)

            dve.sem_inc(h_scaled, 1)

            def split_m(t, b, n, first=False):
                dve.wait_ge(raw_in[b], 16 * (n + 1) + 1)
                if not first:
                    dve.wait_ge(product, t)
                rows = raw[:, b, :].rearrange("p (a t) -> p a t", t=P)
                dve.tensor_copy(m_hi[:, b], rows).then_inc(hi_done, 1)
                dve.wait_ge(hi_done, t + 2)
                dve.tensor_tensor(m_lo[:, b], rows, m_hi[:, b].bitcast(F32), ALU.subtract).then_inc(split, 1)

            def post_norm(t, b, n):
                dve.wait_ge(a_stat, 4 * t + 3)
                dve.reciprocal(stat[:, 2:3], stat[:, 1:2]).then_inc(v_rs, 1)
                dve.wait_ge(v_rs, 2 * t + 2)
                dve.scalar_tensor_tensor(out=pN[:, :], in0=pY[:, b, :], scalar=stat[:, 2:3], in1=post[:, :],
                                         op0=ALU.mult, op1=ALU.mult).then_inc(normed, 1)
                dve.wait_ge(normed, t + 2)
                dve.wait_ge(x_in[b], 16 * (n + 1) + 1)
                dve.tensor_tensor(x_t[:, b, :], x_t[:, b, :], pN[:, :], ALU.add).then_inc(x1_done, 1)
                dve.wait_ge(a_stat, 4 * t + 5)
                dve.reciprocal(stat[:, 5:6], stat[:, 4:5]).then_inc(v_rs, 1)
                dve.wait_ge(v_rs, 2 * t + 3)
                dve.wait_ge(turned, t + 1)
                dve.scalar_tensor_tensor(out=row[:, :], in0=x_t[:, b, :], scalar=stat[:, 5:6], in1=pre[:, :],
                                         op0=ALU.mult, op1=ALU.mult).then_inc(h_scaled, 1)

            def keep_lo(t, b, n):
                dve.wait_ge(h_hi_done, t + 2)
                cols = bass.ds(t * P, P)
                dve.tensor_tensor(h2_lo[:, :, cols], pT[:, :, :], h2_hi[:, :, cols].bitcast(F32),
                                  ALU.subtract).then_inc(h_lo_done, 1)

            split_w(0)
            split_m(*ring(0, 0), first=True)
            for w in range(1, KD):
                split_w(w)
            split_m(*ring(0, 1), first=True)
            for w in range(KD, len(HALVES)):
                split_w(w)
            dve.wait_ge(gain_in, 33)
            with dve.Fori(0, NT // 2 - 1) as i:
                for u in range(2):
                    post_norm(*ring(i, u))
                    split_m(*ring(i, u + 2))
                    keep_lo(*ring(i, u))
            for t in (NT - 2, NT - 1):
                post_norm(*ring(0, t))
                keep_lo(*ring(0, t))

        @block.tensor
        def _(pe):
            def half(t, b, h, first=False):
                for kt in range(KD):
                    if first:
                        pe.wait_ge(w_split, h * KD + kt + 2)
                    last = mm3(pe, pY[:, b, h * CH:(h + 1) * CH], m_hi[:, b, kt, :], m_lo[:, b, kt, :],
                               wo_hi[:, kt, h * CH:(h + 1) * CH], wo_lo[:, kt, h * CH:(h + 1) * CH],
                               kt == 0, kt == KD - 1)
                return last

            def products(t, b, n):
                pe.wait_ge(split, t + 2)
                pe.wait_ge(normed, t)
                half(t, b, 0)
                half(t, b, 1).then_inc(product, 1)

            def turn(t, b, n):
                pe.wait_ge(h_scaled, t + 3)
                pe.wait_ge(h_lo_done, t + 1)
                for kt in range(KD):
                    last = pe.transpose(pT[:, kt, :], row[:, kt * P:(kt + 1) * P], k.ident[:, :])
                last.then_inc(turned, 1)

            pe.wait_ge(split, 2)
            half(0, 0, 0, first=True)
            pe.wait_ge(split, 3)
            half(1, 1, 0)
            half(0, 0, 1, first=True).then_inc(product, 1)
            half(1, 1, 1).then_inc(product, 1)
            with pe.Fori(0, NT // 2 - 1) as i:
                for u in range(2):
                    turn(*ring(i, u))
                    products(*ring(i, u + 2))
            turn(*ring(0, NT - 2))
            turn(*ring(0, NT - 1))


def ffn(nc, k, h2_hi, h2_lo, y_sum):
    with ExitStack() as ctx:
        def sb(name, shape, dt=F32):
            return ctx.enter_context(nc.sbuf_tensor(name, shape, dt))

        used = []

        def sem(name):
            used.append(ctx.enter_context(nc.semaphore(name)))
            return used[-1]

        act_hi, act_lo = sb("act_hi", [P, TOK], F32R), sb("act_lo", [P, TOK], F32R)
        raw = sb("ffn_raw", [P, 2, D])
        g_hi, g_lo = sb("wg_hi", [P, KD, P], F32R), sb("wg_lo", [P, KD, P], F32R)
        v_hi, v_lo = sb("wv_hi", [P, KD, P], F32R), sb("wv_lo", [P, KD, P], F32R)
        d_hi, d_lo = sb("wd_hi", [P, D], F32R), sb("wd_lo", [P, D], F32R)
        GP = TOK + 4
        gate = sb("gate_pad", [P, GP])
        conv = sb("conv", [P, CH])
        gelu = sb("gelu", [P, CH])
        taps = sb("taps", [P, CONV_W, NFF])
        conv_b = sb("conv_b", [P, NFF])
        pG = ctx.enter_context(nc.psum_tensor("pG", [P, NCH, CH], F32))
        pV = ctx.enter_context(nc.psum_tensor("pVal", [P, NCH, CH], F32))
        pD = ctx.enter_context(nc.psum_tensor("pD", [P, 2, CH], F32))
        taps_in, padded = sem("taps_in"), sem("padded")
        raw_in = [sem(f"ffn_in{b}") for b in range(2)]
        whi, wsplit = sem("ffn_whi"), sem("ffn_wsplit")
        gated, gate_copied, vald, downed = sem("gate_done"), sem("gate_copied"), sem("val_done"), sem("down_done")
        conv_s, gelu_done, act_f32, act_h, act_l, summed = (sem("conv_steps"), sem("gelu_done"), sem("act_f32"),
                                                            sem("act_h"), sem("act_l"), sem("y_summed"))
        start_at_one(nc, used)
        block = ctx.enter_context(nc.Block())
        up = k.w_up.rearrange("(t p) n -> p t n", p=P)
        down = k.w_down.rearrange("(f p) n -> f p n", p=P)
        PAD_AT = [1, 3 + CH, 3 + 2 * CH]
        NEEDS = [1, 3, 3]
        NDT = NT * (D // CH)
        last_f = NFF - 1

        def down_bank(j):
            return pV[:, j % 4, :] if j % 4 < 2 else pD[:, j % 4 - 2, :]

        @block.sync
        def _(sp):
            sp.dma_start(taps[:, :, :], k.conv_w).then_inc(taps_in, 16)
            sp.dma_start(conv_b[:, :], k.conv_b).then_inc(taps_in, 16)

            def load(at, b, src, first=False):
                if not first:
                    sp.wait_ge(wsplit, at)
                sp.dma_start(raw[:, b, :] if src is None else src[0](raw[:, b, :]), src[1]).then_inc(raw_in[b], 16)

            def square(a):
                return a.rearrange("p (t n) -> p t n", n=P)

            def three(f, odd, first=False):
                at = 3 * f
                load(at, odd, (square, up[:, :, bass.ds(f * P, P)]), first)
                load(at + 1, 1 - odd, (square, up[:, :, bass.ds(FF + f * P, P)]), first)
                load(at + 2, odd, (lambda a: a, down[bass.ds(f, 1)].rearrange("a p n -> (a p) n")))

            three(0, 0, first=True)
            three(1, 1)
            with sp.Fori(1, NFF // 2) as i:
                three(2 * i, 0)
                three(2 * i + 1, 1)

        @block.vector
        def _(dve):
            for a in (0, 1 + CH, 2 + CH, GP - 1):
                dve.memset(gate[:, a:a + 1], 0.0).then_inc(padded, 1)
            dve.wait_ge(taps_in, 33)
            dve.wait_ge(padded, 5)

            def split(at, b, n, hi, lo, used, count):
                dve.wait_ge(raw_in[b], 16 * (n + 1) + 1)
                dve.wait_ge(used, count + 1)
                flat = raw[:, b, :]
                dve.tensor_copy(hi, flat).then_inc(whi, 1)
                dve.wait_ge(whi, at + 2)
                dve.tensor_tensor(lo, flat, hi.bitcast(F32), ALU.subtract).then_inc(wsplit, 1)

            def flat(a):
                return a[:, :, :].rearrange("p t n -> p (t n)")

            def place(i, odd, j):
                c = 3 * odd + j
                return 6 * i + c, c % 2, 3 * i + c // 2

            def split_gate(i, odd):
                split(*place(i, odd, 0), flat(g_hi), flat(g_lo), gated, NCH * (2 * i + odd))

            def split_val(i, odd):
                split(*place(i, odd, 1), flat(v_hi), flat(v_lo), vald, NCH * (2 * i + odd))

            def split_down(i, odd):
                split(*place(i, odd, 2), d_hi[:, :], d_lo[:, :], downed, NDT * (2 * i + odd))

            def activate(f):
                for c in range(NCH):
                    at = NCH * f + c
                    dve.wait_ge(gate_copied, NCH * f + NEEDS[c] + 1)
                    dve.wait_ge(gelu_done, at + 1)
                    a = PAD_AT[c]

                    def tap(w):
                        return taps[:, w, bass.ds(f, 1)] if not isinstance(f, int) else taps[:, w, f:f + 1]

                    dve.tensor_scalar(conv[:, :], gate[:, a - 1:a - 1 + CH], tap(0), None, ALU.mult).then_inc(conv_s, 1)
                    for w in (1, 2):
                        dve.wait_ge(conv_s, 3 * at + w + 1)
                        dve.scalar_tensor_tensor(out=conv[:, :], in0=gate[:, a - 1 + w:a - 1 + w + CH], scalar=tap(w),
                                                 in1=conv[:, :], op0=ALU.mult, op1=ALU.add).then_inc(conv_s, 1)
                    dve.wait_ge(gelu_done, at + 2)
                    dve.wait_ge(vald, at + 2)
                    dve.tensor_tensor(gelu[:, :], gelu[:, :], pV[:, c, :], ALU.mult).then_inc(act_f32, 1)
                    dve.wait_ge(act_h, at + 2)
                    cols = slice(c * CH, (c + 1) * CH)
                    dve.tensor_tensor(act_lo[:, cols], gelu[:, :], act_hi[:, cols].bitcast(F32),
                                      ALU.subtract).then_inc(act_l, 1)

            def add_down(f, first=False):
                for t in range(NT):
                    for h in range(D // CH):
                        at = NDT * f + 2 * t + h
                        dve.wait_ge(downed, at + 2)
                        cols = slice(h * CH, (h + 1) * CH)
                        if first:
                            dve.tensor_copy(y_sum[:, t, cols], down_bank(2 * t + h)).then_inc(summed, 1)
                        else:
                            dve.wait_ge(summed, NDT * f + 1)
                            dve.tensor_tensor(y_sum[:, t, cols], y_sum[:, t, cols], down_bank(2 * t + h),
                                              ALU.add).then_inc(summed, 1)

            def step(i, odd, last=False):
                split_val(i, odd)
                add_down(2 * i + odd - 1)
                split_down(i, odd)
                if not last:
                    split_gate(i, odd + 1)
                activate(2 * i + odd)

            split_gate(0, 0)
            split_val(0, 0)
            split_down(0, 0)
            split_gate(0, 1)
            activate(0)
            split_val(0, 1)
            add_down(0, first=True)
            split_down(0, 1)
            split_gate(0, 2)
            activate(1)
            with dve.Fori(1, NFF // 2 - 1) as i:
                step(i, 0)
                step(i, 1)
            step(NFF // 2 - 1, 0)
            step(NFF // 2 - 1, 1, last=True)
            add_down(last_f)

        @block.scalar
        def _(act):
            act.wait_ge(padded, 5)
            act.wait_ge(taps_in, 33)

            def copy_gate(f):
                for c in range(NCH):
                    act.wait_ge(gated, NCH * f + c + 2)
                    act.wait_ge(conv_s, 3 * NCH * f + 1)
                    act.activation(gate[:, PAD_AT[c]:PAD_AT[c] + CH], pG[:, c, :], ACT.Copy).then_inc(gate_copied, 1)

            def gelus(f):
                for c in range(NCH):
                    at = NCH * f + c
                    wait_apart(act, k, conv_s, 3 * at + 3 + 1)
                    wait_apart(act, k, act_l, at + 1)
                    b = conv_b[:, bass.ds(f, 1)] if not isinstance(f, int) else conv_b[:, f:f + 1]
                    act.activation(gelu[:, :], conv[:, :], ACT.Gelu_apprx_tanh, bias=b).then_inc(gelu_done, 1)
                    act.wait_ge(act_f32, at + 2)
                    act.wait_ge(downed, NDT * f + 1)
                    act.activation(act_hi[:, c * CH:(c + 1) * CH], gelu[:, :], ACT.Copy).then_inc(act_h, 1)

            with act.Fori(0, NFF) as f:
                copy_gate(f)
                gelus(f)

        @block.tensor
        def _(pe):
            def ups(f, at_split, w_hi, w_lo, bank, done, free, shared=False):
                pe.wait_ge(wsplit, at_split + 2)
                for c in range(NCH):
                    pe.wait_ge(free, NCH * f + 1)
                    if shared and c < 2:
                        pe.wait_ge(summed, NDT * (f - 1) + NDT - 4 + c + 2)
                    for kt in range(KD):
                        last = mm3(pe, bank[:, c, :], w_hi[:, kt, :], w_lo[:, kt, :],
                                   h2_hi[:, kt, c * CH:(c + 1) * CH], h2_lo[:, kt, c * CH:(c + 1) * CH],
                                   kt == 0, kt == KD - 1)
                    last.then_inc(done, 1)

            def gate_products(f):
                ups(f, 3 * f, g_hi, g_lo, pG, gated, gate_copied)

            def val_products(f, first=False):
                ups(f, 3 * f + 1, v_hi, v_lo, pV, vald, act_f32, shared=not first)

            def down_products(f, first=False):
                pe.wait_ge(wsplit, 3 * f + 4)
                pe.wait_ge(act_l, NCH * f + NCH + 1)
                for t in range(NT):
                    for h in range(D // CH):
                        j = 2 * t + h
                        if j >= 4:
                            pe.wait_ge(summed, NDT * f + j - 4 + 2)
                        elif j >= 2 and not first:
                            pe.wait_ge(summed, NDT * f + 1)
                        cols = slice(h * CH, (h + 1) * CH)
                        mm3(pe, down_bank(j), act_hi[:, t * P:(t + 1) * P], act_lo[:, t * P:(t + 1) * P],
                            d_hi[:, cols], d_lo[:, cols], True, True).then_inc(downed, 1)

            gate_products(0)
            val_products(0, first=True)
            gate_products(1)
            down_products(0, first=True)
            val_products(1)
            with pe.Fori(2, NFF) as f:
                gate_products(f)
                down_products(f - 1)
                val_products(f)
            down_products(last_f)


def final_norm(nc, k, y_sum):
    with ExitStack() as ctx:
        def sb(name, shape, dt=F32):
            return ctx.enter_context(nc.sbuf_tensor(name, shape, dt))

        used = []

        def sem(name):
            used.append(ctx.enter_context(nc.semaphore(name)))
            return used[-1]

        RING = 4
        gain, x_t, y_t = sb("f_gain", [P, D]), sb("f_x1", [P, RING, D]), sb("f_y", [P, RING, D])
        squares, stat = sb("f_sq", [P, D]), sb("f_stat", [P, 3, RING])
        gain_in, x_in = sem("f_gain_in"), [sem(f"f_x1_in{b}") for b in range(RING)]
        squared, rooted, inverted, scaled, added = sem("f_squared"), sem("f_rooted"), sem("f_inverted"), sem("f_scaled"), sem("f_added")
        out = [sem(f"y_out{b}") for b in range(RING)]
        start_at_one(nc, used)
        block = ctx.enter_context(nc.Block())

        def tiles(eng, body):
            with eng.Fori(0, NT // RING) as i:
                for b in range(RING):
                    body(RING * i + b, b, i)

        @block.sync
        def _(sp):
            sp.dma_start(gain[:, :], k.norm_ffn_post.partition_broadcast(P)).then_inc(gain_in, 16)
            for b in range(RING):
                sp.dma_start(x_t[:, b, :], k.x1[b * P:(b + 1) * P, :]).then_inc(x_in[b], 16)

            def store(t, b):
                sp.wait_ge(added, t + 2)
                sp.dma_start(k.y[bass.ds(t * P, P), :], y_t[:, b, :]).then_inc(out[b], 16)

            with sp.Fori(0, NT // RING - 1) as i:
                for b in range(RING):
                    t = RING * i + b
                    store(t, b)
                    sp.dma_start(x_t[:, b, :], k.x1[bass.ds((t + RING) * P, P), :]).then_inc(x_in[b], 16)
            for b in range(RING):
                store(NT - RING + b, b)
            for b in range(RING):
                sp.wait_ge(out[b], 16 * (NT // RING) + 1)

        @block.scalar
        def _(act):
            act.sem_inc(inverted, RING - 1)

            def statistics(t, b, i):
                act.wait_ge(rooted, t + 1)
                act.activation(squares[:, :], y_sum[:, bass.ds(t, 1), :].rearrange("p a n -> p (a n)"), ACT.Square,
                               accum_out=stat[:, 0, b:b + 1]).then_inc(squared, 1)
                act.wait_ge(squared, t + 2)
                act.wait_ge(inverted, t + 1)
                act.activation(stat[:, 1, b:b + 1], stat[:, 0, b:b + 1], ACT.Sqrt, scale=1.0 / D,
                               bias=k.eps[:, 0:1]).then_inc(rooted, 1)

            tiles(act, statistics)

        @block.vector
        def _(dve):
            dve.wait_ge(gain_in, 17)
            dve.wait_ge(inverted, RING)

            def finish(t, b, i):
                dve.wait_ge(rooted, t + 2)
                dve.reciprocal(stat[:, 2, b:b + 1], stat[:, 1, b:b + 1]).then_inc(inverted, 1)
                dve.wait_ge(inverted, t + RING + 1)
                dve.wait_ge(out[b], 16 * i + 1)
                dve.scalar_tensor_tensor(out=y_t[:, b, :], in0=y_sum[:, bass.ds(t, 1), :].rearrange("p a n -> p (a n)"),
                                         scalar=stat[:, 2, b:b + 1], in1=gain[:, :],
                                         op0=ALU.mult, op1=ALU.mult).then_inc(scaled, 1)
                dve.wait_ge(scaled, t + 2)
                dve.wait_ge(x_in[b], 16 * (i + 1) + 1)
                dve.tensor_tensor(y_t[:, b, :], y_t[:, b, :], x_t[:, b, :], ALU.add).then_inc(added, 1)

            tiles(dve, finish)


class Names:
    pass


def start_at_one(nc, semaphores):
    with nc.Block() as block:
        @block.gpsimd
        def _(pool):
            for s in semaphores:
                pool.sem_inc(s, 1)


def clear(nc, semaphores):
    with nc.Block() as block:
        @block.gpsimd
        def _(pool):
            for s in semaphores:
                pool.sem_clear(s)


def constants(nc, k):
    made = k.made
    with nc.Block() as block:
        @block.gpsimd
        def _(pool):
            pool.memset(k.eps[:, :], EPS).then_inc(made, 1)
            pool.memset(k.one[:, :], 1.0).then_inc(made, 1)
            pool.memset(k.ident[:, :], 0.0).then_inc(made, 1)
            pool.memset(k.mask[:, :, :], 0.0).then_inc(made, 1)
            pool.wait_ge(made, 4)
            pool.affine_select(out=k.ident[:, :], in_=k.ident[:, :], compare_op=ALU.not_equal, fill=1.0, base=0,
                               pattern=[[-1, P]], channel_multiplier=1).then_inc(made, 1)
            pool.affine_select(out=k.mask[:, 0, :], in_=k.mask[:, 0, :], compare_op=ALU.is_ge, fill=NEG, base=0,
                               pattern=[[1, P]], channel_multiplier=-1).then_inc(made, 1)
            pool.affine_select(out=k.mask[:, 1, :], in_=k.mask[:, 1, :], compare_op=ALU.is_ge, fill=NEG, base=0,
                               pattern=[[-1, P]], channel_multiplier=1).then_inc(made, 1)
            pool.wait_ge(made, 7)


def encoder_block(nc, x, norm_mix_pre, w_in, b_if, q_norm, k_norm, mlstm_norm_w, w_attn_o, w_mlstm_o, w_out,
                  norm_mix_post, norm_ffn_pre, w_up, conv_w, conv_b, w_down, norm_ffn_post, cos, sin, y):
    k = Names()
    k.x, k.norm_mix_pre, k.w_in, k.b_if, k.q_norm, k.k_norm = x, norm_mix_pre, w_in, b_if, q_norm, k_norm
    k.mlstm_norm, k.w_attn_o, k.w_mlstm_o, k.w_out = mlstm_norm_w, w_attn_o, w_mlstm_o, w_out
    k.norm_mix_post, k.norm_ffn_pre, k.w_up, k.conv_w, k.conv_b = norm_mix_post, norm_ffn_pre, w_up, conv_w, conv_b
    k.w_down, k.norm_ffn_post, k.cos, k.sin, k.y = w_down, norm_ffn_post, cos, sin, y

    def scratch(name, shape):
        return nc.dram_tensor(name, shape, F32).ap()

    k.v = scratch("v_scratch", (TOK, NKV * HEAD))
    k.qkT = scratch("qkT_scratch", (QK, TOK))
    k.zT = scratch("zT_scratch", (4 * MW + 2 * D, TOK))
    k.negA = scratch("negA_scratch", (2 * MH, TOK))
    k.mergedT, k.x1 = scratch("mergedT_scratch", (D, TOK)), scratch("x1_scratch", (TOK, D))

    with ExitStack() as ctx:
        def sb(stack, name, shape, dt=F32):
            return stack.enter_context(nc.sbuf_tensor(name, shape, dt))

        k.ident, k.mask = sb(ctx, "ident", [P, P]), sb(ctx, "mask", [P, 2, P])
        k.eps, k.one = sb(ctx, "eps", [P, 1]), sb(ctx, "one", [P, 1])
        k.made = ctx.enter_context(nc.semaphore("constants_made"))
        k.waits_apart = ctx.enter_context(nc.semaphore("waits_apart"))
        constants(nc, k)
        with ExitStack() as mix:
            k.a_col = sb(mix, "a_col", [P, 2, NT, MH])
            k.floor = sb(mix, "floor", [P, 2, NT, MH])
            with ExitStack() as proj:
                k.gates = sb(proj, "gates", [P, TOK])
                with ExitStack() as first:
                    hT_hi, hT_lo = (sb(first, f"hT_{s}", [P, KD, TOK], F32R) for s in ("hi", "lo"))
                    clear(nc, norm_and_qkv(nc, k, hT_hi, hT_lo))
                    clear(nc, input_projection(nc, k, hT_hi, hT_lo))
            k.a_T = sb(mix, "a_T", [P, MW // P, TOK])
            attention(nc, k)
            k.h_sum = sb(mix, "h_sum", [P, NT, MH, MD])
            mlstm(nc, k)
            k.b_hi, k.b_lo = (sb(mix, f"branch_{s}", [P, 2 * MW // P, TOK], F32R) for s in ("hi", "lo"))
            mlstm_norm(nc, k)
            merge(nc, k)
        with ExitStack() as second:
            h2_hi, h2_lo = (sb(second, f"h2T_{s}", [P, KD, TOK], F32R) for s in ("hi", "lo"))
            out_projection(nc, k, h2_hi, h2_lo)
            y_sum = sb(second, "y_sum", [P, NT, D])
            ffn(nc, k, h2_hi, h2_lo, y_sum)
            final_norm(nc, k, y_sum)


def rotary_tables():
    import numpy as np

    pairs = HEAD // 4
    freq = np.float32(10000.0) ** (-np.arange(pairs, dtype=np.float32) / np.float32(pairs))
    pos = np.concatenate([np.arange(n * P) for n in SEG_TILES])
    angle = np.concatenate([(pos // GRID_W).astype(np.float32)[:, None] * freq,
                            (pos % GRID_W).astype(np.float32)[:, None] * freq], axis=1)
    table = angle.reshape(NT, P, HEAD // 2).transpose(1, 0, 2)
    return np.ascontiguousarray(np.cos(table)), np.ascontiguousarray(np.sin(table))


_WEIGHTS = ["norm_mix_pre", "w_in", "b_if", "q_norm", "k_norm", "mlstm_norm", "w_attn_o", "w_mlstm_o", "w_out",
            "norm_mix_post", "norm_ffn_pre", "w_up", "conv_w", "conv_b", "w_down", "norm_ffn_post"]


def kernel(**inputs):
    import numpy as np
    import concourse.bacc as bacc
    from concourse.bass_utils import run_bass_kernel_spmd

    x = np.concatenate([np.asarray(inputs[n])[0] for n in ("x_prompt", "x_sample")], axis=0)
    arrays = {"in_x": np.ascontiguousarray(x)}
    for name in _WEIGHTS:
        arrays[f"in_{name}"] = np.ascontiguousarray(np.asarray(inputs[name])[0])
    for name in ("in_conv_w", "in_conv_b"):
        a = arrays[name].reshape(-1, NFF, P)
        arrays[name] = np.ascontiguousarray(a.transpose(2, 0, 1) if name == "in_conv_w" else a[0].T)
    arrays["in_cos"], arrays["in_sin"] = rotary_tables()
    nc = bacc.Bacc("TRN2", target_bir_lowering=False, num_devices=1)
    args = [nc.dram_tensor(n, a.shape, mybir.dt.from_np(a.dtype), kind="ExternalInput").ap()
            for n, a in arrays.items()]
    args.append(nc.dram_tensor("out_y", (TOK, D), F32, kind="ExternalOutput").ap())
    encoder_block(nc, *args)
    y = run_bass_kernel_spmd(nc, [arrays], core_ids=[0]).results[0]["out_y"]
    n = SEG_TILES[0] * P
    return y[None, :n], y[None, n:]
```
